# Optimizing a Trainium2 kernel written in Bass

```python
import numpy as np
import jax
import jax.numpy as jnp
from jax import lax

D_MODEL = 1024
BATCH = 1
SEQ = 256
DEPTH = 2

CTX_LEN = 256
GRID_W = 64
N_DIR = 2
N_BRANCH = 3
BRANCH_WIDTH = 512
RMS_EPS = 1e-6
NEG_INF = -1e30

RWKV_HEAD = 64
RWKV_HEADS = BRANCH_WIDTH // RWKV_HEAD
RWKV_DECAY_LORA = 64
RWKV_A_LORA = 64
RWKV_V_LORA = 32
RWKV_G_LORA = 128
RWKV_LNX_EPS = 64e-5

NA_HEAD = 64
NA_HEADS = BRANCH_WIDTH // NA_HEAD
NA_WIN_R = 8
NA_WIN_C = 16
NA_QC = 16
NA_BAND = NA_QC + NA_WIN_C
NA_NCB = GRID_W // NA_QC

MLSTM_HEADS = 4
MLSTM_DQK = 64
MLSTM_DV = BRANCH_WIDTH // MLSTM_HEADS
MLSTM_CHUNK = 64
GATE_CAP = 15.0
ROPE_ROT = MLSTM_DQK // 4
ROPE_BASE = 10000.0

N_EXPERTS = 64
TOP_K = 8
N_GROUPS = 8
TOPK_GROUPS = 4
D_EXPERT = 128
D_SHARED = 256
ROUTED_SCALE = 2.5

RWKV_COLS = 3 * BRANCH_WIDTH + N_DIR * RWKV_DECAY_LORA + N_DIR * RWKV_A_LORA + RWKV_G_LORA
NA_COLS = 3 * BRANCH_WIDTH
MLSTM_QK = MLSTM_HEADS * MLSTM_DQK
MLSTM_COLS = 2 * MLSTM_QK + 2 * BRANCH_WIDTH + 2 * N_DIR * MLSTM_HEADS
GATE_COLS = N_BRANCH * D_MODEL
IN_COLS = RWKV_COLS + NA_COLS + MLSTM_COLS + GATE_COLS
IN_SPLITS = [RWKV_COLS, RWKV_COLS + NA_COLS, RWKV_COLS + NA_COLS + MLSTM_COLS]
RWKV_SPLITS = [BRANCH_WIDTH, 2 * BRANCH_WIDTH, 3 * BRANCH_WIDTH, 3 * BRANCH_WIDTH + N_DIR * RWKV_DECAY_LORA, 3 * BRANCH_WIDTH + N_DIR * (RWKV_DECAY_LORA + RWKV_A_LORA)]
MLSTM_SPLITS = [MLSTM_QK, 2 * MLSTM_QK, 2 * MLSTM_QK + BRANCH_WIDTH, 2 * MLSTM_QK + 2 * BRANCH_WIDTH, 2 * MLSTM_QK + 2 * BRANCH_WIDTH + N_DIR * MLSTM_HEADS]

kernel_name = 'hybrid_rwkv7_natten_mlstm_moe_dit'

def rms_norm(z, g):
    zf = z.astype(jnp.float32)
    zf = zf * lax.rsqrt(jnp.mean(zf * zf, axis=-1, keepdims=True) + RMS_EPS)
    return zf.astype(z.dtype) * g

def soft_cap(z):
    return GATE_CAP * jnp.tanh(z / GATE_CAP)

def token_shift(z, mu):
    zp = jnp.pad(z, ((0, 0), (1, 1), (0, 0)))
    return z + mu * (0.5 * (zp[:, :-2] + zp[:, 2:]) - z)

def rwkv_features(z, v_first, mu, w0, w2, a0, a2, k_k, k_a, g2, vres):
    B, T, _ = z.shape
    z = token_shift(z, mu)
    r, k, v, wd, ad, gd = jnp.split(z, RWKV_SPLITS, axis=-1)
    wd = wd.reshape(B, T, N_DIR, RWKV_DECAY_LORA)
    ad = ad.reshape(B, T, N_DIR, RWKV_A_LORA)
    w = -jax.nn.softplus(-(w0 + jnp.einsum('btdl,dlc->btdc', jnp.tanh(wd), w2))) - 0.5
    decay = jnp.exp(-jnp.exp(w.astype(jnp.float32)))
    a = jax.nn.sigmoid(a0 + jnp.einsum('btdl,dlc->btdc', ad, a2))
    kk = (k * k_k).astype(jnp.float32).reshape(B, T, RWKV_HEADS, RWKV_HEAD)
    kk = kk / jnp.maximum(jnp.sqrt(jnp.sum(kk * kk, axis=-1, keepdims=True)), 1e-12)
    k_dir = k[:, :, None, :] * (1 + (a - 1) * k_a)
    if vres is None:
        v_first = v
    else:
        v0, v1, v2 = vres
        v = v + (v_first - v) * jax.nn.sigmoid(v0 + (v @ v1) @ v2)
    g = jax.nn.sigmoid(gd) @ g2
    return (r, k_dir, v, decay, a, kk, g), v_first

def rwkv_scan_inputs(feats, d):
    r, k_dir, v, decay, a, kk, g = feats
    B, T, _ = r.shape
    heads = lambda t: t.astype(jnp.float32).reshape(B, T, RWKV_HEADS, RWKV_HEAD)
    return heads(r), heads(decay[:, :, d]), -kk, kk * heads(a[:, :, d]), heads(k_dir[:, :, d]), heads(v)

def wkv_scan(state, r, w, a, b, k, v, reverse):
    def step(S, inp):
        r_t, w_t, a_t, b_t, k_t, v_t = inp
        sa = jnp.einsum('bhvk,bhk->bhv', S, a_t)
        S = S * w_t[:, :, None, :] + sa[..., None] * b_t[:, :, None, :] + v_t[..., None] * k_t[:, :, None, :]
        return S, jnp.einsum('bhvk,bhk->bhv', S, r_t)
    xs = tuple(jnp.moveaxis(t, 1, 0) for t in (r, w, a, b, k, v))
    state, y = lax.scan(step, state, xs, reverse=reverse)
    return state, jnp.moveaxis(y, 0, 1)

def rwkv_readout(y, feats, r_k, lnx_g, lnx_b):
    r, k_dir, v, decay, a, kk, g = feats
    B, T, C = r.shape
    mean = jnp.mean(y, axis=-1, keepdims=True)
    var = jnp.mean(jnp.square(y - mean), axis=-1, keepdims=True)
    yn = ((y - mean) * lax.rsqrt(var + RWKV_LNX_EPS)).reshape(B, T, C).astype(r.dtype) * lnx_g + lnx_b
    rh = r.reshape(B, T, RWKV_HEADS, RWKV_HEAD)
    kh = k_dir.reshape(B, T, N_DIR, RWKV_HEADS, RWKV_HEAD)
    bonus = jnp.einsum('bthn,btdhn,hn->bth', rh, kh, r_k)[..., None] * v.reshape(B, T, RWKV_HEADS, RWKV_HEAD)
    return (yn + bonus.reshape(B, T, C)) * g

def rwkv_mix(zx, zc, vf_x, vf_c, mu, w0, w2, a0, a2, k_k, k_a, r_k, g2, lnx_g, lnx_b, vres, need_ctx):
    fx, vf_x = rwkv_features(zx, vf_x, mu, w0, w2, a0, a2, k_k, k_a, g2, vres)
    fc, vf_c = rwkv_features(zc, vf_c, mu, w0, w2, a0, a2, k_k, k_a, g2, vres)
    B = zx.shape[0]
    y_x = 0.0
    y_c = 0.0
    for d in range(N_DIR):
        rev = d == 1
        s0 = jnp.zeros((B, RWKV_HEADS, RWKV_HEAD, RWKV_HEAD), jnp.float32)
        s_ctx, yc = wkv_scan(s0, *rwkv_scan_inputs(fc, d), reverse=rev)
        _, yx = wkv_scan(s_ctx, *rwkv_scan_inputs(fx, d), reverse=rev)
        y_x = y_x + yx
        y_c = y_c + yc
    out_x = rwkv_readout(y_x, fx, r_k, lnx_g, lnx_b)
    out_c = rwkv_readout(y_c, fc, r_k, lnx_g, lnx_b) if need_ctx else None
    return out_x, out_c, vf_x, vf_c

def neighbourhood_attention(q, k, v, kc, vc, rpb, rows):
    B, S, H, DH = q.shape
    win_r = min(NA_WIN_R, rows)
    qcol = np.arange(GRID_W).reshape(NA_NCB, NA_QC)
    band0 = np.clip(np.arange(NA_NCB) * NA_QC - NA_WIN_C // 2, 0, GRID_W - NA_BAND)
    keycol = band0[:, None] + np.arange(NA_BAND)[None, :]
    cs = np.clip(qcol - NA_WIN_C // 2, 0, GRID_W - NA_WIN_C)
    kcol = keycol[:, None, :]
    col_valid = (kcol >= cs[..., None]) & (kcol < cs[..., None] + NA_WIN_C)
    col_idx = np.clip(kcol - qcol[..., None] + NA_WIN_C - 1, 0, 2 * NA_WIN_C - 2)
    qg = (q * DH ** -0.5).reshape(B, rows, GRID_W, H, DH)
    kg = k.reshape(B, rows, GRID_W, H, DH)
    vg = v.reshape(B, rows, GRID_W, H, DH)
    n_loc = win_r * NA_BAND

    def row_block(r):
        rs = jnp.clip(r - win_r // 2, 0, rows - win_r)
        q_b = lax.dynamic_index_in_dim(qg, r, axis=1, keepdims=False).reshape(B, NA_NCB, NA_QC, H, DH)
        k_b = lax.dynamic_slice_in_dim(kg, rs, win_r, axis=1)[:, :, keycol]
        v_b = lax.dynamic_slice_in_dim(vg, rs, win_r, axis=1)[:, :, keycol]
        s_loc = jnp.einsum('bnqhd,brnkhd->bhnqrk', q_b, k_b).astype(jnp.float32)
        row_off = rs + jnp.arange(win_r) - r + NA_WIN_R - 1
        bias = rpb[:, row_off][:, :, col_idx].transpose(0, 2, 3, 1, 4).astype(jnp.float32)
        s_loc = jnp.where(col_valid[:, :, None, :], s_loc + bias, NEG_INF)
        s_ctx = jnp.einsum('bnqhd,bchd->bhnqc', q_b, kc).astype(jnp.float32)
        s = jnp.concatenate([s_loc.reshape(B, H, NA_NCB, NA_QC, n_loc), s_ctx], axis=-1)
        p = jax.nn.softmax(s, axis=-1).astype(v.dtype)
        p_loc = p[..., :n_loc].reshape(B, H, NA_NCB, NA_QC, win_r, NA_BAND)
        o = jnp.einsum('bhnqrk,brnkhd->bnqhd', p_loc, v_b) + jnp.einsum('bhnqc,bchd->bnqhd', p[..., n_loc:], vc)
        return o.reshape(B, GRID_W, H * DH)

    out = lax.map(row_block, jnp.arange(rows))
    return jnp.moveaxis(out, 0, 1).reshape(B, S, H * DH)

def ctx_attention(q, k, v):
    s = jnp.einsum('bqhd,bkhd->bhqk', q * q.shape[-1] ** -0.5, k).astype(jnp.float32)
    p = jax.nn.softmax(s, axis=-1).astype(v.dtype)
    return jnp.einsum('bhqk,bkhd->bqhd', p, v)

def na_mix(zx, zc, qn_g, kn_g, rpb, rows, need_ctx):
    heads = lambda t: t.reshape(t.shape[0], t.shape[1], NA_HEADS, NA_HEAD)
    qx, kx, vx = jnp.split(zx, 3, axis=-1)
    qc, kc, vc = jnp.split(zc, 3, axis=-1)
    kc = rms_norm(heads(kc), kn_g)
    vc = heads(vc)
    out_x = neighbourhood_attention(rms_norm(heads(qx), qn_g), rms_norm(heads(kx), kn_g), heads(vx), kc, vc, rpb, rows)
    out_c = None
    if need_ctx:
        out_c = ctx_attention(rms_norm(heads(qc), qn_g), kc, vc)
        out_c = out_c.reshape(out_c.shape[0], out_c.shape[1], BRANCH_WIDTH)
    return out_x, out_c

def axial_rope_tables(n_tokens, dtype):
    t = jnp.arange(n_tokens)
    pos = jnp.stack([t // GRID_W, t % GRID_W], axis=-1).astype(jnp.float32)
    inv = ROPE_BASE ** (-jnp.arange(ROPE_ROT, dtype=jnp.float32) / ROPE_ROT)
    ang = pos[:, :, None] * inv
    return jnp.cos(ang).astype(dtype), jnp.sin(ang).astype(dtype)

def apply_axial_rope(z, cos, sin):
    B, T, H, DK = z.shape
    zr = z.reshape(B, T, H, 2, 2, ROPE_ROT)
    z1, z2 = zr[..., 0, :], zr[..., 1, :]
    c, s = cos[None, :, None], sin[None, :, None]
    return jnp.stack([z1 * c - z2 * s, z2 * c + z1 * s], axis=-2).reshape(B, T, H, DK)

def mlstm_features(z, i_bias, f_bias, cos, sin):
    B, T, _ = z.shape
    q, k, v, o, ig, fg = jnp.split(z, MLSTM_SPLITS, axis=-1)
    q = q.reshape(B, T, MLSTM_HEADS, MLSTM_DQK)
    k = k.reshape(B, T, MLSTM_HEADS, MLSTM_DQK)
    if cos is not None:
        q = apply_axial_rope(q, cos, sin)
        k = apply_axial_rope(k, cos, sin)
    v = v.reshape(B, T, MLSTM_HEADS, MLSTM_DV)
    hf = lambda t: t.astype(jnp.float32).transpose(0, 2, 1, 3)
    gate = lambda g, bias: soft_cap(g.reshape(B, T, N_DIR, MLSTM_HEADS).astype(jnp.float32) + bias.astype(jnp.float32)).transpose(2, 0, 3, 1)
    return hf(q), hf(k), hf(v), o, gate(ig, i_bias), gate(fg, f_bias)

def mlstm_chunkwise(q, k, v, ig, fg, state):
    B, H, T, DK = q.shape
    DV = v.shape[-1]
    L = MLSTM_CHUNK
    NC = T // L
    q = q * DK ** -0.5
    split = lambda t: jnp.moveaxis(t.reshape(B, H, NC, L, *t.shape[3:]), 2, 0)
    causal = jnp.tril(jnp.ones((L, L), dtype=bool))

    def step(carry, inp):
        C, n, m = carry
        qc, kc, vc, ic, fc = inp
        b = jnp.cumsum(jax.nn.log_sigmoid(fc), axis=-1)
        d = jnp.where(causal, b[..., :, None] - b[..., None, :] + ic[..., None, :], NEG_INF)
        inter = b + m[..., None]
        m_t = jnp.maximum(inter, jnp.max(d, axis=-1))
        s = jnp.einsum('bhtk,bhsk->bhts', qc, kc) * jnp.exp(d - m_t[..., None])
        sc_inter = jnp.exp(inter - m_t)
        num = sc_inter[..., None] * jnp.einsum('bhtk,bhkv->bhtv', qc, C) + jnp.einsum('bhts,bhsv->bhtv', s, vc)
        den = sc_inter * jnp.einsum('bhtk,bhk->bht', qc, n) + jnp.sum(s, axis=-1)
        h = num / jnp.maximum(jnp.abs(den), jnp.exp(-m_t))[..., None]
        b_last = b[..., -1]
        wlog = b_last[..., None] - b + ic
        m_new = jnp.maximum(b_last + m, jnp.max(wlog, axis=-1))
        dec = jnp.exp(b_last + m - m_new)
        wexp = jnp.exp(wlog - m_new[..., None])
        C = dec[..., None, None] * C + jnp.einsum('bhs,bhsk,bhsv->bhkv', wexp, kc, vc)
        n = dec[..., None] * n + jnp.einsum('bhs,bhsk->bhk', wexp, kc)
        return (C, n, m_new), h

    state, h = lax.scan(step, state, (split(q), split(k), split(v), split(ig), split(fg)))
    return jnp.moveaxis(h, 0, 2).reshape(B, H, T, DV), state

def mlstm_readout(h, o, norm_g):
    B, H, T, DV = h.shape
    h = h.transpose(0, 2, 1, 3)
    h = h * lax.rsqrt(jnp.mean(h * h, axis=-1, keepdims=True) + RMS_EPS)
    h = h.reshape(B, T, H * DV).astype(o.dtype) * norm_g
    return h * jax.nn.sigmoid(o)

def mlstm_mix(zx, zc, i_bias, f_bias, norm_g, cos, sin, need_ctx):
    qx, kx, vx, ox, ix, fx = mlstm_features(zx, i_bias, f_bias, cos, sin)
    qc, kc, vc, oc, ic, fc = mlstm_features(zc, i_bias, f_bias, None, None)
    B = zx.shape[0]
    h_x = 0.0
    h_c = 0.0
    for d in range(N_DIR):
        fl = (lambda t: jnp.flip(t, axis=2)) if d == 1 else (lambda t: t)
        st0 = (jnp.zeros((B, MLSTM_HEADS, MLSTM_DQK, MLSTM_DV), jnp.float32),
               jnp.zeros((B, MLSTM_HEADS, MLSTM_DQK), jnp.float32),
               jnp.zeros((B, MLSTM_HEADS), jnp.float32))
        hc_d, st_ctx = mlstm_chunkwise(fl(qc), fl(kc), fl(vc), fl(ic[d]), fl(fc[d]), st0)
        hx_d, _ = mlstm_chunkwise(fl(qx), fl(kx), fl(vx), fl(ix[d]), fl(fx[d]), st_ctx)
        h_x = h_x + fl(hx_d)
        h_c = h_c + fl(hc_d)
    out_x = mlstm_readout(h_x, ox, norm_g)
    out_c = mlstm_readout(h_c, oc, norm_g) if need_ctx else None
    return out_x, out_c

def merge_branches(ya, yb, yc, gate_cols, w_branch, w_out):
    ga, gb, gc = jnp.split(jax.nn.sigmoid(gate_cols), N_BRANCH, axis=-1)
    merged = ga * (ya @ w_branch[0]) + gb * (yb @ w_branch[1]) + gc * (yc @ w_branch[2])
    return merged @ w_out

def moe_ffn(h, w_router, router_bias, w_gate, w_up, w_down, s_gate, s_up, s_down):
    def per_sample(hs):
        T = hs.shape[0]
        scores = jax.nn.sigmoid((hs @ w_router).astype(jnp.float32))
        sel = scores + router_bias.astype(jnp.float32)
        grp = sel.reshape(T, N_GROUPS, N_EXPERTS // N_GROUPS)
        gscore = jnp.sum(lax.top_k(grp, 2)[0], axis=-1)
        gidx = lax.top_k(gscore, TOPK_GROUPS)[1]
        gmask = jnp.sum(jax.nn.one_hot(gidx, N_GROUPS, dtype=jnp.float32), axis=-2) > 0
        emask = jnp.repeat(gmask, N_EXPERTS // N_GROUPS, axis=-1)
        eidx = lax.top_k(jnp.where(emask, sel, NEG_INF), TOP_K)[1]
        w = jnp.take_along_axis(scores, eidx, axis=-1)
        w = w / jnp.sum(w, axis=-1, keepdims=True) * ROUTED_SCALE
        gates = jnp.sum(jax.nn.one_hot(eidx, N_EXPERTS, dtype=jnp.float32) * w[..., None], axis=-2).astype(hs.dtype)
        hg = jnp.einsum('td,edf->tef', hs, w_gate)
        hu = jnp.einsum('td,edf->tef', hs, w_up)
        routed = jnp.einsum('tef,efd->td', jax.nn.silu(hg) * hu * gates[:, :, None], w_down)
        shared = (jax.nn.silu(hs @ s_gate) * (hs @ s_up)) @ s_down
        return routed + shared
    return lax.map(per_sample, h)

def setup_inputs(seed: int = 0) -> dict:
    key = jax.random.key(seed)
    keys = iter(jax.random.split(key, 64))

    def nrm(shape, scale, shift=0.0):
        return shift + scale * jax.random.normal(next(keys), shape, jnp.float32)

    L, D, C = DEPTH, D_MODEL, BRANCH_WIDTH
    return {
        'x': nrm((BATCH, SEQ, D), 1.0),
        'c': nrm((BATCH, D), 1.0),
        'ctx': nrm((BATCH, CTX_LEN, D), 1.0),
        'c_ctx': nrm((D,), 1.0),
        'w_ada': nrm((L, D, 6 * D), 0.5 * D ** -0.5),
        'b_ada': nrm((L, 6 * D), 0.02),
        'norm1_g': nrm((L, D), 0.1, 1.0),
        'norm2_g': nrm((L, D), 0.1, 1.0),
        'w_in': nrm((L, D, IN_COLS), D ** -0.5),
        'rw_mu': jax.random.uniform(next(keys), (L, RWKV_COLS), jnp.float32),
        'rw_w0': nrm((L, N_DIR, C), 0.5, -1.0),
        'rw_w2': nrm((L, N_DIR, RWKV_DECAY_LORA, C), 0.1),
        'rw_a0': nrm((L, N_DIR, C), 0.5),
        'rw_a2': nrm((L, N_DIR, RWKV_A_LORA, C), 0.1),
        'rw_k_k': nrm((L, C), 0.1, 1.0),
        'rw_k_a': nrm((L, C), 0.1, 1.0),
        'rw_r_k': nrm((L, RWKV_HEADS, RWKV_HEAD), 0.1),
        'rw_g2': nrm((L, RWKV_G_LORA, C), RWKV_G_LORA ** -0.5),
        'rw_lnx_g': nrm((L, C), 0.1, 1.0),
        'rw_lnx_b': nrm((L, C), 0.02),
        'rw_v0': nrm((L - 1, C), 0.5),
        'rw_v1': nrm((L - 1, C, RWKV_V_LORA), C ** -0.5),
        'rw_v2': nrm((L - 1, RWKV_V_LORA, C), 0.1),
        'na_qn_g': nrm((L, NA_HEAD), 0.1, 1.0),
        'na_kn_g': nrm((L, NA_HEAD), 0.1, 1.0),
        'na_rpb': nrm((L, NA_HEADS, 2 * NA_WIN_R - 1, 2 * NA_WIN_C - 1), 0.5),
        'ml_i_bias': nrm((L, N_DIR, MLSTM_HEADS), 0.5, -1.0),
        'ml_f_bias': nrm((L, N_DIR, MLSTM_HEADS), 0.5, 3.0),
        'ml_norm_g': nrm((L, C), 0.1, 1.0),
        'w_branch': nrm((L, N_BRANCH, C, D), C ** -0.5),
        'w_out': nrm((L, D, D), D ** -0.5),
        'moe_router': nrm((L, D, N_EXPERTS), D ** -0.5),
        'moe_bias': nrm((L, N_EXPERTS), 0.01),
        'moe_w_gate': nrm((L, N_EXPERTS, D, D_EXPERT), D ** -0.5),
        'moe_w_up': nrm((L, N_EXPERTS, D, D_EXPERT), D ** -0.5),
        'moe_w_down': nrm((L, N_EXPERTS, D_EXPERT, D), D_EXPERT ** -0.5),
        'sh_w_gate': nrm((L, D, D_SHARED), D ** -0.5),
        'sh_w_up': nrm((L, D, D_SHARED), D ** -0.5),
        'sh_w_down': nrm((L, D_SHARED, D), D_SHARED ** -0.5),
    }

def reference(x, c, ctx, c_ctx, w_ada, b_ada, norm1_g, norm2_g, w_in, rw_mu, rw_w0, rw_w2, rw_a0, rw_a2,
              rw_k_k, rw_k_a, rw_r_k, rw_g2, rw_lnx_g, rw_lnx_b, rw_v0, rw_v1, rw_v2, na_qn_g, na_kn_g, na_rpb,
              ml_i_bias, ml_f_bias, ml_norm_g, w_branch, w_out, moe_router, moe_bias, moe_w_gate, moe_w_up,
              moe_w_down, sh_w_gate, sh_w_up, sh_w_down):
    B, S, D = x.shape
    rows = S // GRID_W
    cos, sin = axial_rope_tables(S, x.dtype)
    s_c = jax.nn.silu(c)
    s_cctx = jax.nn.silu(c_ctx)
    vf_x = None
    vf_c = None
    for l in range(DEPTH):
        need_ctx = l < DEPTH - 1
        mod_x = (s_c @ w_ada[l] + b_ada[l])[:, None, :]
        mod_c = s_cctx @ w_ada[l] + b_ada[l]
        shx1, scx1, gx1, shx2, scx2, gx2 = jnp.split(mod_x, 6, axis=-1)
        shc1, scc1, gc1, shc2, scc2, gc2 = jnp.split(mod_c, 6, axis=-1)
        hx = rms_norm(x, norm1_g[l]) * (1 + scx1) + shx1
        hc = rms_norm(ctx, norm1_g[l]) * (1 + scc1) + shc1
        px = hx @ w_in[l]
        pc = hc @ w_in[l]
        ax, bx, cx, gx = jnp.split(px, IN_SPLITS, axis=-1)
        ac, bc, cc, gcol = jnp.split(pc, IN_SPLITS, axis=-1)
        vres = None if l == 0 else (rw_v0[l - 1], rw_v1[l - 1], rw_v2[l - 1])
        ya_x, ya_c, vf_x, vf_c = rwkv_mix(ax, ac, vf_x, vf_c, rw_mu[l], rw_w0[l], rw_w2[l], rw_a0[l], rw_a2[l],
                                          rw_k_k[l], rw_k_a[l], rw_r_k[l], rw_g2[l], rw_lnx_g[l], rw_lnx_b[l],
                                          vres, need_ctx)
        yb_x, yb_c = na_mix(bx, bc, na_qn_g[l], na_kn_g[l], na_rpb[l], rows, need_ctx)
        yc_x, yc_c = mlstm_mix(cx, cc, ml_i_bias[l], ml_f_bias[l], ml_norm_g[l], cos, sin, need_ctx)
        x = x + gx1 * merge_branches(ya_x, yb_x, yc_x, gx, w_branch[l], w_out[l])
        h2 = rms_norm(x, norm2_g[l]) * (1 + scx2) + shx2
        x = x + gx2 * moe_ffn(h2, moe_router[l], moe_bias[l], moe_w_gate[l], moe_w_up[l], moe_w_down[l],
                              sh_w_gate[l], sh_w_up[l], sh_w_down[l])
        if need_ctx:
            ctx = ctx + gc1 * merge_branches(ya_c, yb_c, yc_c, gcol, w_branch[l], w_out[l])
            hc2 = rms_norm(ctx, norm2_g[l]) * (1 + scc2) + shc2
            ctx = ctx + gc2 * moe_ffn(hc2, moe_router[l], moe_bias[l], moe_w_gate[l], moe_w_up[l], moe_w_down[l],
                                      sh_w_gate[l], sh_w_up[l], sh_w_down[l])
    return x


_drawn_inputs = setup_inputs


def setup_inputs(seed=0):
    import zlib

    import numpy as np

    out = dict(_drawn_inputs(seed))
    spreads = {}
    factors = {'rw_lnx_b': 3.946, 'na_qn_g': 3.639, 'na_kn_g': 4.943}
    for name, (base, spread) in spreads.items():
        noise = np.random.default_rng([zlib.crc32(name.encode()), seed]).standard_normal(out[name].shape)
        drawn = base * np.exp(spread * noise) if base else spread * noise
        out[name] = jnp.asarray(drawn.astype(out[name].dtype))
    for name, factor in factors.items():
        out[name] = (out[name] * factor).astype(out[name].dtype)
    return out
```

```python
from contextlib import ExitStack

import numpy as np

import concourse.bass as bass
from concourse import mybir

F32 = mybir.dt.float32
ALU = mybir.AluOpType
ACT = mybir.ActivationFunctionType
AX = mybir.AxisListType

P = 128
D = 1024
KD = D // P
SEQ = 256
CTX = 256
T = CTX + SEQ
DEPTH = 2
C = 512
KC = C // P
GRID_W = 64
HD = 64
HEADS = C // HD
L = 64
N_LORA_TILES = 3
ML_HEADS = 4
NA_WIN_R, NA_WIN_C = 8, 16
ROWS = SEQ // GRID_W
E_ROUTED = 64
E_ALL = E_ROUTED + 2
TOP_K = 8
GROUPS = 8
TOPK_GROUPS = 4
ROUTED_SCALE = 2.5
RMS_EPS = 1e-6
LNX_EPS = 64e-5
GATE_CAP = 15.0
NEG = -1e30
DECAY = float(np.exp(-0.5))
LEVELS = (1, 2, 4, 8, 16, 32)

R_T, K_T, V_T, WD_T, AD_T, GD_T, GATE_T = 0, 4, 8, 12, 13, 14, 15
NQ_T, NK_T, MQ_T, MK_T, MO_T = 0, 4, 8, 10, 12

PAR = {}


def _par_layout():
    at = 0
    for name, n in (("n1", KD), ("n2", KD), ("bada", 6 * KD), ("mu", 15), ("w0", 2 * KC), ("a0", 2 * KC), ("kk", KC),
                    ("ka", KC), ("rk", KC), ("lg", KC), ("lb", KC), ("v0", KC), ("mg", KC), ("qn", 1), ("kn", 1),
                    ("ib", 1), ("fb", 1)):
        PAR[name] = (at, n)
        at += n
    return at


NPAR = _par_layout()

CST = {}


def _cst_layout():
    at = 0
    for name, n in (("ident", P), ("ones", P), ("blk", P), ("perm", P), ("cos", SEQ), ("sin", SEQ),
                    ("mra0", P), ("mra1", P), ("lev0", 6 * L), ("lev1", 6 * L), ("eye", L), ("reset", KC * L),
                    ("segres", T), ("eps", 4), ("sgn", 2)):
        CST[name] = (at, n)
        at += n
    return at


NCST = _cst_layout()
NMLC = 4 * SEQ + 8 * P


def constants():
    c = np.zeros((P, NCST), np.float32)

    def put(name, a):
        at, n = CST[name]
        c[:a.shape[0], at:at + n] = a.reshape(a.shape[0], n)

    put("ident", np.eye(P))
    put("ones", np.ones((P, P)))
    half = np.arange(P) // HD
    put("blk", (half[:, None] == half[None, :]).astype(np.float32))
    perm = np.zeros((P, P))
    cos, sin = np.zeros((P, SEQ)), np.zeros((P, SEQ))
    t = np.arange(SEQ)
    pos = np.stack([t // GRID_W, t % GRID_W]).astype(np.float32)
    inv = (np.float32(10000.0) ** (-np.arange(16, dtype=np.float32) / np.float32(16))).astype(np.float32)
    for p in range(P):
        axis, second, i = (p % HD) // 32, (p % 32) // 16, p % 16
        ang = (pos[axis] * inv[i]).astype(np.float32)
        cos[p], sin[p] = np.cos(ang), np.sin(ang)
        perm[p - 16 if second else p + 16, p] = 1.0 if second else -1.0
    put("perm", perm)
    put("cos", cos)
    put("sin", sin)
    s = np.arange(P) % L
    q = np.arange(L)
    put("mra0", np.concatenate([s[:, None] <= q, s[:, None] < q], 1).astype(np.float32))
    put("mra1", np.concatenate([s[:, None] >= q, s[:, None] > q], 1).astype(np.float32))
    for d in range(2):
        lev = []
        for m in LEVELS:
            same = (s[:, None] // (2 * m)) == (q[None, :] // (2 * m))
            first_s, first_q = (s[:, None] // m) % 2 == 0, (q[None, :] // m) % 2 == 0
            lev.append(same & (first_s & ~first_q if d == 0 else ~first_s & first_q))
        put(f"lev{d}", np.stack(lev, 1).astype(np.float32))
    put("eye", (s[:, None] == q[None, :]).astype(np.float32))
    put("reset", np.broadcast_to((np.arange(KC * L) % L != 0).astype(np.float32), (P, KC * L)))
    put("segres", np.broadcast_to((np.arange(T) % SEQ != 0).astype(np.float32), (P, T)))
    put("eps", np.broadcast_to(np.array([RMS_EPS, LNX_EPS, 0, 0], np.float32), (P, 4)))
    row = np.arange(P)[:, None]
    put("sgn", np.concatenate([np.where(row < 4, 1.0, -1.0), np.where(row < 4, 0.0, 1.0)], 1))
    m = np.zeros((P, NMLC), np.float32)
    for d in range(2):
        for i in range(2):
            key = i * P + np.arange(P)[:, None]
            ok = key <= np.arange(SEQ)[None, :] if d == 0 else key >= np.arange(SEQ)[None, :]
            m[:, (d * 2 + i) * SEQ:(d * 2 + i + 1) * SEQ] = np.where(ok, 0.0, NEG)
    for r in range(8):
        m[r, 4 * SEQ + r * P:4 * SEQ + (r + 1) * P] = 1.0
    return c, m


class Signal:

    def __init__(self, sem):
        self.sem = sem
        self.base = 0

    def at(self, n):
        return self.base + n

    def advance(self, n):
        self.base += n


class Kit:

    def __init__(self, nc, ctx):
        self.nc, self.ctx, self.named = nc, ctx, {}

    def signals(self, *names):
        for n in names:
            if n not in self.named:
                self.named[n] = Signal(self.ctx.enter_context(self.nc.semaphore(n)))
        return [self.named[n] for n in names]

    def cst(self, name, rows=P):
        at, n = CST[name]
        return self.cst_sb[0:rows, at:at + n]

    def par(self, l, name, rows=P):
        at, n = PAR[name]
        return self.par_sb[0:rows, l * NPAR + at:l * NPAR + at + n]


def stage_modulation(nc, k):
    NB = 6 * D // 512
    names = ["ada_cst_in", "ada_silu", "ada_block", "ada_row", "ada_turned", "ada_mod"] + [f"ada_in{j}" for j in range(4)]
    cst_in, silu, block_done, row_out, turned, mod_done, *ada_in = k.signals(*names)
    with ExitStack() as ctx:
        ring = ctx.enter_context(nc.sbuf_tensor("ada_ring", [P, 4, KD, 512], F32))
        cv = ctx.enter_context(nc.sbuf_tensor("cv", [P, KD, 2], F32))
        sg = ctx.enter_context(nc.sbuf_tensor("cv_sig", [P, KD, 2], F32))
        sv = ctx.enter_context(nc.sbuf_tensor("cv_silu", [P, KD, 2], F32))
        row = ctx.enter_context(nc.sbuf_tensor("mod_row", [2, 6 * D], F32))
        ps = ctx.enter_context(nc.psum_tensor("mod_ps", [P, 2, 512], F32))
        psT = ctx.enter_context(nc.psum_tensor("modT_ps", [P, 512], F32))
        with nc.Block() as block:

            @block.sync
            def _(sp):
                sp.dma_start(k.cst_sb[:], k.d_cst).then_inc(cst_in.sem, 16)
                sp.dma_start(cv[:], k.d_c).then_inc(cst_in.sem, 16)
                sp.dma_start(k.par_sb[:], k.d_par).then_inc(cst_in.sem, 16)
                for l in range(DEPTH):
                    with sp.Fori(0, NB // 4) as i:
                        for j in range(4):
                            sp.wait_ge(block_done.sem, block_done.at(l * NB + 1 + j) + i * 4)
                            sp.dma_start(ring[:, j], k.d_ada[l, bass.ds(i * 4 + j, 1)].rearrange(
                                "a p (k n) -> p (a k) n", k=KD)).then_inc(ada_in[j].sem, 16)

            @block.gpsimd
            def _(pool):
                pool.memset(k.scratch[:, 0:1], 0.0).then_inc(block_done.sem, 4)
                pool.memset(k.scratch[:, 1:2], 0.0).then_inc(row_out.sem, 2)

            @block.scalar
            def _(act):
                act.wait_ge(cst_in.sem, cst_in.at(48))
                act.activation(sg[:], cv[:], ACT.Sigmoid).then_inc(silu.sem, 1)
                for l in range(DEPTH):
                    if l:
                        act.wait_ge(turned.sem, turned.at(l))
                    with act.Fori(0, NB // 2) as i:
                        for j in range(2):
                            act.wait_ge(block_done.sem, block_done.at(l * NB + j + 5) + i * 2)
                            act.activation(row[:, bass.ds(i * 1024 + j * 512, 512)], ps[0:2, j], ACT.Copy
                                           ).then_inc(row_out.sem, 1)

            @block.tensor
            def _(pe):
                pe.wait_ge(silu.sem, silu.at(2))
                for l in range(DEPTH):
                    with pe.Fori(0, NB // 4) as i:
                        for j in range(4):
                            pe.wait_ge(ada_in[j].sem, ada_in[j].at(l * NB * 4 + 16) + i * 16)
                            pe.wait_ge(row_out.sem, row_out.at(l * NB + j + 1) + i * 4)
                            for c in range(KD):
                                last = pe.matmul(ps[0:2, j % 2], sv[:, c], ring[:, j, c], start=c == 0,
                                                 stop=c == KD - 1)
                            last.then_inc(block_done.sem, 1)
                    pe.wait_ge(row_out.sem, row_out.at((l + 1) * NB + 2))
                    if l:
                        pe.wait_ge(mod_done.sem, mod_done.at(l))
                    for j in range(6 * KD):
                        last = pe.transpose(psT[:, 2 * j:2 * j + 2], row[:, j * P:(j + 1) * P],
                                            k.cst("ident", 2)[:, 0:2])
                    last.then_inc(turned.sem, 1)

            @block.vector
            def _(dve):
                dve.wait_ge(silu.sem, silu.at(1))
                dve.tensor_tensor(sv[:], sg[:], cv[:], ALU.mult).then_inc(silu.sem, 1)
                for l in range(DEPTH):
                    dve.wait_ge(turned.sem, turned.at(l + 1))
                    for s in range(2):
                        dve.tensor_tensor(k.mod[:, l, s], psT[:, 0:12 * KD].rearrange("p (j s) -> p s j", s=2)[:, s],
                                          k.par(l, "bada"), ALU.add)
                    dve.drain()
                    for s in range(2):
                        for at, g in ((1, "n1"), (4, "n2")):
                            last = dve.scalar_tensor_tensor(
                                out=k.mod[:, l, s, at * KD:(at + 1) * KD], in0=k.mod[:, l, s, at * KD:(at + 1) * KD],
                                scalar=1.0, in1=k.par(l, g), op0=ALU.add, op1=ALU.mult)
                    last.then_inc(mod_done.sem, 1)
        for s, n in zip((cst_in, silu, block_done, row_out, turned, mod_done), (48, 2, 2 * NB + 4, 2 * NB + 2, 2, 2)):
            s.advance(n)
        for s in ada_in:
            s.advance(2 * 4 * NB)


def stage_norm(nc, k, l, which, x, h, t0, x_source=None):
    sq_done, sum_done, root_done, scaled, h_done, x_in = k.signals(
        "norm_sq", "norm_sum", "norm_root", "norm_scaled", "norm_h", "norm_x_in")
    N = T - t0
    shift, scale = (0, 1) if which == 1 else (3, 4)
    with ExitStack() as ctx:
        tmp = ctx.enter_context(nc.sbuf_tensor(f"norm_tmp{l}{which}", [P, KD, T], F32))
        rstd = ctx.enter_context(nc.sbuf_tensor(f"norm_rstd{l}{which}", [P, T], F32))
        ps = ctx.enter_context(nc.psum_tensor(f"norm_ps{l}{which}", [P, 512], F32))
        with nc.Block(no_gpsimd_drain=True) as block:
            if x_source is not None:
                @block.sync
                def _(sp):
                    for c in range(KD):
                        sp.dma_start(x[:, c], x_source[:, c]).then_inc(x_in.sem, 16)

            @block.scalar
            def _(act):
                if x_source is not None:
                    act.wait_ge(x_in.sem, x_in.at(16 * KD))
                for c in range(KD):
                    act.activation(tmp[:, c, t0:T], x[:, c, t0:T], ACT.Square).then_inc(sq_done.sem, 1)
                act.wait_ge(sum_done.sem, sum_done.at(1))
                act.activation(rstd[:, t0:T], ps[:, 0:N], ACT.Sqrt, scale=1.0 / D, bias=k.cst("eps")[:, 0:1]
                               ).then_inc(root_done.sem, 1)
                for c in range(KD):
                    act.wait_ge(scaled.sem, scaled.at(c + 1))
                    for s in range(2):
                        if s * CTX >= t0:
                            last = act.activation(h[:, c, s * CTX:(s + 1) * CTX], tmp[:, c, s * CTX:(s + 1) * CTX],
                                                  ACT.Identity,
                                                  scale=k.mod[:, l, s, scale * KD + c:scale * KD + c + 1],
                                                  bias=k.mod[:, l, s, shift * KD + c:shift * KD + c + 1])
                    last.then_inc(h_done.sem, 1)

            @block.vector
            def _(dve):
                dve.wait_ge(root_done.sem, root_done.at(1))
                dve.reciprocal(rstd[:, t0:T], rstd[:, t0:T])
                dve.drain()
                for c in range(KD):
                    dve.tensor_tensor(tmp[:, c, t0:T], x[:, c, t0:T], rstd[:, t0:T], ALU.mult).then_inc(scaled.sem, 1)

            @block.tensor
            def _(pe):
                for c in range(KD):
                    pe.wait_ge(sq_done.sem, sq_done.at(c + 1))
                    last = pe.matmul(ps[:, 0:N], k.cst("ones"), tmp[:, c, t0:T], start=c == 0, stop=c == KD - 1)
                last.then_inc(sum_done.sem, 1)
        for s, n in zip((sq_done, sum_done, root_done, scaled, h_done), (KD, 1, 1, KD, KD)):
            s.advance(n)
        if x_source is not None:
            x_in.advance(16 * KD)


def stage_projection(nc, k, l, h, pr, pn, vna, vml):
    NBLK = 8
    win0, win1, tile_done, tile_out, h_saved = k.signals("win_in0", "win_in1", "win_tile", "win_out", "h_saved")
    win_in = (win0, win1)
    with ExitStack() as ctx:
        ring = ctx.enter_context(nc.sbuf_tensor(f"win_ring{l}", [P, 2, KD, 512], F32))
        ps = ctx.enter_context(nc.psum_tensor(f"win_ps{l}", [P, 8, 512], F32))
        with nc.Block() as block:

            @block.sync
            def _(sp):
                def load(j, i):
                    sp.dma_start(ring[:, j], k.d_win[l, bass.ds(i * 2 + j, 1)].rearrange(
                        "a p (k n) -> p (a k) n", k=KD)).then_inc(win_in[j].sem, 16)

                load(0, 0)
                load(1, 0)
                sp.dma_start(k.d_h, h[:]).then_inc(h_saved.sem, 16)
                with sp.Fori(1, (NBLK + 2) // 2) as i:
                    for j in range(2):
                        sp.wait_ge(tile_done.sem, tile_done.at(4 * (j - 1)) + i * 8)
                        load(j, i)
                sp.wait_ge(h_saved.sem, h_saved.at(16))

            @block.gpsimd
            def _(pool):
                pool.memset(k.scratch[:, 0:1], 0.0).then_inc(tile_out.sem, 8)

            @block.tensor
            def _(pe):
                with pe.Fori(0, NBLK // 2) as i:
                    for j in range(2):
                        pe.wait_ge(win_in[j].sem, win_in[j].at(16) + i * 16)
                        for m in range(4):
                            b = j * 4 + m
                            pe.wait_ge(tile_out.sem, tile_out.at(b + 1) + i * 8)
                            for c in range(KD):
                                last = pe.matmul(ps[:, b], ring[:, j, c, m * P:(m + 1) * P], h[:, c],
                                                 start=c == 0, stop=c == KD - 1)
                            last.then_inc(tile_done.sem, 1)
                for j in range(2):
                    pe.wait_ge(win_in[j].sem, win_in[j].at((NBLK // 2) * 16 + 16))
                    for tt in range(4):
                        b = j * 4 + tt
                        pe.wait_ge(tile_out.sem, tile_out.at(NBLK * 4 + b + 1))
                        for c in range(KD):
                            last = pe.matmul(ps[:, b], h[:, c, tt * P:(tt + 1) * P], ring[:, j, c],
                                             start=c == 0, stop=c == KD - 1)
                        last.then_inc(tile_done.sem, 1)

            @block.scalar
            def _(act):
                for half, dst in enumerate((pr, pn)):
                    with act.Fori(0, 2) as i:
                        for b in range(8):
                            act.wait_ge(tile_done.sem, tile_done.at(16 * half + b + 1) + i * 8)
                            act.activation(dst[:, bass.ds(i * 8 + b, 1)].rearrange("p a t -> p (a t)"), ps[:, b],
                                           ACT.Copy).then_inc(tile_out.sem, 1)
                for j, dst in enumerate((vna, vml)):
                    for tt in range(4):
                        act.wait_ge(tile_done.sem, tile_done.at(NBLK * 4 + j * 4 + tt + 1))
                        act.activation(dst[:, tt], ps[:, j * 4 + tt], ACT.Copy).then_inc(tile_out.sem, 1)
        for s, n in zip((win0, win1, tile_done, tile_out, h_saved), (80, 80, 40, 48, 16)):
            s.advance(n)


def stage_attention(nc, k, l, pn, vna):
    qt0 = 0 if l == 0 else 2
    units = [(h, qt) for h in range(HEADS) for qt in range(qt0, 4)]
    NU = len(units)
    (bias_in, sq_done, sum_done, root_done, normed, s_done, max_done, exp_done, p_done, t_done, pt_out, o_done,
     o_out, gq_done) = k.signals("na_bias_in", "na_sq", "na_sum", "na_root", "na_normed", "na_scores", 
                                 "na_max", "na_exp", "na_probs", "na_turned", "na_turned_out", "na_pv", "na_pv_out",
                                 "na_gq")

    def nk(u):
        return CTX if units[u][1] < 2 else T

    with ExitStack() as ctx:
        bias = ctx.enter_context(nc.sbuf_tensor(f"na_bias{l}", [P, HEADS, 2, SEQ], F32))
        sq = ctx.enter_context(nc.sbuf_tensor(f"na_sqb{l}", [P, 2, T], F32))
        rstd = ctx.enter_context(nc.sbuf_tensor(f"na_rstd{l}", [P, 2, T], F32))
        gq = ctx.enter_context(nc.sbuf_tensor(f"na_gqb{l}", [P, 1], F32))
        s = ctx.enter_context(nc.sbuf_tensor(f"na_s{l}", [P, 3, T], F32))
        pt = ctx.enter_context(nc.sbuf_tensor(f"na_pt{l}", [P, 2, 4, P], F32))
        neg = ctx.enter_context(nc.sbuf_tensor(f"na_neg{l}", [P, NU], F32))
        tot = ctx.enter_context(nc.sbuf_tensor(f"na_tot{l}", [P, NU], F32))
        rec = ctx.enter_context(nc.sbuf_tensor(f"na_rec{l}", [P, NU], F32))
        psS = ctx.enter_context(nc.psum_tensor(f"na_psS{l}", [P, 3, 512], F32))
        psT = ctx.enter_context(nc.psum_tensor(f"na_psT{l}", [P, 2, 4, P], F32))
        psO = ctx.enter_context(nc.psum_tensor(f"na_psO{l}", [P, 2, 512], F32))
        with nc.Block(no_gpsimd_drain=True) as block:

            @block.sync
            def _(sp):
                sp.dma_start(bias[:], k.d_nab[l].rearrange("p (h q n) -> p h q n", h=HEADS, q=2)
                             ).then_inc(bias_in.sem, 16)

            @block.scalar
            def _(act):
                def root(i):
                    act.wait_ge(sum_done.sem, sum_done.at(i + 1))
                    if i >= 2:
                        act.wait_ge(normed.sem, normed.at(i - 1))
                    act.activation(rstd[:, i % 2], psO[:, i % 2], ACT.Sqrt, scale=1.0 / HD, bias=k.cst("eps")[:, 0:1]
                                   ).then_inc(root_done.sem, 1)

                for i in range(8):
                    if i >= 2:
                        act.wait_ge(sum_done.sem, sum_done.at(i - 1))
                    act.activation(sq[:, i % 2], pn[:, i], ACT.Square).then_inc(sq_done.sem, 1)
                    if i >= 1:
                        root(i - 1)
                root(7)
                for u in range(NU + 2):
                    if u < NU:
                        act.wait_ge(max_done.sem, max_done.at(u + 1))
                        act.activation(s[:, u % 3, 0:nk(u)], s[:, u % 3, 0:nk(u)], ACT.Exp, bias=neg[:, u:u + 1],
                                       accum_out=tot[:, u:u + 1]).then_inc(exp_done.sem, 1)
                    if u >= 2:
                        act.wait_ge(t_done.sem, t_done.at(u - 1))
                        if u >= 4:
                            act.wait_ge(o_done.sem, o_done.at(u - 3))
                        n = nk(u - 2) // P
                        act.activation(pt[:, u % 2, 0:n], psT[:, u % 2, 0:n], ACT.Copy).then_inc(pt_out.sem, 1)

            @block.vector
            def _(dve):
                dve.tensor_scalar(gq[:], k.par(l, "qn"), HD ** -0.5, None, ALU.mult)
                for i in range(8):
                    dve.wait_ge(root_done.sem, root_done.at(i + 1))
                    dve.reciprocal(rstd[:, i % 2], rstd[:, i % 2])
                    dve.drain()
                    dve.scalar_tensor_tensor(out=pn[:, i], in0=pn[:, i], scalar=gq[:] if i < 4 else k.par(l, "kn"),
                                             in1=rstd[:, i % 2], op0=ALU.mult, op1=ALU.mult).then_inc(normed.sem, 1)
                dve.wait_ge(bias_in.sem, bias_in.at(16))
                for u in range(NU + 3):
                    if u < NU:
                        h, qt = units[u]
                        dve.wait_ge(s_done.sem, s_done.at(u + 1))
                        if u >= 3:
                            dve.wait_ge(t_done.sem, t_done.at(u - 2))
                        dve.tensor_copy(s[:, u % 3, 0:CTX], psS[:, u % 3, 0:CTX])
                        if qt >= 2:
                            dve.tensor_tensor(s[:, u % 3, CTX:T], psS[:, u % 3, CTX:T], bias[:, h, qt - 2], ALU.add)
                        dve.drain()
                        dve.tensor_reduce(neg[:, u:u + 1], s[:, u % 3, 0:nk(u)], AX.X, ALU.max, negate=True
                                          ).then_inc(max_done.sem, 1)
                    if 1 <= u <= NU:
                        v = u - 1
                        dve.wait_ge(exp_done.sem, exp_done.at(v + 1))
                        dve.reciprocal(rec[:, v:v + 1], tot[:, v:v + 1])
                        dve.drain()
                        dve.tensor_scalar(s[:, v % 3, 0:nk(v)], s[:, v % 3, 0:nk(v)], rec[:, v:v + 1], None, ALU.mult
                                          ).then_inc(p_done.sem, 1)
                    if u >= 3:
                        v = u - 3
                        h, qt = units[v]
                        r = (h % 2) * HD
                        dve.wait_ge(o_done.sem, o_done.at(v + 1))
                        dve.tensor_copy(pn[r:r + HD, NQ_T + h // 2, qt * P:(qt + 1) * P], psO[r:r + HD, v % 2, 0:P]
                                        ).then_inc(o_out.sem, 1)

            @block.tensor
            def _(pe):
                for i in range(8):
                    pe.wait_ge(sq_done.sem, sq_done.at(i + 1))
                    if i >= 2:
                        pe.wait_ge(root_done.sem, root_done.at(i - 1))
                    pe.matmul(psO[:, i % 2], k.cst("blk"), sq[:, i % 2], start=True, stop=True
                              ).then_inc(sum_done.sem, 1)
                pe.wait_ge(normed.sem, normed.at(8))

                def scores(u):
                    h, qt = units[u]
                    r = (h % 2) * HD
                    if u >= 3:
                        pe.wait_ge(max_done.sem, max_done.at(u - 2))
                    pe.matmul(psS[:, u % 3, 0:nk(u)], pn[r:r + HD, NQ_T + h // 2, qt * P:(qt + 1) * P],
                              pn[r:r + HD, NK_T + h // 2, 0:nk(u)], start=True, stop=True).then_inc(s_done.sem, 1)

                def turn(u):
                    pe.wait_ge(p_done.sem, p_done.at(u + 1))
                    if u >= 2:
                        pe.wait_ge(pt_out.sem, pt_out.at(u - 1))
                    for j in range(nk(u) // P):
                        last = pe.transpose(psT[:, u % 2, j], s[:, u % 3, j * P:(j + 1) * P], k.cst("ident"))
                    last.then_inc(t_done.sem, 1)

                def mix(u):
                    h, qt = units[u]
                    r = (h % 2) * HD
                    n = nk(u) // P
                    pe.wait_ge(pt_out.sem, pt_out.at(u + 1))
                    if u >= 2:
                        pe.wait_ge(o_out.sem, o_out.at(u - 1))
                    for j in range(n):
                        last = pe.matmul(psO[r:r + HD, u % 2, 0:P], vna[:, j, h * HD:(h + 1) * HD], pt[:, u % 2, j],
                                         start=j == 0, stop=j == n - 1)
                    last.then_inc(o_done.sem, 1)

                scores(0)
                scores(1)
                for u in range(NU + 1):
                    if u + 2 < NU:
                        scores(u + 2)
                    if u < NU:
                        turn(u)
                    if u >= 1:
                        mix(u - 1)
        for sg, n in zip((bias_in, sq_done, sum_done, root_done, normed, s_done, max_done, exp_done, p_done,
                          t_done, pt_out, o_done, o_out), (16, 8, 8, 8, 8) + (NU,) * 8):
            sg.advance(n)


def stage_mlstm(nc, k, l, pr, pn, vml):
    (cap_in, tanh_done, sig_done, log_done, b_done, gt_ps, gt_done, rot_ps, rot_done, cst_in, qk_done, bb_done, bs_done, arg_done,
     w_done, pw_done, nd_done, h_dir, hsq_done, hsum_done, hroot_done, o_sig, h_out) = k.signals(
        "ml_cap_in", "ml_tanh", "ml_sigmoid", "ml_log", "ml_b", "ml_gate_turned", "ml_gate_out", "ml_rot_ps", "ml_rot",
        "ml_cst_in", "ml_scores", "ml_bcast", "ml_bcast_out", "ml_arg", "ml_weight", "ml_weighted", "ml_numden", "ml_dir", "ml_hsq",
        "ml_hsum", "ml_hroot", "ml_osig", "ml_out")
    with ExitStack() as ctx:
        def sb(name, shape):
            return ctx.enter_context(nc.sbuf_tensor(f"ml_{name}{l}", shape, F32))

        def pp(name, shape):
            return ctx.enter_context(nc.psum_tensor(f"ml_{name}{l}", shape, F32))

        mc = sb("mc", [P, NMLC])
        cap = sb("cap", [P, 1])
        lf = sb("lf", [8, T])
        ig = sb("ig", [8, T])
        F = sb("F", [8, T])
        side = sb("side", [8, T])
        b = sb("b", [8, T])
        g = sb("g", [8, T])
        gc = sb("gc", [8, CTX])
        gT = sb("gT", [P, 6, 8])
        rot = sb("rot", [P, 4, SEQ])
        w = sb("w", [P, 4, T])
        pw = sb("pw", [P, 3, T])
        den = sb("den", [P, T])
        hh = sb("hh", [P, T])
        bs = sb("bs", [P, T])
        hd = sb("hd", [P, T])
        os = sb("os", [P, T])
        psA = pp("psA", [P, 3, 512])
        psB = pp("psB", [P, 512])
        psN = pp("psN", [P, 512])
        psD = pp("psD", [P, 512])
        psM = pp("psM", [P, 2, 512])
        mask = mc[:, 0:4 * SEQ].rearrange("p (d i n) -> p d i n", d=2, i=2)
        sel = mc[0:8, 4 * SEQ:].rearrange("p (r n) -> p r n", r=8)
        units = [(h, d) for h in range(ML_HEADS) for d in range(2)]
        with nc.Block(no_gpsimd_drain=True) as block:

            @block.sync
            def _(sp):
                sp.dma_start(mc[:], k.d_mlc).then_inc(cst_in.sem, 16)

            @block.scalar
            def _(act):
                act.wait_ge(cap_in.sem, cap_in.at(1))
                act.activation(ig[:], pr[0:8, GATE_T], ACT.Tanh, scale=1 / GATE_CAP, bias=cap[0:8]
                               ).then_inc(tanh_done.sem, 1)
                act.activation(pr[32:40, GATE_T], pr[32:40, GATE_T], ACT.Tanh, scale=1 / GATE_CAP, bias=cap[32:40]
                               ).then_inc(tanh_done.sem, 1)
                act.wait_ge(tanh_done.sem, tanh_done.at(2))
                act.activation(pr[32:40, GATE_T], pr[32:40, GATE_T], ACT.Sigmoid, scale=GATE_CAP
                               ).then_inc(sig_done.sem, 1)
                act.wait_ge(sig_done.sem, sig_done.at(1))
                act.activation(lf[:], pr[32:40, GATE_T], ACT.Ln).then_inc(log_done.sem, 1)
                act.wait_ge(gt_ps.sem, gt_ps.at(1))
                act.activation(gT[:], psM[:, 1, 0:48].rearrange("p (i r) -> p i r", i=6), ACT.Copy
                               ).then_inc(gt_done.sem, 1)
                act.wait_ge(gt_done.sem, gt_done.at(1))
                for u, (h, d) in enumerate(units):
                    row = d * 4 + h
                    act.wait_ge(bb_done.sem, bb_done.at(u + 1))
                    if u:
                        act.wait_ge(pw_done.sem, pw_done.at(3 * u))
                    act.activation(bs[:], psB[:], ACT.Copy).then_inc(bs_done.sem, 1)
                    act.wait_ge(bs_done.sem, bs_done.at(u + 1))
                    for i in range(2):
                        act.activation(w[:, i, CTX:T], bs[:, CTX:T], ACT.Exp, bias=gT[:, 4 + i, row:row + 1])
                    for i in range(2):
                        act.wait_ge(arg_done.sem, arg_done.at(4 * u + 1 + i))
                        act.activation(w[:, i, 0:CTX], w[:, i, 0:CTX], ACT.Exp, bias=gT[:, i, row:row + 1]
                                       ).then_inc(w_done.sem, 1)
                    for i in range(2):
                        act.wait_ge(arg_done.sem, arg_done.at(4 * u + 3 + i))
                        last = act.activation(w[:, 2, i * SEQ:(i + 1) * SEQ], w[:, 2, i * SEQ:(i + 1) * SEQ], ACT.Exp,
                                              bias=gT[:, 2 + i, row:row + 1])
                    last.then_inc(w_done.sem, 1)
                    if d == 1:
                        act.activation(os[:], pn[:, MO_T + h], ACT.Sigmoid).then_inc(o_sig.sem, 1)
                        act.wait_ge(h_dir.sem, h_dir.at(u + 1))
                        act.activation(hd[:], hh[:], ACT.Square).then_inc(hsq_done.sem, 1)
                        act.wait_ge(hsum_done.sem, hsum_done.at(h + 1))
                        act.activation(hd[:], psM[:, 0], ACT.Sqrt, scale=1.0 / P, bias=k.cst("eps")[:, 0:1]
                                       ).then_inc(hroot_done.sem, 1)

            @block.vector
            def _(dve):
                dve.tensor_scalar(cap[0:8], k.par(l, "ib", 8), 1 / GATE_CAP, None, ALU.mult)
                dve.tensor_scalar(cap[32:40], k.par_sb[32:40, l * NPAR + PAR["fb"][0]:l * NPAR + PAR["fb"][0] + 1],
                                  1 / GATE_CAP, None, ALU.mult).then_inc(cap_in.sem, 1)
                for i in range(4):
                    dve.wait_ge(rot_ps.sem, rot_ps.at(i + 1))
                    dve.tensor_tensor(rot[:, i], psM[:, 0, 0:SEQ] if i % 2 == 0 else psN[:, 0:SEQ], k.cst("sin"),
                                      ALU.mult)
                    dve.tensor_tensor(pn[:, MQ_T + i, CTX:T], pn[:, MQ_T + i, CTX:T], k.cst("cos"), ALU.mult)
                    dve.drain()
                    dve.tensor_tensor(pn[:, MQ_T + i, CTX:T], pn[:, MQ_T + i, CTX:T], rot[:, i], ALU.add
                                      ).then_inc(rot_done.sem, 1)
                dve.wait_ge(log_done.sem, log_done.at(1))
                dve.tensor_scalar(ig[:], ig[:], GATE_CAP, None, ALU.mult)
                dve.tensor_tensor_scan(F[:], k.cst("segres", 8), lf[:], 0.0, ALU.mult, ALU.add)
                dve.drain()
                sgn = k.cst("sgn", 8)
                for s in range(2):
                    dve.tensor_scalar(side[:, s * SEQ:(s + 1) * SEQ], lf[:, s * SEQ:(s + 1) * SEQ],
                                      F[:, (s + 1) * SEQ - 1:(s + 1) * SEQ], sgn[:, 1:2], ALU.add, ALU.mult)
                dve.drain()
                dve.scalar_tensor_tensor(out=b[:], in0=F[:], scalar=sgn[:, 0:1], in1=side[:], op0=ALU.mult,
                                         op1=ALU.add)
                dve.drain()
                dve.tensor_tensor(g[:], ig[:], b[:], ALU.subtract)
                dve.drain()
                dve.tensor_scalar(gc[:], g[:, 0:CTX], F[:, CTX - 1:CTX], None, ALU.add).then_inc(b_done.sem, 1)
                dve.wait_ge(cst_in.sem, cst_in.at(16))
                for u, (h, d) in enumerate(units):
                    dve.wait_ge(bs_done.sem, bs_done.at(u + 1))
                    if u:
                        dve.drain()
                    for i in range(2):
                        dve.tensor_tensor(w[:, i, 0:CTX], bs[:, 0:CTX], mask[:, d, i], ALU.add
                                          ).then_inc(arg_done.sem, 1)
                    for i in range(2):
                        dve.tensor_tensor(w[:, 2, i * SEQ:(i + 1) * SEQ], bs[:, CTX:T], mask[:, d, i], ALU.add
                                          ).then_inc(arg_done.sem, 1)
                    if d == 0:
                        dve.wait_ge(qk_done.sem, qk_done.at(h + 1))
                    if u:
                        dve.wait_ge(nd_done.sem, nd_done.at(u))
                    for i in range(3):
                        dve.wait_ge(w_done.sem, w_done.at(3 * u + i + 1))
                        dve.scalar_tensor_tensor(out=pw[:, i], in0=psA[:, i], scalar=HD ** -0.5, in1=w[:, i],
                                                 op0=ALU.mult, op1=ALU.mult).then_inc(pw_done.sem, 1)
                    dve.wait_ge(nd_done.sem, nd_done.at(u + 1))
                    dve.tensor_scalar(den[:], psD[:], -1.0, 1.0, ALU.mult, ALU.max)
                    dve.drain()
                    dve.tensor_tensor(den[:], psD[:], den[:], ALU.max)
                    dve.drain()
                    dve.reciprocal(den[:], den[:])
                    dve.drain()
                    if d == 0:
                        dve.tensor_tensor(hh[:], psN[:], den[:], ALU.mult).then_inc(h_dir.sem, 1)
                    else:
                        dve.tensor_tensor(den[:], psN[:], den[:], ALU.mult)
                        dve.drain()
                        dve.tensor_tensor(hh[:], hh[:], den[:], ALU.add).then_inc(h_dir.sem, 1)
                        dve.wait_ge(hroot_done.sem, hroot_done.at(h + 1))
                        dve.reciprocal(hd[:], hd[:])
                        dve.drain()
                        dve.scalar_tensor_tensor(out=hh[:], in0=hh[:], scalar=k.par(l, "mg")[:, h:h + 1], in1=hd[:],
                                                 op0=ALU.mult, op1=ALU.mult)
                        dve.drain()
                        dve.wait_ge(o_sig.sem, o_sig.at(h + 1))
                        dve.tensor_tensor(pn[:, MO_T + h], hh[:], os[:], ALU.mult).then_inc(h_out.sem, 1)
                        dve.drain()

            @block.tensor
            def _(pe):
                for i in range(4):
                    if i >= 2:
                        pe.wait_ge(rot_done.sem, rot_done.at(i - 1))
                    pe.matmul(psM[:, 0, 0:SEQ] if i % 2 == 0 else psN[:, 0:SEQ], k.cst("perm"), pn[:, MQ_T + i, CTX:T],
                              start=True, stop=True).then_inc(rot_ps.sem, 1)
                pe.wait_ge(b_done.sem, b_done.at(1))
                for i in range(6):
                    src = g[:, i * P:(i + 1) * P] if i < 4 else gc[:, (i - 4) * P:(i - 3) * P]
                    last = pe.transpose(psM[:, 1, i * 8:(i + 1) * 8], src, k.cst("ident", 8)[:, 0:8])
                last.then_inc(gt_ps.sem, 1)
                pe.wait_ge(rot_done.sem, rot_done.at(4))
                pe.wait_ge(cst_in.sem, cst_in.at(16))
                for u, (h, d) in enumerate(units):
                    r = (h % 2) * HD
                    kt, qt = MK_T + h // 2, MQ_T + h // 2
                    if u:
                        pe.wait_ge(pw_done.sem, pw_done.at(3 * u))
                    pe.matmul(psB[:], sel[:, d * 4 + h], b[:], start=True, stop=True).then_inc(bb_done.sem, 1)
                    if d == 0:
                        for i in range(2):
                            pe.matmul(psA[:, i], pn[r:r + HD, kt, i * P:(i + 1) * P], pn[r:r + HD, qt],
                                      start=True, stop=True)
                        for i in range(2):
                            last = pe.matmul(psA[:, 2, i * SEQ:(i + 1) * SEQ],
                                             pn[r:r + HD, kt, CTX + i * P:CTX + (i + 1) * P], pn[r:r + HD, qt, CTX:T],
                                             start=True, stop=True)
                        last.then_inc(qk_done.sem, 1)
                    if u:
                        pe.wait_ge(h_dir.sem, h_dir.at(u))
                    for ps, lhs in ((psN, lambda i: vml[:, i, h * P:(h + 1) * P]), (psD, lambda i: k.cst("ones"))):
                        for i in range(4):
                            pe.wait_ge(pw_done.sem, pw_done.at(3 * u + min(i, 2) + 1))
                            if i < 2:
                                last = pe.matmul(ps[:], lhs(i), pw[:, i], start=i == 0, stop=False)
                            else:
                                last = pe.matmul(ps[:, CTX:T], lhs(i), pw[:, 2, (i - 2) * SEQ:(i - 1) * SEQ],
                                                 start=False, stop=i == 3)
                    last.then_inc(nd_done.sem, 1)
                    if d == 1:
                        pe.wait_ge(hsq_done.sem, hsq_done.at(h + 1))
                        if h:
                            pe.wait_ge(hroot_done.sem, hroot_done.at(h))
                        pe.matmul(psM[:, 0], k.cst("ones"), hd[:], start=True, stop=True).then_inc(hsum_done.sem, 1)
        for sg, n in zip((cap_in, tanh_done, sig_done, log_done, b_done, gt_ps, gt_done, rot_ps, rot_done, cst_in,
                          qk_done, bb_done, bs_done, arg_done, w_done, pw_done, nd_done, h_dir, hsq_done, hsum_done, hroot_done,
                          o_sig, h_out),
                         (1, 2, 1, 1, 1, 1, 1, 4, 4, 16, 4, 8, 8, 32, 24, 24, 8, 8, 4, 4, 4, 4, 4)):
            sg.advance(n)


def stage_rwkv_features(nc, k, l, pr, sg, aa, kk, ka, g):
    (w_in, mix_done, sum_done, own_done, shifted, act_done, lora_done, lora_out, vf_moved, low_out, gate_out, v_done,
     ksq_done, ksum_done, kroot_done, kk_done) = k.signals(
        "rw_w_in", "rw_mix", "rw_shift_sum", "rw_shift_own", "rw_shifted", "rw_lora_in", "rw_lora", "rw_lora_out",
        "rw_vf", "rw_low_out", "rw_vgate", "rw_v", "rw_ksq", "rw_ksum", "rw_kroot", "rw_kk")
    NT = 15
    jobs = [("w", d, c) for d in range(2) for c in range(KC)] + [("a", d, c) for d in range(2) for c in range(KC)] + \
        [("g", None, c) for c in range(KC)]
    if l:
        jobs += [("v1", None, 0)] + [("v2", None, c) for c in range(KC)]
    with ExitStack() as ctx:
        def sb(name, shape):
            return ctx.enter_context(nc.sbuf_tensor(f"rf_{name}{l}", shape, F32))

        lw = sb("lw", [P, 3 * C + KC * 32 + C])
        m1 = sb("m1", [P, NT])
        mh = sb("mh", [P, NT])
        oka = sb("oka", [P, KC])
        s = sb("s", [P, 2, T])
        sq = sb("sq", [P, 2, T])
        root = sb("root", [P, 2, T])
        if l:
            vf = sb("vf", [P, KC, T])
            vs = sb("vs", [P, KC, T])
            low = sb("low", [32, T])
        ps = ctx.enter_context(nc.psum_tensor(f"rf_ps{l}", [P, 4, 512], F32))
        psK = ctx.enter_context(nc.psum_tensor(f"rf_psK{l}", [P, 2, 512], F32))
        w2, a2, g2 = lw[:, 0:C], lw[:, C:2 * C], lw[:, 2 * C:3 * C]
        v1 = lw[:, 3 * C:3 * C + KC * 32].rearrange("p (c n) -> p c n", c=KC)
        v2 = lw[0:32, 3 * C + KC * 32:]
        with nc.Block(no_gpsimd_drain=True) as block:

            @block.sync
            def _(sp):
                sp.dma_start(lw[:], k.d_lora[l]).then_inc(w_in.sem, 16)
                if l:
                    sp.dma_start(vf[:], k.d_vf).then_inc(vf_moved.sem, 16)
                else:
                    sp.wait_ge(shifted.sem, shifted.at(NT))
                    sp.dma_start(k.d_vf, pr[:, V_T:V_T + KC]).then_inc(vf_moved.sem, 16)
                    sp.wait_ge(vf_moved.sem, vf_moved.at(16))

            @block.scalar
            def _(act):
                act.wait_ge(mix_done.sem, mix_done.at(1))
                for i in range(NT):
                    act.wait_ge(sum_done.sem, sum_done.at(i + 1))
                    act.activation(pr[:, i], pr[:, i], ACT.Identity, scale=m1[:, i:i + 1]).then_inc(own_done.sem, 1)
                act.wait_ge(shifted.sem, shifted.at(NT))
                act.activation(pr[:, WD_T], pr[:, WD_T], ACT.Tanh).then_inc(act_done.sem, 1)
                act.activation(pr[:, GD_T], pr[:, GD_T], ACT.Sigmoid).then_inc(act_done.sem, 1)
                for n, (kind, d, c) in enumerate(jobs):
                    act.wait_ge(lora_done.sem, lora_done.at(n + 1))
                    if kind == "w":
                        last = act.activation(sg[:, d, c], ps[:, n % 4], ACT.Sigmoid,
                                              bias=k.par(l, "w0")[:, d * KC + c:d * KC + c + 1])
                    elif kind == "a":
                        last = act.activation(aa[:, d, c], ps[:, n % 4], ACT.Sigmoid,
                                              bias=k.par(l, "a0")[:, d * KC + c:d * KC + c + 1])
                    elif kind == "g":
                        last = act.activation(g[:, c], ps[:, n % 4], ACT.Copy)
                    elif kind == "v1":
                        last = act.activation(low[:], ps[0:32, n % 4], ACT.Copy)
                    else:
                        last = act.activation(vs[:, c], ps[:, n % 4], ACT.Sigmoid, bias=k.par(l, "v0")[:, c:c + 1])
                    last.then_inc(lora_out.sem, 1)
                for c in range(KC):
                    act.wait_ge(ksum_done.sem, ksum_done.at(c + 1))
                    if c >= 2:
                        act.wait_ge(kk_done.sem, kk_done.at(c - 1))
                    act.activation(root[:, c % 2], psK[:, c % 2], ACT.Sqrt).then_inc(kroot_done.sem, 1)

            @block.vector
            def _(dve):
                mu = k.par(l, "mu")
                dve.tensor_scalar(m1[:], mu, -1.0, 1.0, ALU.mult, ALU.add)
                dve.tensor_scalar(oka[:], k.par(l, "ka"), -1.0, 1.0, ALU.mult, ALU.add)
                dve.tensor_scalar(mh[:], mu, 0.5, None, ALU.mult).then_inc(mix_done.sem, 1)

                def both(ap):
                    return ap.rearrange("p (s t) -> p s t", s=2)

                def finish(i):
                    dve.wait_ge(own_done.sem, own_done.at(i + 1))
                    dve.scalar_tensor_tensor(out=pr[:, i], in0=s[:, i % 2], scalar=mh[:, i:i + 1], in1=pr[:, i],
                                             op0=ALU.mult, op1=ALU.add).then_inc(shifted.sem, 1)

                for i in range(NT):
                    z, o = both(pr[:, i]), both(s[:, i % 2])
                    dve.drain()
                    dve.tensor_tensor(o[:, :, 1:SEQ - 1], z[:, :, 0:SEQ - 2], z[:, :, 2:SEQ], ALU.add)
                    dve.tensor_copy(o[:, :, 0:SEQ:SEQ - 1], z[:, :, 1:SEQ - 1:SEQ - 3]).then_inc(sum_done.sem, 1)
                    if i:
                        finish(i - 1)
                dve.drain()
                finish(NT - 1)
                dve.drain()
                for c in range(KC):
                    dve.tensor_scalar(kk[:, c], pr[:, K_T + c], k.par(l, "kk")[:, c:c + 1], None, ALU.mult)
                    dve.drain()
                    if c >= 2:
                        dve.wait_ge(ksum_done.sem, ksum_done.at(c - 1))
                    dve.tensor_tensor(sq[:, c % 2], kk[:, c], kk[:, c], ALU.mult).then_inc(ksq_done.sem, 1)
                for c in range(KC):
                    dve.tensor_scalar(ka[:, c], pr[:, K_T + c], k.par(l, "ka")[:, c:c + 1], None, ALU.mult)
                    dve.tensor_scalar(pr[:, K_T + c], pr[:, K_T + c], oka[:, c:c + 1], None, ALU.mult)
                for c in range(KC):
                    dve.wait_ge(kroot_done.sem, kroot_done.at(c + 1))
                    dve.tensor_scalar(root[:, c % 2], root[:, c % 2], 1e-12, None, ALU.max)
                    dve.drain()
                    dve.reciprocal(root[:, c % 2], root[:, c % 2])
                    dve.drain()
                    dve.tensor_tensor(kk[:, c], kk[:, c], root[:, c % 2], ALU.mult).then_inc(kk_done.sem, 1)
                if l:
                    dve.wait_ge(vf_moved.sem, vf_moved.at(16))
                    dve.wait_ge(lora_out.sem, lora_out.at(len(jobs)))
                    for c in range(KC):
                        dve.tensor_tensor(vf[:, c], vf[:, c], pr[:, V_T + c], ALU.subtract)
                    dve.drain()
                    for c in range(KC):
                        dve.tensor_tensor(vf[:, c], vf[:, c], vs[:, c], ALU.mult)
                    dve.drain()
                    for c in range(KC):
                        dve.tensor_tensor(pr[:, V_T + c], pr[:, V_T + c], vf[:, c], ALU.add)

            @block.tensor
            def _(pe):
                pe.wait_ge(w_in.sem, w_in.at(16))
                pe.wait_ge(act_done.sem, act_done.at(2))
                for n, (kind, d, c) in enumerate(jobs):
                    if n >= 4:
                        pe.wait_ge(lora_out.sem, lora_out.at(n - 3))
                    o = ps[:, n % 4]
                    if kind in "wa":
                        src, wt = (pr[:, WD_T], w2) if kind == "w" else (pr[:, AD_T], a2)
                        r = d * HD
                        last = pe.matmul(o, wt[r:r + HD, c * P:(c + 1) * P], src[r:r + HD], start=True, stop=True)
                    elif kind == "g":
                        last = pe.matmul(o, g2[:, c * P:(c + 1) * P], pr[:, GD_T], start=True, stop=True)
                    elif kind == "v1":
                        for i in range(KC):
                            last = pe.matmul(ps[0:32, n % 4], v1[:, i], pr[:, V_T + i], start=i == 0, stop=i == KC - 1)
                    else:
                        if c == 0:
                            pe.wait_ge(lora_out.sem, lora_out.at(n))
                        last = pe.matmul(o, v2[:, c * P:(c + 1) * P], low[:], start=True, stop=True)
                    last.then_inc(lora_done.sem, 1)
                for c in range(KC):
                    pe.wait_ge(ksq_done.sem, ksq_done.at(c + 1))
                    if c >= 2:
                        pe.wait_ge(kroot_done.sem, kroot_done.at(c - 1))
                    pe.matmul(psK[:, c % 2], k.cst("blk"), sq[:, c % 2], start=True, stop=True
                              ).then_inc(ksum_done.sem, 1)
        for x, n in zip((w_in, mix_done, sum_done, own_done, shifted, act_done, lora_done, lora_out, vf_moved,
                         ksq_done, ksum_done, kroot_done, kk_done),
                        (16, 1, NT, NT, NT, 2, len(jobs), len(jobs), 16, KC, KC, KC, KC)):
            x.advance(n)


def stage_rwkv_scan(nc, k, l, pr, sg, aa, kk, ka, y):
    names = ("gates", "exps", "feats", "mats", "turned", "masked", "parts", "tok", "cmask", "x", "xi", "nn", "nout",
             "rhs", "rhsout", "u", "uout", "sy", "yout", "state")
    per_step = dict(gates=1, exps=1, feats=1, mats=1, turned=1, masked=1, parts=1, tok=1, cmask=1, x=6, xi=6, nn=5,
                    nout=5, rhs=1, rhsout=1, u=1, uout=1, sy=1, yout=1, state=1)
    sem = [dict(zip(names, k.signals(*[f"scan{d}_{n}" for n in names]))) for d in range(2)]
    (waited,) = k.signals("scan_waited")
    NCH = SEQ // L
    with ExitStack() as ctx:
        def sb(name, shape):
            return [ctx.enter_context(nc.sbuf_tensor(f"sc_{name}{l}{d}", shape, F32)) for d in range(2)]

        sgs = sb("sgs", [P, KC, L])
        F = sb("F", [P, KC, L])
        E = sb("E", [P, KC, L])
        R = sb("R", [P, KC, L])
        Z = sb("Z", [P, KC, L])
        vst = sb("vst", [P, KC, L])
        ex = sb("ex", [P, 4, KC, L])
        bb, kd, S2 = E, R, Z
        ra = sb("ra", [P, KC, 2, L])
        hat = sb("hat", [P, KC, 3, L])
        pri = sb("pri", [P, KC, 3, L])
        M = sb("M", [P, 2, KC, P])
        at = sb("at", [P, KC, L])
        cm = [pr[:, WD_T:WD_T + 3].rearrange("p a (b c n) -> p (a b) c n", b=2, c=KC),
              ctx.enter_context(nc.sbuf_tensor(f"sc_cm{l}", [P, 6, KC, L], F32))[:]]
        N = sb("N", [P, KC, L])
        NT = sb("NT", [P, KC, L])
        XI = sb("XI", [P, KC, L])
        bk = sb("bk", [P, HEADS, L])
        uv = sb("uv", [P, HEADS, L])
        rhs = sb("rhsb", [P, KC, L])
        S = sb("S", [P, KC, L])
        wl = sb("wl", [P, KC])
        ps = [ctx.enter_context(nc.psum_tensor(f"sc_ps{l}{d}", [P, 4, 512], F32)) for d in range(2)]

        def half(d, bank, i):
            return ps[d][:, bank, i * 256:(i + 1) * 256].rearrange("p (c n) -> p c n", c=KC)

        psA = [ps[d][:, 0:2].rearrange("p b (h n) -> p b h n", n=P) for d in range(2)]
        psX = [half(d, 0, 0) for d in range(2)]
        psN = [half(d, 0, 1) for d in range(2)]
        psNT = [half(d, 1, 0) for d in range(2)]
        psR = [half(d, 3, 1) for d in range(2)]
        psBK = [[half(d, 2 + o, 0) for o in range(2)] for d in range(2)]
        psV = [[half(d, 2 + o, 1) for o in range(2)] for d in range(2)]
        psAV = [half(d, 2, 1) for d in range(2)]
        psU = [half(d, 2, 0) for d in range(2)]
        psS = [half(d, 2, 1) for d in range(2)]
        psY = [half(d, 3, 0) for d in range(2)]

        def columns(d, seg, i):
            return bass.ds(seg * SEQ + (i * L if d == 0 else (NCH - 1) * L - i * L), L)

        def w(eng, d, name, seg, i, n=1):
            s, m = sem[d][name], per_step[name]
            eng.wait_ge(s.sem, s.at(n) + (seg * NCH + i) * m)

        eye = k.cst("eye").unsqueeze(1).broadcast_to([P, KC, L])
        with nc.Block(no_gpsimd_drain=True) as block:

            @block.scalar
            def _(act):
                with act.Fori(0, 2) as seg, act.Fori(0, NCH) as i:
                    for d in range(2):
                        w(act, d, "gates", seg, i)
                        incl, excl, prime = (F, E, R) if d == 0 else (Z, R, E)
                        act.activation(wl[d][:], F[d][:, :, L - 1], ACT.Exp, scale=-DECAY)
                        act.activation(ex[d][:, 0], incl[d][:], ACT.Exp, scale=-DECAY)
                        act.activation(ex[d][:, 1], excl[d][:], ACT.Exp, scale=-DECAY)
                        act.activation(ex[d][:, 2], incl[d][:], ACT.Exp, scale=DECAY)
                        act.activation(ex[d][:, 3], prime[d][:], ACT.Exp, scale=-DECAY).then_inc(sem[d]["exps"].sem, 1)
                    for d in range(2):
                        w(act, d, "turned", seg, i)
                        act.activation(bk[d][:, 0:HEADS:2], psBK[d][0], ACT.Copy)
                        act.activation(bk[d][:, 1:HEADS:2], psBK[d][1], ACT.Copy)
                        act.activation(uv[d][HD:P, 0:HEADS:2], psV[d][0][HD:P], ACT.Copy)
                        act.activation(uv[d][0:HD, 1:HEADS:2], psV[d][1][0:HD], ACT.Copy
                                       ).then_inc(sem[d]["tok"].sem, 1)
                        w(act, d, "masked", seg, i)
                        act.activation(at[d][0:HD], M[d][0:HD, 0, :, L:P], ACT.Copy)
                        act.activation(at[d][HD:P], M[d][HD:P, 1, :, L:P], ACT.Copy
                                       ).then_inc(sem[d]["parts"].sem, 1)
                    for m in range(1, 6):
                        for d in range(2):
                            w(act, d, "nn", seg, i, m)
                            if m < 5:
                                act.activation(N[d][:], psN[d], ACT.Copy)
                            act.activation(NT[d][:], psNT[d], ACT.Copy).then_inc(sem[d]["nout"].sem, 1)
                    for d in range(2):
                        w(act, d, "u", seg, i)
                        act.activation(uv[d][0:HD, 0:HEADS:2], psU[d][0:HD], ACT.Copy)
                        act.activation(uv[d][HD:P, 1:HEADS:2], psU[d][HD:P], ACT.Copy).then_inc(sem[d]["uout"].sem, 1)
                    for d in range(2):
                        w(act, d, "sy", seg, i)
                        act.activation(y[:, d, :, columns(d, seg, i)], psY[d], ACT.Copy
                                       ).then_inc(sem[d]["yout"].sem, 1)

            @block.vector
            def _(dve):
                for d in range(2):
                    dve.memset(S[d][:], 0.0)
                dve.drain()
                with dve.Fori(0, 2) as seg, dve.Fori(0, NCH) as i:
                    for d in range(2):
                        col = columns(d, seg, i)
                        dve.tensor_copy(sgs[d][:], sg[:, d, :, col])
                        dve.tensor_copy(vst[d][:], pr[:, V_T:V_T + KC, col])
                        dve.drain()
                        dve.tensor_tensor_scan(F[d][:].rearrange("p c n -> p (c n)"), k.cst("reset"),
                                               sgs[d][:].rearrange("p c n -> p (c n)"), 0.0, ALU.mult, ALU.add)
                        dve.drain()
                        dve.tensor_tensor(R[d][:], F[d][:, :, L - 1:L].broadcast_to([P, KC, L]), F[d][:],
                                          ALU.subtract)
                        dve.tensor_tensor(E[d][:], F[d][:], sgs[d][:], ALU.subtract)
                        dve.drain()
                        dve.tensor_tensor(Z[d][:], R[d][:], sgs[d][:], ALU.add).then_inc(sem[d]["gates"].sem, 1)
                    for d in range(2):
                        col = columns(d, seg, i)
                        w(dve, d, "exps", seg, i)
                        dve.tensor_tensor(bb[d][:], kk[:, :, col], aa[:, d, :, col], ALU.mult)
                        dve.tensor_tensor(kd[d][:], ka[:, :, col], aa[:, d, :, col], ALU.mult)
                        dve.drain()
                        dve.tensor_tensor(kd[d][:], kd[d][:], pr[:, K_T:K_T + KC, col], ALU.add)
                        dve.tensor_tensor(ra[d][:, :, 0], pr[:, R_T:R_T + KC, col], ex[d][:, 0], ALU.mult)
                        dve.scalar_tensor_tensor(out=ra[d][:, :, 1], in0=kk[:, :, col], scalar=-1.0,
                                                 in1=ex[d][:, 1], op0=ALU.mult, op1=ALU.mult)
                        dve.drain()
                        for o, e in ((hat, 2), (pri, 3)):
                            dve.tensor_tensor(o[d][:, :, 0], bb[d][:], ex[d][:, e], ALU.mult)
                            dve.tensor_tensor(o[d][:, :, 1], kd[d][:], ex[d][:, e], ALU.mult)
                            last = dve.tensor_tensor(o[d][HD:P, :, 2], bb[d][HD:P], ex[d][HD:P, e], ALU.mult)
                        last.then_inc(sem[d]["feats"].sem, 1)
                    for d in range(2):
                        w(dve, d, "mats", seg, i)
                        for o in range(2):
                            last = dve.tensor_tensor(M[d][:, o], psA[d][:, o],
                                                     k.cst(f"mra{d}").unsqueeze(1).broadcast_to([P, KC, P]), ALU.mult)
                        last.then_inc(sem[d]["masked"].sem, 1)
                    for d in range(2):
                        w(dve, d, "parts", seg, i)
                        lev = k.cst(f"lev{d}").rearrange("p (m n) -> p m n", m=6)
                        for m in range(6):
                            last = dve.tensor_tensor(cm[d][:, m], at[d][:],
                                                     lev[:, m].unsqueeze(1).broadcast_to([P, KC, L]), ALU.mult)
                        dve.drain()
                        dve.tensor_tensor(NT[d][:], cm[d][:, 0], eye, ALU.add).then_inc(sem[d]["cmask"].sem, 1)
                    for m in range(6):
                        for d in range(2):
                            w(dve, d, "x", seg, i, m + 1)
                            dve.tensor_tensor(N[d][:] if m == 0 else XI[d][:], psX[d], eye, ALU.add
                                              ).then_inc(sem[d]["xi"].sem, 1)
                    for d in range(2):
                        w(dve, d, "rhs", seg, i)
                        dve.tensor_copy(rhs[d][:], psR[d])
                        dve.drain()
                        dve.tensor_tensor(rhs[d][:], rhs[d][:], psAV[d], ALU.add).then_inc(sem[d]["rhsout"].sem, 1)
                        dve.tensor_tensor(S2[d][:], S[d][:], wl[d][:].unsqueeze(2).broadcast_to([P, KC, L]), ALU.mult)
                    dve.drain()
                    for d in range(2):
                        w(dve, d, "sy", seg, i)
                        dve.tensor_tensor(S[d][:], S2[d][:], psS[d], ALU.add).then_inc(sem[d]["state"].sem, 1)
                    dve.drain()
                    for d in range(2):
                        w(dve, d, "yout", seg, i)

            @block.tensor
            def _(pe):
                heads = [(h, h // 2, (h % 2) * HD) for h in range(HEADS)]
                def wp(d, name, seg, i, n=1):
                    w(pe, d, name, seg, i, n)
                    pe.sem_inc(waited.sem, 1)

                with pe.Fori(0, 2) as seg, pe.Fori(0, NCH) as i:
                    for d in range(2):
                        w(pe, d, "feats", seg, i)
                        for h, hp, r in heads:
                            o = h % 2
                            last = pe.matmul(psA[d][:, o, hp], hat[d][r:r + HD, hp, o:o + 2].rearrange("p a n -> p (a n)"),
                                             ra[d][r:r + HD, hp].rearrange("p a n -> p (a n)"), start=True, stop=True)
                        last.then_inc(sem[d]["mats"].sem, 1)
                        for h, hp, r in heads:
                            o = h % 2
                            pe.transpose(psBK[d][o][:, hp], pri[d][r:r + HD, hp, o:o + 2].rearrange("p a n -> p (a n)"),
                                         k.cst("ident")[r:r + HD, r:r + HD])
                        for h, hp, r in heads:
                            q = HD - r
                            last = pe.matmul(psV[d][h % 2][q:q + HD, hp], vst[d][r:r + HD, hp],
                                             k.cst("ident")[r:r + HD, r:r + HD], start=True, stop=True)
                        last.then_inc(sem[d]["turned"].sem, 1)
                    for m in range(6):
                        for d in range(2):
                            if m == 0:
                                wp(d, "cmask", seg, i)
                            elif m > 1:
                                wp(d, "nout", seg, i, m - 1)
                            else:
                                wp(d, "xi", seg, i, 1)
                            for h, hp, r in heads:
                                last = pe.matmul(psX[d][r:r + HD, hp], cm[d][r:r + HD, m, hp],
                                                 N[d][r:r + HD, hp] if m else k.cst("eye")[r:r + HD],
                                                 start=True, stop=True)
                            last.then_inc(sem[d]["x"].sem, 1)
                        if m == 0:
                            continue
                        for d in range(2):
                            wp(d, "xi", seg, i, m + 1)
                            for h, hp, r in heads:
                                if m < 5:
                                    pe.matmul(psN[d][r:r + HD, hp], NT[d][r:r + HD, hp], XI[d][r:r + HD, hp],
                                              start=True, stop=True)
                                last = pe.matmul(psNT[d][r:r + HD, hp], XI[d][r:r + HD, hp], NT[d][r:r + HD, hp],
                                                 start=True, stop=True)
                            last.then_inc(sem[d]["nn"].sem, 1)
                    for d in range(2):
                        wp(d, "tok", seg, i)
                        for h, hp, r in heads:
                            q = HD - r
                            pe.matmul(psR[d][r:r + HD, hp], ra[d][r:r + HD, hp, 1], S[d][r:r + HD, hp],
                                      start=True, stop=True)
                            last = pe.matmul(psAV[d][r:r + HD, hp], M[d][q:q + HD, h % 2, hp, L:P], uv[d][q:q + HD, h],
                                             start=True, stop=True)
                        last.then_inc(sem[d]["rhs"].sem, 1)
                    for d in range(2):
                        wp(d, "rhsout", seg, i)
                        wp(d, "nout", seg, i, 5)
                        for h, hp, r in heads:
                            last = pe.matmul(psU[d][r:r + HD, hp], NT[d][r:r + HD, hp], rhs[d][r:r + HD, hp],
                                             start=True, stop=True)
                        last.then_inc(sem[d]["u"].sem, 1)
                    for d in range(2):
                        wp(d, "uout", seg, i)
                        for h, hp, r in heads:
                            pe.matmul(psS[d][r:r + HD, hp], bk[d][:, h], uv[d][:, h], start=True, stop=True)
                        for h, hp, r in heads:
                            pe.matmul(psY[d][r:r + HD, hp], S[d][r:r + HD, hp], ra[d][r:r + HD, hp, 0],
                                      start=True, stop=False)
                            last = pe.matmul(psY[d][r:r + HD, hp], uv[d][:, h], M[d][:, h % 2, hp, 0:L],
                                             start=False, stop=True)
                        last.then_inc(sem[d]["sy"].sem, 1)
        for d in range(2):
            for n in names:
                sem[d][n].advance(per_step[n] * 2 * NCH)


def stage_rwkv_readout(nc, k, l, pr, aa, ka, g, y):
    (y_sum, mean_ps, cen, sq_done, var_ps, root_done, bon_in, bon_ps, out_done) = k.signals(
        "ro_ysum", "ro_mean", "ro_centred", "ro_sq", "ro_var", "ro_root", "ro_bonus_in", "ro_bonus", "ro_out")
    with ExitStack() as ctx:
        def sb(name):
            return ctx.enter_context(nc.sbuf_tensor(f"ro_{name}{l}", [P, 2, T], F32))

        sq, root, bon, t1 = sb("sq"), sb("root"), sb("bon"), sb("t1")
        psM = ctx.enter_context(nc.psum_tensor(f"ro_psM{l}", [P, 2, 512], F32))
        psV = ctx.enter_context(nc.psum_tensor(f"ro_psV{l}", [P, 2, 512], F32))
        psB = ctx.enter_context(nc.psum_tensor(f"ro_psB{l}", [P, 2, 512], F32))
        with nc.Block(no_gpsimd_drain=True) as block:

            @block.vector
            def _(dve):
                for c in range(KC):
                    dve.tensor_tensor(y[:, 0, c], y[:, 0, c], y[:, 1, c], ALU.add).then_inc(y_sum.sem, 1)
                for c in range(KC):
                    dve.tensor_tensor(t1[:, c % 2], aa[:, 0, c], aa[:, 1, c], ALU.add)
                    dve.drain()
                    dve.tensor_tensor(t1[:, c % 2], t1[:, c % 2], ka[:, c], ALU.mult)
                    dve.drain()
                    dve.scalar_tensor_tensor(out=t1[:, c % 2], in0=pr[:, K_T + c], scalar=2.0, in1=t1[:, c % 2],
                                             op0=ALU.mult, op1=ALU.add)
                    dve.drain()
                    if c >= 2:
                        dve.wait_ge(bon_ps.sem, bon_ps.at(c - 1))
                    dve.scalar_tensor_tensor(out=bon[:, c % 2], in0=t1[:, c % 2], scalar=k.par(l, "rk")[:, c:c + 1],
                                             in1=pr[:, R_T + c], op0=ALU.mult, op1=ALU.mult).then_inc(bon_in.sem, 1)
                    dve.wait_ge(mean_ps.sem, mean_ps.at(c + 1))
                    dve.scalar_tensor_tensor(out=y[:, 0, c], in0=psM[:, c % 2], scalar=-1.0 / HD, in1=y[:, 0, c],
                                             op0=ALU.mult, op1=ALU.add).then_inc(cen.sem, 1)
                    dve.wait_ge(bon_ps.sem, bon_ps.at(c + 1))
                    dve.tensor_tensor(t1[:, c % 2], psB[:, c % 2], pr[:, V_T + c], ALU.mult)
                    dve.wait_ge(root_done.sem, root_done.at(c + 1))
                    dve.reciprocal(root[:, c % 2], root[:, c % 2])
                    dve.drain()
                    dve.tensor_tensor(y[:, 0, c], y[:, 0, c], root[:, c % 2], ALU.mult)
                    dve.drain()
                    dve.tensor_scalar(y[:, 0, c], y[:, 0, c], k.par(l, "lg")[:, c:c + 1], k.par(l, "lb")[:, c:c + 1],
                                      ALU.mult, ALU.add)
                    dve.drain()
                    dve.tensor_tensor(y[:, 0, c], y[:, 0, c], t1[:, c % 2], ALU.add)
                    dve.drain()
                    dve.tensor_tensor(pr[:, R_T + c], y[:, 0, c], g[:, c], ALU.mult).then_inc(out_done.sem, 1)

            @block.scalar
            def _(act):
                for c in range(KC):
                    act.wait_ge(cen.sem, cen.at(c + 1))
                    if c >= 2:
                        act.wait_ge(var_ps.sem, var_ps.at(c - 1))
                    act.activation(sq[:, c % 2], y[:, 0, c], ACT.Square).then_inc(sq_done.sem, 1)
                    act.wait_ge(var_ps.sem, var_ps.at(c + 1))
                    if c >= 2:
                        act.wait_ge(out_done.sem, out_done.at(c - 1))
                    act.activation(root[:, c % 2], psV[:, c % 2], ACT.Sqrt, scale=1.0 / HD, bias=k.cst("eps")[:, 1:2]
                                   ).then_inc(root_done.sem, 1)

            @block.tensor
            def _(pe):
                for c in range(KC):
                    pe.wait_ge(y_sum.sem, y_sum.at(c + 1))
                    if c >= 2:
                        pe.wait_ge(cen.sem, cen.at(c - 1))
                    pe.matmul(psM[:, c % 2], k.cst("blk"), y[:, 0, c], start=True, stop=True).then_inc(mean_ps.sem, 1)
                    pe.wait_ge(bon_in.sem, bon_in.at(c + 1))
                    if c >= 2:
                        pe.wait_ge(out_done.sem, out_done.at(c - 1))
                    pe.matmul(psB[:, c % 2], k.cst("blk"), bon[:, c % 2], start=True, stop=True
                              ).then_inc(bon_ps.sem, 1)
                    pe.wait_ge(sq_done.sem, sq_done.at(c + 1))
                    if c >= 2:
                        pe.wait_ge(root_done.sem, root_done.at(c - 1))
                    pe.matmul(psV[:, c % 2], k.cst("blk"), sq[:, c % 2], start=True, stop=True).then_inc(var_ps.sem, 1)
        for x in (y_sum, mean_ps, cen, sq_done, var_ps, root_done, bon_in, bon_ps, out_done):
            x.advance(KC)


def stage_merge(nc, k, l, pr, pn, x, h, t0, x_source):
    N = T - t0
    (w_in, mg_in, wo_in, hx_in, g_done, g_out, y_done, y_used, merged, o_done, x_done) = k.signals(
        "mg_w_in0", "mg_w_in1", "mg_wo_in", "mg_hx_in", "mg_gate", "mg_gate_out", "mg_y", "mg_y_used", "mg_merged",
        "mg_o", "mg_x")
    ring_in = (w_in, mg_in)
    NW = 3 * KD + 3 * KC
    with ExitStack() as ctx:
        ring = ctx.enter_context(nc.sbuf_tensor(f"mg_ring{l}", [P, 2, NW, P], F32))
        wo = ctx.enter_context(nc.sbuf_tensor(f"mg_wo{l}", [P, KD, D], F32))
        gate = ctx.enter_context(nc.sbuf_tensor(f"mg_gateb{l}", [P, 3, T], F32))
        mg = ctx.enter_context(nc.sbuf_tensor(f"mg_m{l}", [P, KD, T], F32))
        psG = ctx.enter_context(nc.psum_tensor(f"mg_psG{l}", [P, 3, 512], F32))
        psY = ctx.enter_context(nc.psum_tensor(f"mg_psY{l}", [P, 3, 512], F32))
        psO = ctx.enter_context(nc.psum_tensor(f"mg_psO{l}", [P, 2, 512], F32))
        branch = (lambda c: pr[:, R_T + c, t0:T], lambda c: pn[:, NQ_T + c, t0:T], lambda c: pn[:, MO_T + c, t0:T])
        with nc.Block(no_gpsimd_drain=True) as block:

            @block.sync
            def _(sp):
                def load(j, i):
                    sp.dma_start(ring[:, j], k.d_mg[l, bass.ds(i * 2 + j, 1)].rearrange(
                        "a p (k n) -> p (a k) n", n=P)).then_inc(ring_in[j].sem, 16)

                sp.dma_start(h[:, :, t0:T], k.d_h[:, :, t0:T]).then_inc(hx_in.sem, 16)
                load(0, 0)
                load(1, 0)
                sp.dma_start(wo[:], k.d_wo[l]).then_inc(wo_in.sem, 16)
                sp.dma_start(x[:, :, t0:T], x_source[:, :, t0:T]).then_inc(wo_in.sem, 16)
                with sp.Fori(1, KD // 2) as i:
                    for j in range(2):
                        sp.wait_ge(y_done.sem, y_done.at(3 * (j - 1)) + i * 6)
                        load(j, i)

            @block.gpsimd
            def _(pool):
                pool.memset(k.scratch[:, 0:1], 0.0).then_inc(y_used.sem, 1)

            @block.tensor
            def _(pe):
                pe.wait_ge(hx_in.sem, hx_in.at(16))
                with pe.Fori(0, KD // 2) as i:
                    for j in range(2):
                        pe.wait_ge(ring_in[j].sem, ring_in[j].at(16) + i * 16)
                        pe.wait_ge(y_used.sem, y_used.at(1 + j) + i * 2)
                        for b in range(3):
                            for c in range(KD):
                                last = pe.matmul(psG[:, b, 0:N], ring[:, j, b * KD + c], h[:, c, t0:T],
                                                 start=c == 0, stop=c == KD - 1)
                            last.then_inc(g_done.sem, 1)
                        for b in range(3):
                            for c in range(KC):
                                last = pe.matmul(psY[:, b, 0:N], ring[:, j, 3 * KD + b * KC + c], branch[b](c),
                                                 start=c == 0, stop=c == KC - 1)
                            last.then_inc(y_done.sem, 1)
                pe.wait_ge(wo_in.sem, wo_in.at(32))
                pe.wait_ge(merged.sem, merged.at(KD))
                for m in range(KD):
                    if m >= 2:
                        pe.wait_ge(x_done.sem, x_done.at(m - 1))
                    for c in range(KD):
                        last = pe.matmul(psO[:, m % 2, 0:N], wo[:, c, m * P:(m + 1) * P], mg[:, c, t0:T],
                                         start=c == 0, stop=c == KD - 1)
                    last.then_inc(o_done.sem, 1)

            @block.scalar
            def _(act):
                with act.Fori(0, KD // 2) as i:
                    for j in range(2):
                        act.wait_ge(y_used.sem, y_used.at(1 + j) + i * 2)
                        for b in range(3):
                            act.wait_ge(g_done.sem, g_done.at(3 * j + b + 1) + i * 6)
                            act.activation(gate[:, b, 0:N], psG[:, b, 0:N], ACT.Sigmoid).then_inc(g_out.sem, 1)

            @block.vector
            def _(dve):
                with dve.Fori(0, KD // 2) as i:
                    for j in range(2):
                        for b in range(3):
                            dve.wait_ge(g_out.sem, g_out.at(3 * j + b + 1) + i * 6)
                            dve.wait_ge(y_done.sem, y_done.at(3 * j + b + 1) + i * 6)
                            dve.tensor_tensor(gate[:, b, 0:N], gate[:, b, 0:N], psY[:, b, 0:N], ALU.mult)
                        dve.drain()
                        dve.tensor_tensor(gate[:, 0, 0:N], gate[:, 0, 0:N], gate[:, 1, 0:N], ALU.add)
                        dve.drain()
                        dve.tensor_tensor(mg[:, bass.ds(i * 2 + j, 1), t0:T].rearrange("p a t -> p (a t)"),
                                          gate[:, 0, 0:N], gate[:, 2, 0:N], ALU.add).then_inc(merged.sem, 1)
                        dve.wait_ge(merged.sem, merged.at(j + 1) + i * 2)
                        dve.memset(k.scratch[:, 1:2], 0.0).then_inc(y_used.sem, 1)
                for m in range(KD):
                    dve.wait_ge(o_done.sem, o_done.at(m + 1))
                    for s in range(2):
                        if s * CTX >= t0:
                            last = dve.scalar_tensor_tensor(
                                out=x[:, m, s * CTX:(s + 1) * CTX], in0=psO[:, m % 2, s * CTX - t0:(s + 1) * CTX - t0],
                                scalar=k.mod[:, l, s, 2 * KD + m:2 * KD + m + 1], in1=x[:, m, s * CTX:(s + 1) * CTX],
                                op0=ALU.mult, op1=ALU.add)
                    last.then_inc(x_done.sem, 1)
        for s, n in zip((w_in, mg_in, wo_in, hx_in, g_done, g_out, y_done, y_used, merged, o_done, x_done),
                        (64, 64, 32, 16, 24, 24, 24, 9, 8, 8, 8)):
            s.advance(n)


def stage_router(nc, k, l, h, gT, t0):
    N = T - t0
    NTT = N // P
    (w_in, s_ps, s_out, picked, turned, out) = k.signals("ro_w_in", "rt_ps", "rt_scores", "rt_gates", "rt_turned",
                                                         "rt_out")
    NE, GS = E_ROUTED, E_ROUTED // GROUPS
    with ExitStack() as ctx:
        def sb(name, shape):
            return ctx.enter_context(nc.sbuf_tensor(f"rt_{name}{l}", shape, F32))

        wr = sb("wr", [P, KD + 1, NE])
        sc = sb("sc", [P, NTT, NE])
        sel = sb("sel", [P, NTT, NE])
        top = sb("top", [P, NTT, GROUPS, 8])
        gs = sb("gs", [P, NTT, GROUPS])
        best = sb("best", [P, NTT, 8])
        rep = sb("rep", [P, NTT, GROUPS])
        msk = sb("msk", [P, NTT, GROUPS])
        neg = sb("neg", [P, NTT, GROUPS])
        cut = sb("cut", [P, NTT, NE])
        gates = sb("gates", [P, NTT, NE])
        tot = sb("tot", [P, NTT])
        ps = ctx.enter_context(nc.psum_tensor(f"rt_psb{l}", [P, 4, NE], F32))
        psT = ctx.enter_context(nc.psum_tensor(f"rt_psT{l}", [P, 512], F32))
        with nc.Block(no_gpsimd_drain=True) as block:

            @block.sync
            def _(sp):
                sp.dma_start(wr[:], k.d_rt[l].rearrange("p (c n) -> p c n", n=NE)).then_inc(w_in.sem, 16)

            @block.tensor
            def _(pe):
                pe.wait_ge(w_in.sem, w_in.at(16))
                for tt in range(NTT):
                    for c in range(KD):
                        last = pe.matmul(ps[:, tt], h[:, c, t0 + tt * P:t0 + (tt + 1) * P], wr[:, c],
                                         start=c == 0, stop=c == KD - 1)
                last.then_inc(s_ps.sem, 1)
                pe.wait_ge(picked.sem, picked.at(1))
                for tt in range(NTT):
                    last = pe.transpose(psT[0:NE, tt * P:(tt + 1) * P], gates[:, tt], k.cst("ident"))
                last.then_inc(turned.sem, 1)

            @block.scalar
            def _(act):
                act.wait_ge(s_ps.sem, s_ps.at(1))
                act.activation(sc[:], ps[:, 0:NTT], ACT.Sigmoid).then_inc(s_out.sem, 1)
                act.wait_ge(turned.sem, turned.at(1))
                act.activation(gT[0:NE, 0:N], psT[0:NE, 0:N], ACT.Copy).then_inc(out.sem, 1)

            @block.vector
            def _(dve):
                dve.memset(gT[NE:NE + 2, 0:N], 1.0)
                dve.wait_ge(s_out.sem, s_out.at(1))
                dve.tensor_tensor(sel[:], sc[:], wr[:, KD:KD + 1].broadcast_to([P, NTT, NE]), ALU.add)
                dve.drain()
                for tt in range(NTT):
                    for q in range(GROUPS):
                        dve.max(top[:, tt, q], sel[:, tt, q * GS:(q + 1) * GS])
                dve.drain()
                dve.tensor_tensor(gs[:], top[:, :, :, 0], top[:, :, :, 1], ALU.add)
                dve.drain()
                for tt in range(NTT):
                    dve.max(best[:, tt], gs[:, tt])
                dve.drain()
                dve.memset(best[:, :, TOPK_GROUPS:8], -NEG)
                dve.drain()
                for tt in range(NTT):
                    dve.match_replace(rep[:, tt], best[:, tt], gs[:, tt], NEG)
                dve.drain()
                dve.tensor_scalar(msk[:], rep[:], NEG, None, ALU.is_equal)
                dve.drain()
                dve.tensor_scalar(neg[:], msk[:], -1.0, -NEG, ALU.add, ALU.mult)
                dve.drain()
                for tt in range(NTT):
                    g3 = cut[:, tt].rearrange("p (q e) -> p q e", q=GROUPS)
                    dve.tensor_tensor(g3, sel[:, tt].rearrange("p (q e) -> p q e", q=GROUPS),
                                      msk[:, tt].unsqueeze(2).broadcast_to([P, GROUPS, GS]), ALU.mult)
                dve.drain()
                for tt in range(NTT):
                    g3 = cut[:, tt].rearrange("p (q e) -> p q e", q=GROUPS)
                    dve.tensor_tensor(g3, g3, neg[:, tt].unsqueeze(2).broadcast_to([P, GROUPS, GS]), ALU.add)
                dve.drain()
                for tt in range(NTT):
                    dve.max(best[:, tt], cut[:, tt])
                dve.drain()
                for tt in range(NTT):
                    dve.match_replace(gates[:, tt], best[:, tt], cut[:, tt], 2 * NEG)
                dve.drain()
                dve.tensor_scalar(gates[:], gates[:], 2 * NEG, None, ALU.is_equal)
                dve.drain()
                dve.tensor_tensor(gates[:], gates[:], sc[:], ALU.mult)
                dve.drain()
                dve.tensor_reduce(tot[:], gates[:], AX.X, ALU.add)
                dve.drain()
                dve.reciprocal(tot[:], tot[:])
                dve.drain()
                dve.tensor_tensor(gates[:], gates[:], tot[:].unsqueeze(2).broadcast_to([P, NTT, NE]), ALU.mult)
                dve.drain()
                dve.tensor_scalar(gates[:], gates[:], ROUTED_SCALE, None, ALU.mult).then_inc(picked.sem, 1)
        for s, n in zip((w_in, s_ps, s_out, picked, turned, out), (16, 1, 1, 1, 1, 1)):
            s.advance(n)


def stage_moe(nc, k, l, x, h, gT, t0):
    N = T - t0
    (w_in00, w_in01, w_in10, w_in11, gate_row, gb_done, gb_out, gu_done, sig_done, act_done, d_done, acc_done, x_out) = k.signals(
        "moe_w_in00", "moe_w_in01", "moe_w_in10", "moe_w_in11", "moe_gate_row", "moe_gate_bcast", "moe_gate_out",
        "moe_gu", "moe_sig", "moe_act", "moe_down",
        "moe_acc", "moe_x_out")
    w_in = (w_in00, w_in01, w_in10, w_in11)
    NP = E_ALL // 2
    last_layer = l == DEPTH - 1
    with ExitStack() as ctx:
        ring = ctx.enter_context(nc.sbuf_tensor(f"moe_ring{l}", [P, 4, 3 * KD, P], F32))
        acc = ctx.enter_context(nc.sbuf_tensor(f"moe_accb{l}", [P, KD, T], F32))
        row = ctx.enter_context(nc.sbuf_tensor(f"moe_row{l}", [E_ALL, 2, T], F32))
        gb = ctx.enter_context(nc.sbuf_tensor(f"moe_gb{l}", [P, 2, T], F32))
        sg = ctx.enter_context(nc.sbuf_tensor(f"moe_sg{l}", [P, 2, T], F32))
        a = ctx.enter_context(nc.sbuf_tensor(f"moe_a{l}", [P, 2, T], F32))
        psG = ctx.enter_context(nc.psum_tensor(f"moe_psG{l}", [P, 2, 512], F32))
        psU = ctx.enter_context(nc.psum_tensor(f"moe_psU{l}", [P, 2, 512], F32))
        psB = ctx.enter_context(nc.psum_tensor(f"moe_psB{l}", [P, 512], F32))
        psD = ctx.enter_context(nc.psum_tensor(f"moe_psD{l}", [P, 3, 512], F32))
        with nc.Block(no_gpsimd_drain=True) as block:

            @block.sync
            def _(sp):
                def load(slot, i, j):
                    sp.dma_start(ring[:, slot], k.d_moe[l, bass.ds(i * 2 + j, 1)].rearrange(
                        "a p (c n) -> p (a c) n", n=P)).then_inc(w_in[slot].sem, 16)

                for q in range(2):
                    for j in range(2):
                        load(q * 2 + j, q, j)
                with sp.Fori(1, (NP - 1) // 2) as i:
                    for q in range(2):
                        sp.wait_ge(d_done.sem, d_done.at((q - 1) * KD) + i * 2 * KD)
                        for j in range(2):
                            load(q * 2 + j, i * 2 + q, j)
                sp.wait_ge(d_done.sem, d_done.at((NP - 2) * KD))
                for j in range(2):
                    load(j, NP - 1, j)
                if last_layer:
                    for c in range(KD):
                        sp.wait_ge(acc_done.sem, acc_done.at(NP * KD + 3 + c + 1))
                        sp.dma_start(k.d_out[:, c], x[:, c, CTX:T]).then_inc(x_out.sem, 16)
                    sp.wait_ge(x_out.sem, x_out.at(16 * KD))

            @block.gpsimd
            def _(pool):
                pool.memset(acc[:], 0.0).then_inc(acc_done.sem, 3)
                pool.memset(k.scratch[:, 0:1], 0.0).then_inc(gb_out.sem, 1)

            def pairs(eng, body):
                with eng.Fori(0, (NP - 1) // 2) as i:
                    for q in range(2):
                        body(i * 2 + q, q, i)
                body(NP - 1, 0, (NP - 1) // 2)

            @block.tensor
            def _(pe):
                def pair(n, q, i):
                    for j in range(2):
                        pe.wait_ge(w_in[2 * q + j].sem, w_in[2 * q + j].at(16) + i * 16)
                        pe.wait_ge(gate_row.sem, gate_row.at(j + 1) + n * 2)
                        pe.wait_ge(gb_out.sem, gb_out.at(j + 1) + n * 2)
                        pe.matmul(psB[:, 0:N], k.cst("ones", E_ALL), row[:, j, 0:N], start=True, stop=True
                                  ).then_inc(gb_done.sem, 1)
                        for ps, at in ((psG, 0), (psU, KD)):
                            for c in range(KD):
                                last = pe.matmul(ps[:, j, 0:N], ring[:, 2 * q + j, at + c], h[:, c, t0:T],
                                                 start=c == 0, stop=c == KD - 1)
                        last.then_inc(gu_done.sem, 1)
                    pe.wait_ge(act_done.sem, act_done.at(2) + n * 2)
                    for c in range(KD):
                        pe.wait_ge(acc_done.sem, acc_done.at(c + 1) + n * KD)
                        for j in range(2):
                            last = pe.matmul(psD[:, c % 3, 0:N], ring[:, 2 * q + j, 2 * KD + c], a[:, j, 0:N],
                                             start=j == 0, stop=j == 1)
                        last.then_inc(d_done.sem, 1)

                pairs(pe, pair)

            @block.scalar
            def _(act):
                def pair(n, q, i):
                    for j in range(2):
                        act.wait_ge(gb_done.sem, gb_done.at(j + 1) + n * 2)
                        act.activation(gb[:, j, 0:N], psB[:, 0:N], ACT.Copy).then_inc(gb_out.sem, 1)
                        act.wait_ge(gu_done.sem, gu_done.at(j + 1) + n * 2)
                        act.activation(sg[:, j, 0:N], psG[:, j, 0:N], ACT.Sigmoid).then_inc(sig_done.sem, 1)

                pairs(act, pair)

            @block.vector
            def _(dve):
                def gate_rows(n):
                    for j in range(2):
                        dve.tensor_scalar(row[:, j, 0:N], gT[:, 0:N], k.cst("ident", E_ALL)[:, bass.ds(n * 2 + j, 1)],
                                          None, ALU.mult).then_inc(gate_row.sem, 1)

                def pair(n, q, i):
                    gate_rows(n)
                    for j in range(2):
                        dve.wait_ge(sig_done.sem, sig_done.at(j + 1) + n * 2)
                        dve.tensor_tensor(sg[:, j, 0:N], sg[:, j, 0:N], psG[:, j, 0:N], ALU.mult)
                        dve.drain()
                        dve.tensor_tensor(sg[:, j, 0:N], sg[:, j, 0:N], psU[:, j, 0:N], ALU.mult)
                        dve.drain()
                        dve.tensor_tensor(a[:, j, 0:N], sg[:, j, 0:N], gb[:, j, 0:N], ALU.mult
                                          ).then_inc(act_done.sem, 1)
                    for c in range(KD):
                        dve.wait_ge(d_done.sem, d_done.at(c + 1) + n * KD)
                        dve.tensor_tensor(acc[:, c, 0:N], acc[:, c, 0:N], psD[:, c % 3, 0:N], ALU.add
                                          ).then_inc(acc_done.sem, 1)
                    dve.drain()

                dve.wait_ge(acc_done.sem, acc_done.at(3))
                pairs(dve, pair)
                for c in range(KD):
                    for s in range(2):
                        if s * CTX >= t0:
                            last = dve.scalar_tensor_tensor(
                                out=x[:, c, s * CTX:(s + 1) * CTX], in0=acc[:, c, s * CTX - t0:(s + 1) * CTX - t0],
                                scalar=k.mod[:, l, s, 5 * KD + c:5 * KD + c + 1], in1=x[:, c, s * CTX:(s + 1) * CTX],
                                op0=ALU.mult, op1=ALU.add)
                    last.then_inc(acc_done.sem, 1)
        for s, n in zip((w_in00, w_in01, w_in10, w_in11, gate_row, gb_done, gb_out, gu_done, sig_done, act_done, d_done, acc_done),
                        (16 * (NP // 2 + 1),) * 2 + (16 * (NP // 2),) * 2 + (2 * NP, 2 * NP, 2 * NP + 1, 2 * NP, 2 * NP, 2 * NP, NP * KD, NP * KD + 3 + KD)):
            s.advance(n)


def hybrid_backbone_kernel(nc, d):
    with ExitStack() as top:
        k = Kit(nc, top)
        k.d_cst, k.d_par, k.d_mlc, k.d_xin, k.d_c, k.d_ada = (d[n] for n in ("cst", "par", "mlc", "xin", "c", "ada"))
        k.d_win, k.d_mg, k.d_wo, k.d_lora, k.d_nab = (d[n] for n in ("win", "mg", "wo", "lora", "nab"))
        k.d_rt, k.d_moe, k.d_out = d["rt"], d["moe"], d["out"]
        k.d_x = nc.dram_tensor("x_keep", (P, KD, T), F32).ap()
        k.d_h = nc.dram_tensor("h_keep", (P, KD, T), F32).ap()
        k.d_vf = nc.dram_tensor("v_first", (P, KC, T), F32).ap()
        k.cst_sb = top.enter_context(nc.sbuf_tensor("cst", [P, NCST], F32))
        k.par_sb = top.enter_context(nc.sbuf_tensor("par", [P, DEPTH * NPAR], F32))
        k.mod = top.enter_context(nc.sbuf_tensor("mod", [P, DEPTH, 2, 6 * KD], F32))
        k.scratch = top.enter_context(nc.sbuf_tensor("scratch", [P, 4], F32))
        stage_modulation(nc, k)
        for l in range(DEPTH):
            t0 = 0 if l < DEPTH - 1 else CTX
            with ExitStack() as lay:
                pr = lay.enter_context(nc.sbuf_tensor(f"pr{l}", [P, 16, T], F32))
                pn = lay.enter_context(nc.sbuf_tensor(f"pn{l}", [P, 16, T], F32))
                with ExitStack() as mix:
                    vna = mix.enter_context(nc.sbuf_tensor(f"vna{l}", [P, 4, C], F32))
                    vml = mix.enter_context(nc.sbuf_tensor(f"vml{l}", [P, 4, C], F32))
                    with nc.sbuf_tensor(f"h1_{l}", [P, KD, T], F32) as h:
                        with nc.sbuf_tensor(f"x1_{l}", [P, KD, T], F32) as x:
                            stage_norm(nc, k, l, 1, x, h, 0, k.d_xin if l == 0 else k.d_x)
                        stage_projection(nc, k, l, h, pr, pn, vna, vml)
                    stage_attention(nc, k, l, pn, vna)
                    stage_mlstm(nc, k, l, pr, pn, vml)
                with ExitStack() as rw:
                    def big(name, shape):
                        return rw.enter_context(nc.sbuf_tensor(f"{name}{l}", shape, F32))

                    sg = big("decay", [P, 2, KC, T])
                    aa = big("aa", [P, 2, KC, T])
                    kk = big("kkn", [P, KC, T])
                    ka = big("kka", [P, KC, T])
                    g = big("gg", [P, KC, T])
                    stage_rwkv_features(nc, k, l, pr, sg, aa, kk, ka, g)
                    stage_rwkv_scan(nc, k, l, pr, sg, aa, kk, ka, sg)
                    stage_rwkv_readout(nc, k, l, pr, aa, ka, g, sg)
                with nc.sbuf_tensor(f"x2_{l}", [P, KD, T], F32) as x, nc.sbuf_tensor(f"h2_{l}", [P, KD, T], F32) as h:
                    stage_merge(nc, k, l, pr, pn, x, h, t0, k.d_xin if l == 0 else k.d_x)
                    save_x(nc, k, x, t0)
            with nc.sbuf_tensor(f"x3_{l}", [P, KD, T], F32) as x, nc.sbuf_tensor(f"h3_{l}", [P, KD, T], F32) as h, \
                    nc.sbuf_tensor(f"gT_{l}", [E_ALL, T], F32) as gT:
                stage_norm(nc, k, l, 2, x, h, t0, k.d_x)
                stage_router(nc, k, l, h, gT, t0)
                stage_moe(nc, k, l, x, h, gT, t0)
                if l < DEPTH - 1:
                    save_x(nc, k, x, t0)


def save_x(nc, k, x, t0):
    (saved,) = k.signals("x_saved")
    with nc.Block(no_gpsimd_drain=True) as block:

        @block.sync
        def _(sp):
            sp.dma_start(k.d_x[:, :, t0:T], x[:, :, t0:T]).then_inc(saved.sem, 16)
            sp.wait_ge(saved.sem, saved.at(16))
    saved.advance(16)


def layout(i):
    f = np.float32
    a = {n: np.asarray(v) for n, v in i.items()}

    def tiles(v):
        return np.moveaxis(v.reshape(*v.shape[:-1], -1, P), -1, -2)

    def wt(w, cols=None):
        return w.reshape(-1, P, w.shape[-1]).transpose(1, 0, 2)

    out = {}
    xin = np.concatenate([a["ctx"][0], a["x"][0]], 0)
    out["xin"] = xin.T.reshape(KD, P, T).transpose(1, 0, 2)
    out["c"] = np.stack([a["c_ctx"], a["c"][0]], -1).reshape(KD, P, 2).transpose(1, 0, 2)
    out["ada"] = a["w_ada"].reshape(DEPTH, KD, P, 12, 512).transpose(0, 3, 2, 1, 4).reshape(DEPTH, 12, P, KD * 512)
    o = np.cumsum([0, C, C, C, 384, C, C, C, 256, 256, C, C, 16])
    w = a["w_in"]
    r, kk, v, lora, nq, nk_, nv, mq, mk, mv, mo, gates = [w[:, :, o[j]:o[j + 1]] for j in range(12)]
    gt = np.zeros((DEPTH, D, P), f)
    gt[:, :, 0:8], gt[:, :, 32:40] = gates[:, :, 0:8], gates[:, :, 8:16]
    blocks = [r, kk, v, np.concatenate([lora, gt], -1), nq, nk_, np.concatenate([mq, mk], -1), mo, nv, mv]
    out["win"] = np.stack(blocks, 1).reshape(DEPTH, 10, KD, P, 512).transpose(0, 1, 3, 2, 4).reshape(
        DEPTH, 10, P, KD * 512)
    g3 = w[:, :, o[12]:].reshape(DEPTH, KD, P, 3, KD, P).transpose(0, 4, 2, 3, 1, 5).reshape(DEPTH, KD, P, -1)
    b3 = a["w_branch"].reshape(DEPTH, 3, KC, P, KD, P).transpose(0, 4, 3, 1, 2, 5).reshape(DEPTH, KD, P, -1)
    out["mg"] = np.concatenate([g3, b3], -1)
    out["wo"] = a["w_out"].reshape(DEPTH, KD, P, D).transpose(0, 2, 1, 3)
    zero = np.zeros((1, C), f)
    par = []
    for l in range(DEPTH):
        ib, fb = np.zeros((P, 1), f), np.zeros((P, 1), f)
        ib[0:8, 0], fb[32:40, 0] = a["ml_i_bias"][l].reshape(8), a["ml_f_bias"][l].reshape(8)
        par += [tiles(a["norm1_g"][l]), tiles(a["norm2_g"][l]), tiles(a["b_ada"][l]), tiles(a["rw_mu"][l]),
                tiles(a["rw_w0"][l].reshape(-1)), tiles(a["rw_a0"][l].reshape(-1)), tiles(a["rw_k_k"][l]),
                tiles(a["rw_k_a"][l]), tiles(a["rw_r_k"][l].reshape(-1)), tiles(a["rw_lnx_g"][l]),
                tiles(a["rw_lnx_b"][l]), tiles(a["rw_v0"][l - 1] if l else zero[0]), tiles(a["ml_norm_g"][l]),
                np.tile(a["na_qn_g"][l], 2)[:, None], np.tile(a["na_kn_g"][l], 2)[:, None], ib, fb]
    out["par"] = np.concatenate(par, 1)
    lora = np.zeros((DEPTH, P, 3 * C + KC * 32 + C), f)
    for l in range(DEPTH):
        lora[l, :, 0:C] = a["rw_w2"][l].reshape(P, C)
        lora[l, :, C:2 * C] = a["rw_a2"][l].reshape(P, C)
        lora[l, :, 2 * C:3 * C] = a["rw_g2"][l]
        if l:
            lora[l, :, 3 * C:3 * C + KC * 32] = wt(a["rw_v1"][l - 1]).reshape(P, -1)
            lora[l, 0:32, 3 * C + KC * 32:] = a["rw_v2"][l - 1]
    out["lora"] = lora
    t = np.arange(SEQ)
    row, col = t // GRID_W, t % GRID_W
    cs = np.clip(col - NA_WIN_C // 2, 0, GRID_W - NA_WIN_C)
    inside = (col[None, :] >= cs[:, None]) & (col[None, :] < cs[:, None] + NA_WIN_C)
    ri = row[None, :] - row[:, None] + NA_WIN_R - 1
    ci = np.clip(col[None, :] - col[:, None] + NA_WIN_C - 1, 0, 2 * NA_WIN_C - 2)
    nab = np.full((DEPTH, HEADS, SEQ, SEQ), NEG, f)
    nab[:, :, inside] = a["na_rpb"][:, :, ri[inside], ci[inside]]
    out["nab"] = nab.reshape(DEPTH, HEADS, 2, P, SEQ).transpose(0, 3, 1, 2, 4).reshape(DEPTH, P, -1)
    rt = np.concatenate([a["moe_router"].reshape(DEPTH, KD, P, E_ROUTED).transpose(0, 2, 1, 3).reshape(DEPTH, P, -1),
                         np.broadcast_to(a["moe_bias"][:, None, :], (DEPTH, P, E_ROUTED))], -1)
    out["rt"] = rt
    moe = np.zeros((DEPTH, E_ALL, P, 3 * KD * P), f)
    for j, (rn, sn) in enumerate((("moe_w_gate", "sh_w_gate"), ("moe_w_up", "sh_w_up"))):
        sh = a[sn].reshape(DEPTH, D, 2, P).transpose(0, 2, 1, 3)
        full = np.concatenate([a[rn], sh], 1)
        moe[..., j * D:(j + 1) * D] = full.reshape(DEPTH, E_ALL, KD, P, P).transpose(0, 1, 3, 2, 4).reshape(
            DEPTH, E_ALL, P, D)
    moe[..., 2 * D:] = np.concatenate([a["moe_w_down"], a["sh_w_down"].reshape(DEPTH, 2, P, D)], 1)
    out["moe"] = moe
    out["cst"], out["mlc"] = constants()
    return {n: np.ascontiguousarray(v) for n, v in out.items()}


def kernel(**inputs):
    import concourse.bacc as bacc
    from concourse.bass_utils import run_bass_kernel_spmd

    nc = bacc.Bacc("TRN2", target_bir_lowering=False, num_devices=1)
    arrays = layout(inputs)
    d = {n: nc.dram_tensor("in_" + n, v.shape, mybir.dt.from_np(v.dtype), kind="ExternalInput").ap()
         for n, v in arrays.items()}
    d["out"] = nc.dram_tensor("out_dram", (P, KD, SEQ), F32, kind="ExternalOutput").ap()
    hybrid_backbone_kernel(nc, d)
    r = run_bass_kernel_spmd(nc, [{"in_" + n: v for n, v in arrays.items()}], core_ids=[0])
    got = r.results[0]["out_dram"]
    return got.transpose(2, 1, 0).reshape(1, SEQ, D)
```

```python
from contextlib import ExitStack

import numpy as np

import concourse.bass as bass
from concourse import mybir

F32 = mybir.dt.float32
U32 = mybir.dt.uint32
ALU = mybir.AluOpType
ACT = mybir.ActivationFunctionType
AX = mybir.AxisListType

P = 128
D = 1024
KD = D // P
SEQ = 256
CTX = 256
T = CTX + SEQ
DEPTH = 2
C = 512
KC = C // P
GRID_W = 64
HD = 64
HEADS = C // HD
L = 64
N_LORA_TILES = 3
ML_HEADS = 4
NA_WIN_R, NA_WIN_C = 8, 16
ROWS = SEQ // GRID_W
E_ROUTED = 64
E_ALL = E_ROUTED + 2
TOP_K = 8
GROUPS = 8
TOPK_GROUPS = 4
ROUTED_SCALE = 2.5
SLOTS = 128
NO_TOKEN = 1 << 20
RMS_EPS = 1e-6
LNX_EPS = 64e-5
GATE_CAP = 15.0
NEG = -1e30
DECAY = float(np.exp(-0.5))
LEVELS = (1, 2, 4, 8, 16, 32)

R_T, K_T, V_T, WD_T, AD_T, GD_T, GATE_T = 0, 4, 8, 12, 13, 14, 15
NQ_T, NK_T, MQ_T, MK_T, MO_T = 0, 4, 8, 10, 12

PAR = {}


def _par_layout():
    at = 0
    for name, n in (("n1", KD), ("n2", KD), ("bada", 6 * KD), ("mu", 15), ("w0", 2 * KC), ("a0", 2 * KC), ("kk", KC),
                    ("ka", KC), ("rk", KC), ("lg", KC), ("lb", KC), ("v0", KC), ("mg", KC), ("qn", 1), ("kn", 1),
                    ("ib", 1), ("fb", 1)):
        PAR[name] = (at, n)
        at += n
    return at


NPAR = _par_layout()

CST = {}


def _cst_layout():
    at = 0
    for name, n in (("ident", P), ("ones", P), ("blk", P), ("perm", P), ("cos", SEQ), ("sin", SEQ),
                    ("mra0", P), ("mra1", P), ("lev0", 6 * L), ("lev1", 6 * L), ("eye", L), ("reset", KC * L),
                    ("segres", T), ("eps", 4), ("sgn", 2), ("ecol", 1)):
        CST[name] = (at, n)
        at += n
    return at


NCST = _cst_layout()
NMLC = 4 * SEQ + 8 * P


def constants():
    c = np.zeros((P, NCST), np.float32)

    def put(name, a):
        at, n = CST[name]
        c[:a.shape[0], at:at + n] = a.reshape(a.shape[0], n)

    put("ident", np.eye(P))
    put("ones", np.ones((P, P)))
    half = np.arange(P) // HD
    put("blk", (half[:, None] == half[None, :]).astype(np.float32))
    perm = np.zeros((P, P))
    cos, sin = np.zeros((P, SEQ)), np.zeros((P, SEQ))
    t = np.arange(SEQ)
    pos = np.stack([t // GRID_W, t % GRID_W]).astype(np.float32)
    inv = (np.float32(10000.0) ** (-np.arange(16, dtype=np.float32) / np.float32(16))).astype(np.float32)
    for p in range(P):
        axis, second, i = (p % HD) // 32, (p % 32) // 16, p % 16
        ang = (pos[axis] * inv[i]).astype(np.float32)
        cos[p], sin[p] = np.cos(ang), np.sin(ang)
        perm[p - 16 if second else p + 16, p] = 1.0 if second else -1.0
    put("perm", perm)
    put("cos", cos)
    put("sin", sin)
    s = np.arange(P) % L
    q = np.arange(L)
    put("mra0", np.concatenate([s[:, None] <= q, s[:, None] < q], 1).astype(np.float32))
    put("mra1", np.concatenate([s[:, None] >= q, s[:, None] > q], 1).astype(np.float32))
    for d in range(2):
        lev = []
        for m in LEVELS:
            same = (s[:, None] // (2 * m)) == (q[None, :] // (2 * m))
            first_s, first_q = (s[:, None] // m) % 2 == 0, (q[None, :] // m) % 2 == 0
            lev.append(same & (first_s & ~first_q if d == 0 else ~first_s & first_q))
        put(f"lev{d}", np.stack(lev, 1).astype(np.float32))
    put("eye", (s[:, None] == q[None, :]).astype(np.float32))
    put("reset", np.broadcast_to((np.arange(KC * L) % L != 0).astype(np.float32), (P, KC * L)))
    put("segres", np.broadcast_to((np.arange(T) % SEQ != 0).astype(np.float32), (P, T)))
    put("eps", np.broadcast_to(np.array([RMS_EPS, LNX_EPS, 0, 0], np.float32), (P, 4)))
    row = np.arange(P)[:, None]
    put("ecol", (row - (E_ROUTED - 1)).astype(np.float32))
    put("sgn", np.concatenate([np.where(row < 4, 1.0, -1.0), np.where(row < 4, 0.0, 1.0)], 1))
    m = np.zeros((P, NMLC), np.float32)
    for d in range(2):
        for i in range(2):
            key = i * P + np.arange(P)[:, None]
            ok = key <= np.arange(SEQ)[None, :] if d == 0 else key >= np.arange(SEQ)[None, :]
            m[:, (d * 2 + i) * SEQ:(d * 2 + i + 1) * SEQ] = np.where(ok, 0.0, NEG)
    for r in range(8):
        m[r, 4 * SEQ + r * P:4 * SEQ + (r + 1) * P] = 1.0
    return c, m


class Signal:

    def __init__(self, sem, base=0):
        self.sem = sem
        self.base = base

    def at(self, n):
        return self.base + n

    def advance(self, n):
        self.base += n


class Kit:

    def __init__(self, nc):
        self.nc, self.free, self.used, self.count = nc, [], [], 0

    def signals(self, *names, fresh=False):
        out = []
        for n in names:
            self.count += 1
            if fresh or not self.free:
                s = Signal(self.nc.alloc_semaphore(f"{n}_{self.count}"))
            else:
                s = self.free.pop(0)
            if not fresh:
                self.used.append(s)
            out.append(s)
        return out

    def end_stage(self):
        self.free += self.used
        self.used = []

    def cst(self, name, rows=P):
        at, n = CST[name]
        return self.cst_sb[0:rows, at:at + n]

    def par(self, l, name, rows=P):
        at, n = PAR[name]
        return self.par_sb[0:rows, l * NPAR + at:l * NPAR + at + n]


def stage_modulation(nc, k):
    NB = 6 * D // 512
    names = ["ada_cst_in", "ada_silu", "ada_block", "ada_row", "ada_turned", "ada_mod"] + [f"ada_in{j}" for j in range(4)]
    cst_in, silu, block_done, row_out, turned, mod_done, *ada_in = k.signals(*names)
    with ExitStack() as ctx:
        ring = ctx.enter_context(nc.sbuf_tensor("ada_ring", [P, 4, KD, 512], F32))
        cv = ctx.enter_context(nc.sbuf_tensor("cv", [P, KD, 2], F32))
        sg = ctx.enter_context(nc.sbuf_tensor("cv_sig", [P, KD, 2], F32))
        sv = ctx.enter_context(nc.sbuf_tensor("cv_silu", [P, KD, 2], F32))
        row = ctx.enter_context(nc.sbuf_tensor("mod_row", [2, 6 * D], F32))
        ps = ctx.enter_context(nc.psum_tensor("mod_ps", [P, 2, 512], F32))
        psT = ctx.enter_context(nc.psum_tensor("modT_ps", [P, 512], F32))
        with nc.Block() as block:

            @block.sync
            def _(sp):
                sp.dma_start(k.cst_sb[:], k.d_cst).then_inc(cst_in.sem, 16)
                sp.dma_start(cv[:], k.d_c).then_inc(cst_in.sem, 16)
                sp.dma_start(k.par_sb[:], k.d_par).then_inc(cst_in.sem, 16)
                for l in range(DEPTH):
                    with sp.Fori(0, NB // 4) as i:
                        for j in range(4):
                            sp.wait_ge(block_done.sem, block_done.at(l * NB + 1 + j) + i * 4)
                            sp.dma_start(ring[:, j], k.d_ada[l, bass.ds(i * 4 + j, 1)].rearrange(
                                "a p (k n) -> p (a k) n", k=KD)).then_inc(ada_in[j].sem, 16)

            @block.gpsimd
            def _(pool):
                pool.memset(k.scratch[:, 0:1], 0.0).then_inc(block_done.sem, 4)
                pool.memset(k.scratch[:, 1:2], 0.0).then_inc(row_out.sem, 2)

            @block.scalar
            def _(act):
                act.wait_ge(cst_in.sem, cst_in.at(48))
                act.activation(sg[:], cv[:], ACT.Sigmoid).then_inc(silu.sem, 1)
                for l in range(DEPTH):
                    if l:
                        act.wait_ge(turned.sem, turned.at(l))
                    with act.Fori(0, NB // 2) as i:
                        for j in range(2):
                            act.wait_ge(block_done.sem, block_done.at(l * NB + j + 5) + i * 2)
                            act.activation(row[:, bass.ds(i * 1024 + j * 512, 512)], ps[0:2, j], ACT.Copy
                                           ).then_inc(row_out.sem, 1)

            @block.tensor
            def _(pe):
                pe.wait_ge(silu.sem, silu.at(2))
                for l in range(DEPTH):
                    with pe.Fori(0, NB // 4) as i:
                        for j in range(4):
                            pe.wait_ge(ada_in[j].sem, ada_in[j].at(l * NB * 4 + 16) + i * 16)
                            pe.wait_ge(row_out.sem, row_out.at(l * NB + j + 1) + i * 4)
                            for c in range(KD):
                                last = pe.matmul(ps[0:2, j % 2], sv[:, c], ring[:, j, c], start=c == 0,
                                                 stop=c == KD - 1)
                            last.then_inc(block_done.sem, 1)
                    pe.wait_ge(row_out.sem, row_out.at((l + 1) * NB + 2))
                    if l:
                        pe.wait_ge(mod_done.sem, mod_done.at(l))
                    for j in range(6 * KD):
                        last = pe.transpose(psT[:, 2 * j:2 * j + 2], row[:, j * P:(j + 1) * P],
                                            k.cst("ident", 2)[:, 0:2])
                    last.then_inc(turned.sem, 1)

            @block.vector
            def _(dve):
                dve.wait_ge(silu.sem, silu.at(1))
                dve.tensor_tensor(sv[:], sg[:], cv[:], ALU.mult).then_inc(silu.sem, 1)
                for l in range(DEPTH):
                    dve.wait_ge(turned.sem, turned.at(l + 1))
                    for s in range(2):
                        dve.tensor_tensor(k.mod[:, l, s], psT[:, 0:12 * KD].rearrange("p (j s) -> p s j", s=2)[:, s],
                                          k.par(l, "bada"), ALU.add)
                    dve.drain()
                    for s in range(2):
                        for at, g in ((1, "n1"), (4, "n2")):
                            last = dve.scalar_tensor_tensor(
                                out=k.mod[:, l, s, at * KD:(at + 1) * KD], in0=k.mod[:, l, s, at * KD:(at + 1) * KD],
                                scalar=1.0, in1=k.par(l, g), op0=ALU.add, op1=ALU.mult)
                    last.then_inc(mod_done.sem, 1)
        for s, n in zip((cst_in, silu, block_done, row_out, turned, mod_done), (48, 2, 2 * NB + 4, 2 * NB + 2, 2, 2)):
            s.advance(n)
        for s in ada_in:
            s.advance(2 * 4 * NB)


def stage_norm(nc, k, l, which, x, h, t0, x_source=None):
    sq_done, sum_done, root_done, scaled, h_done, x_in = k.signals(
        "norm_sq", "norm_sum", "norm_root", "norm_scaled", "norm_h", "norm_x_in")
    N = T - t0
    shift, scale = (0, 1) if which == 1 else (3, 4)
    with ExitStack() as ctx:
        tmp = ctx.enter_context(nc.sbuf_tensor(f"norm_tmp{l}{which}", [P, KD, T], F32))
        rstd = ctx.enter_context(nc.sbuf_tensor(f"norm_rstd{l}{which}", [P, T], F32))
        ps = ctx.enter_context(nc.psum_tensor(f"norm_ps{l}{which}", [P, 512], F32))
        with nc.Block(no_gpsimd_drain=True) as block:
            if x_source is not None:
                @block.sync
                def _(sp):
                    for c in range(KD):
                        sp.dma_start(x[:, c], x_source[:, c]).then_inc(x_in.sem, 16)

            @block.scalar
            def _(act):
                if x_source is not None:
                    act.wait_ge(x_in.sem, x_in.at(16 * KD))
                for c in range(KD):
                    act.activation(tmp[:, c, t0:T], x[:, c, t0:T], ACT.Square).then_inc(sq_done.sem, 1)
                act.wait_ge(sum_done.sem, sum_done.at(1))
                act.activation(rstd[:, t0:T], ps[:, 0:N], ACT.Sqrt, scale=1.0 / D, bias=k.cst("eps")[:, 0:1]
                               ).then_inc(root_done.sem, 1)
                for c in range(KD):
                    act.wait_ge(scaled.sem, scaled.at(c + 1))
                    for s in range(2):
                        if s * CTX >= t0:
                            last = act.activation(h[:, c, s * CTX:(s + 1) * CTX], tmp[:, c, s * CTX:(s + 1) * CTX],
                                                  ACT.Identity,
                                                  scale=k.mod[:, l, s, scale * KD + c:scale * KD + c + 1],
                                                  bias=k.mod[:, l, s, shift * KD + c:shift * KD + c + 1])
                    last.then_inc(h_done.sem, 1)

            @block.vector
            def _(dve):
                dve.wait_ge(root_done.sem, root_done.at(1))
                dve.reciprocal(rstd[:, t0:T], rstd[:, t0:T])
                dve.drain()
                for c in range(KD):
                    dve.tensor_tensor(tmp[:, c, t0:T], x[:, c, t0:T], rstd[:, t0:T], ALU.mult).then_inc(scaled.sem, 1)

            @block.tensor
            def _(pe):
                for c in range(KD):
                    pe.wait_ge(sq_done.sem, sq_done.at(c + 1))
                    last = pe.matmul(ps[:, 0:N], k.cst("ones"), tmp[:, c, t0:T], start=c == 0, stop=c == KD - 1)
                last.then_inc(sum_done.sem, 1)
        for s, n in zip((sq_done, sum_done, root_done, scaled, h_done), (KD, 1, 1, KD, KD)):
            s.advance(n)
        if x_source is not None:
            x_in.advance(16 * KD)


def stage_projection(nc, k, l, h, pr, pn, vna, vml):
    NBLK = 8
    win0, win1, tile_done, tile_out, h_saved = k.signals("win_in0", "win_in1", "win_tile", "win_out", "h_saved")
    win_in = (win0, win1)
    with ExitStack() as ctx:
        ring = ctx.enter_context(nc.sbuf_tensor(f"win_ring{l}", [P, 2, KD, 512], F32))
        ps = ctx.enter_context(nc.psum_tensor(f"win_ps{l}", [P, 8, 512], F32))
        with nc.Block() as block:

            @block.sync
            def _(sp):
                def load(j, i):
                    sp.dma_start(ring[:, j], k.d_win[l, bass.ds(i * 2 + j, 1)].rearrange(
                        "a p (k n) -> p (a k) n", k=KD)).then_inc(win_in[j].sem, 16)

                load(0, 0)
                load(1, 0)
                sp.dma_start(k.d_h, h[:]).then_inc(h_saved.sem, 16)
                with sp.Fori(1, (NBLK + 2) // 2) as i:
                    for j in range(2):
                        sp.wait_ge(tile_done.sem, tile_done.at(4 * (j - 1)) + i * 8)
                        load(j, i)
                sp.wait_ge(h_saved.sem, h_saved.at(16))

            @block.gpsimd
            def _(pool):
                pool.memset(k.scratch[:, 0:1], 0.0).then_inc(tile_out.sem, 8)

            @block.tensor
            def _(pe):
                with pe.Fori(0, NBLK // 2) as i:
                    for j in range(2):
                        pe.wait_ge(win_in[j].sem, win_in[j].at(16) + i * 16)
                        for m in range(4):
                            b = j * 4 + m
                            pe.wait_ge(tile_out.sem, tile_out.at(b + 1) + i * 8)
                            for c in range(KD):
                                last = pe.matmul(ps[:, b], ring[:, j, c, m * P:(m + 1) * P], h[:, c],
                                                 start=c == 0, stop=c == KD - 1)
                            last.then_inc(tile_done.sem, 1)
                for j in range(2):
                    pe.wait_ge(win_in[j].sem, win_in[j].at((NBLK // 2) * 16 + 16))
                    for tt in range(4):
                        b = j * 4 + tt
                        pe.wait_ge(tile_out.sem, tile_out.at(NBLK * 4 + b + 1))
                        for c in range(KD):
                            last = pe.matmul(ps[:, b], h[:, c, tt * P:(tt + 1) * P], ring[:, j, c],
                                             start=c == 0, stop=c == KD - 1)
                        last.then_inc(tile_done.sem, 1)

            @block.scalar
            def _(act):
                for half, dst in enumerate((pr, pn)):
                    with act.Fori(0, 2) as i:
                        for b in range(8):
                            act.wait_ge(tile_done.sem, tile_done.at(16 * half + b + 1) + i * 8)
                            act.activation(dst[:, bass.ds(i * 8 + b, 1)].rearrange("p a t -> p (a t)"), ps[:, b],
                                           ACT.Copy).then_inc(tile_out.sem, 1)
                for j, dst in enumerate((vna, vml)):
                    for tt in range(4):
                        act.wait_ge(tile_done.sem, tile_done.at(NBLK * 4 + j * 4 + tt + 1))
                        act.activation(dst[:, tt], ps[:, j * 4 + tt], ACT.Copy).then_inc(tile_out.sem, 1)
        for s, n in zip((win0, win1, tile_done, tile_out, h_saved), (80, 80, 40, 48, 16)):
            s.advance(n)


def stage_attention(nc, k, l, pn, vna):
    qt0 = 0 if l == 0 else 2
    units = [(h, qt) for h in range(HEADS) for qt in range(qt0, 4)]
    NU = len(units)
    (bias_in, sq_done, sum_done, root_done, normed, s_done, max_done, exp_done, p_done, t_done, pt_out, o_done,
     o_out, gq_done) = k.signals("na_bias_in", "na_sq", "na_sum", "na_root", "na_normed", "na_scores", 
                                 "na_max", "na_exp", "na_probs", "na_turned", "na_turned_out", "na_pv", "na_pv_out",
                                 "na_gq")

    def nk(u):
        return CTX if units[u][1] < 2 else T

    with ExitStack() as ctx:
        bias = ctx.enter_context(nc.sbuf_tensor(f"na_bias{l}", [P, HEADS, 2, SEQ], F32))
        sq = ctx.enter_context(nc.sbuf_tensor(f"na_sqb{l}", [P, 2, T], F32))
        rstd = ctx.enter_context(nc.sbuf_tensor(f"na_rstd{l}", [P, 2, T], F32))
        gq = ctx.enter_context(nc.sbuf_tensor(f"na_gqb{l}", [P, 1], F32))
        s = ctx.enter_context(nc.sbuf_tensor(f"na_s{l}", [P, 3, T], F32))
        pt = ctx.enter_context(nc.sbuf_tensor(f"na_pt{l}", [P, 2, 4, P], F32))
        neg = ctx.enter_context(nc.sbuf_tensor(f"na_neg{l}", [P, NU], F32))
        tot = ctx.enter_context(nc.sbuf_tensor(f"na_tot{l}", [P, NU], F32))
        rec = ctx.enter_context(nc.sbuf_tensor(f"na_rec{l}", [P, NU], F32))
        psS = ctx.enter_context(nc.psum_tensor(f"na_psS{l}", [P, 3, 512], F32))
        psT = ctx.enter_context(nc.psum_tensor(f"na_psT{l}", [P, 2, 4, P], F32))
        psO = ctx.enter_context(nc.psum_tensor(f"na_psO{l}", [P, 2, 512], F32))
        with nc.Block(no_gpsimd_drain=True) as block:

            @block.sync
            def _(sp):
                sp.dma_start(bias[:], k.d_nab[l].rearrange("p (h q n) -> p h q n", h=HEADS, q=2)
                             ).then_inc(bias_in.sem, 16)

            @block.scalar
            def _(act):
                def root(i):
                    act.wait_ge(sum_done.sem, sum_done.at(i + 1))
                    if i >= 2:
                        act.wait_ge(normed.sem, normed.at(i - 1))
                    act.activation(rstd[:, i % 2], psO[:, i % 2], ACT.Sqrt, scale=1.0 / HD, bias=k.cst("eps")[:, 0:1]
                                   ).then_inc(root_done.sem, 1)

                for i in range(8):
                    if i >= 2:
                        act.wait_ge(sum_done.sem, sum_done.at(i - 1))
                    act.activation(sq[:, i % 2], pn[:, i], ACT.Square).then_inc(sq_done.sem, 1)
                    if i >= 1:
                        root(i - 1)
                root(7)
                for u in range(NU + 2):
                    if u < NU:
                        act.wait_ge(max_done.sem, max_done.at(u + 1))
                        act.activation(s[:, u % 3, 0:nk(u)], s[:, u % 3, 0:nk(u)], ACT.Exp, bias=neg[:, u:u + 1],
                                       accum_out=tot[:, u:u + 1]).then_inc(exp_done.sem, 1)
                    if u >= 2:
                        act.wait_ge(t_done.sem, t_done.at(u - 1))
                        if u >= 4:
                            act.wait_ge(o_done.sem, o_done.at(u - 3))
                        n = nk(u - 2) // P
                        act.activation(pt[:, u % 2, 0:n], psT[:, u % 2, 0:n], ACT.Copy).then_inc(pt_out.sem, 1)

            @block.vector
            def _(dve):
                dve.tensor_scalar(gq[:], k.par(l, "qn"), HD ** -0.5, None, ALU.mult)
                for i in range(8):
                    dve.wait_ge(root_done.sem, root_done.at(i + 1))
                    dve.reciprocal(rstd[:, i % 2], rstd[:, i % 2])
                    dve.drain()
                    dve.scalar_tensor_tensor(out=pn[:, i], in0=pn[:, i], scalar=gq[:] if i < 4 else k.par(l, "kn"),
                                             in1=rstd[:, i % 2], op0=ALU.mult, op1=ALU.mult).then_inc(normed.sem, 1)
                dve.wait_ge(bias_in.sem, bias_in.at(16))
                for u in range(NU + 3):
                    if u < NU:
                        h, qt = units[u]
                        dve.wait_ge(s_done.sem, s_done.at(u + 1))
                        if u >= 3:
                            dve.wait_ge(t_done.sem, t_done.at(u - 2))
                        dve.tensor_copy(s[:, u % 3, 0:CTX], psS[:, u % 3, 0:CTX])
                        if qt >= 2:
                            dve.tensor_tensor(s[:, u % 3, CTX:T], psS[:, u % 3, CTX:T], bias[:, h, qt - 2], ALU.add)
                        dve.drain()
                        dve.tensor_reduce(neg[:, u:u + 1], s[:, u % 3, 0:nk(u)], AX.X, ALU.max, negate=True
                                          ).then_inc(max_done.sem, 1)
                    if 1 <= u <= NU:
                        v = u - 1
                        dve.wait_ge(exp_done.sem, exp_done.at(v + 1))
                        dve.reciprocal(rec[:, v:v + 1], tot[:, v:v + 1])
                        dve.drain()
                        dve.tensor_scalar(s[:, v % 3, 0:nk(v)], s[:, v % 3, 0:nk(v)], rec[:, v:v + 1], None, ALU.mult
                                          ).then_inc(p_done.sem, 1)
                    if u >= 3:
                        v = u - 3
                        h, qt = units[v]
                        r = (h % 2) * HD
                        dve.wait_ge(o_done.sem, o_done.at(v + 1))
                        dve.tensor_copy(pn[r:r + HD, NQ_T + h // 2, qt * P:(qt + 1) * P], psO[r:r + HD, v % 2, 0:P]
                                        ).then_inc(o_out.sem, 1)

            @block.tensor
            def _(pe):
                for i in range(8):
                    pe.wait_ge(sq_done.sem, sq_done.at(i + 1))
                    if i >= 2:
                        pe.wait_ge(root_done.sem, root_done.at(i - 1))
                    pe.matmul(psO[:, i % 2], k.cst("blk"), sq[:, i % 2], start=True, stop=True
                              ).then_inc(sum_done.sem, 1)
                pe.wait_ge(normed.sem, normed.at(8))

                def scores(u):
                    h, qt = units[u]
                    r = (h % 2) * HD
                    if u >= 3:
                        pe.wait_ge(max_done.sem, max_done.at(u - 2))
                    pe.matmul(psS[:, u % 3, 0:nk(u)], pn[r:r + HD, NQ_T + h // 2, qt * P:(qt + 1) * P],
                              pn[r:r + HD, NK_T + h // 2, 0:nk(u)], start=True, stop=True).then_inc(s_done.sem, 1)

                def turn(u):
                    pe.wait_ge(p_done.sem, p_done.at(u + 1))
                    if u >= 2:
                        pe.wait_ge(pt_out.sem, pt_out.at(u - 1))
                    for j in range(nk(u) // P):
                        last = pe.transpose(psT[:, u % 2, j], s[:, u % 3, j * P:(j + 1) * P], k.cst("ident"))
                    last.then_inc(t_done.sem, 1)

                def mix(u):
                    h, qt = units[u]
                    r = (h % 2) * HD
                    n = nk(u) // P
                    pe.wait_ge(pt_out.sem, pt_out.at(u + 1))
                    if u >= 2:
                        pe.wait_ge(o_out.sem, o_out.at(u - 1))
                    for j in range(n):
                        last = pe.matmul(psO[r:r + HD, u % 2, 0:P], vna[:, j, h * HD:(h + 1) * HD], pt[:, u % 2, j],
                                         start=j == 0, stop=j == n - 1)
                    last.then_inc(o_done.sem, 1)

                scores(0)
                scores(1)
                for u in range(NU + 1):
                    if u + 2 < NU:
                        scores(u + 2)
                    if u < NU:
                        turn(u)
                    if u >= 1:
                        mix(u - 1)
        for sg, n in zip((bias_in, sq_done, sum_done, root_done, normed, s_done, max_done, exp_done, p_done,
                          t_done, pt_out, o_done, o_out), (16, 8, 8, 8, 8) + (NU,) * 8):
            sg.advance(n)


def stage_mlstm(nc, k, l, pr, pn, vml):
    (cap_in, tanh_done, sig_done, log_done, b_done, gt_ps, gt_done, rot_ps, rot_done, cst_in, qk_done, bb_done, bs_done, arg_done,
     w_done, pw_done, nd_done, h_dir, hsq_done, hsum_done, hroot_done, o_sig, h_out) = k.signals(
        "ml_cap_in", "ml_tanh", "ml_sigmoid", "ml_log", "ml_b", "ml_gate_turned", "ml_gate_out", "ml_rot_ps", "ml_rot",
        "ml_cst_in", "ml_scores", "ml_bcast", "ml_bcast_out", "ml_arg", "ml_weight", "ml_weighted", "ml_numden", "ml_dir", "ml_hsq",
        "ml_hsum", "ml_hroot", "ml_osig", "ml_out")
    with ExitStack() as ctx:
        def sb(name, shape):
            return ctx.enter_context(nc.sbuf_tensor(f"ml_{name}{l}", shape, F32))

        def pp(name, shape):
            return ctx.enter_context(nc.psum_tensor(f"ml_{name}{l}", shape, F32))

        mc = sb("mc", [P, NMLC])
        cap = sb("cap", [P, 1])
        lf = sb("lf", [8, T])
        ig = sb("ig", [8, T])
        F = sb("F", [8, T])
        side = sb("side", [8, T])
        b = sb("b", [8, T])
        g = sb("g", [8, T])
        gc = sb("gc", [8, CTX])
        gT = sb("gT", [P, 6, 8])
        rot = sb("rot", [P, 4, SEQ])
        w = sb("w", [P, 4, T])
        pw = sb("pw", [P, 3, T])
        den = sb("den", [P, T])
        hh = sb("hh", [P, T])
        bs = sb("bs", [P, T])
        hd = sb("hd", [P, T])
        os = sb("os", [P, T])
        psA = pp("psA", [P, 3, 512])
        psB = pp("psB", [P, 512])
        psN = pp("psN", [P, 512])
        psD = pp("psD", [P, 512])
        psM = pp("psM", [P, 2, 512])
        mask = mc[:, 0:4 * SEQ].rearrange("p (d i n) -> p d i n", d=2, i=2)
        sel = mc[0:8, 4 * SEQ:].rearrange("p (r n) -> p r n", r=8)
        units = [(h, d) for h in range(ML_HEADS) for d in range(2)]
        with nc.Block(no_gpsimd_drain=True) as block:

            @block.sync
            def _(sp):
                sp.dma_start(mc[:], k.d_mlc).then_inc(cst_in.sem, 16)

            @block.scalar
            def _(act):
                act.wait_ge(cap_in.sem, cap_in.at(1))
                act.activation(ig[:], pr[0:8, GATE_T], ACT.Tanh, scale=1 / GATE_CAP, bias=cap[0:8]
                               ).then_inc(tanh_done.sem, 1)
                act.activation(pr[32:40, GATE_T], pr[32:40, GATE_T], ACT.Tanh, scale=1 / GATE_CAP, bias=cap[32:40]
                               ).then_inc(tanh_done.sem, 1)
                act.wait_ge(tanh_done.sem, tanh_done.at(2))
                act.activation(pr[32:40, GATE_T], pr[32:40, GATE_T], ACT.Sigmoid, scale=GATE_CAP
                               ).then_inc(sig_done.sem, 1)
                act.wait_ge(sig_done.sem, sig_done.at(1))
                act.activation(lf[:], pr[32:40, GATE_T], ACT.Ln).then_inc(log_done.sem, 1)
                act.wait_ge(gt_ps.sem, gt_ps.at(1))
                act.activation(gT[:], psM[:, 1, 0:48].rearrange("p (i r) -> p i r", i=6), ACT.Copy
                               ).then_inc(gt_done.sem, 1)
                act.wait_ge(gt_done.sem, gt_done.at(1))
                for u, (h, d) in enumerate(units):
                    row = d * 4 + h
                    act.wait_ge(bb_done.sem, bb_done.at(u + 1))
                    if u:
                        act.wait_ge(pw_done.sem, pw_done.at(3 * u))
                    act.activation(bs[:], psB[:], ACT.Copy).then_inc(bs_done.sem, 1)
                    act.wait_ge(bs_done.sem, bs_done.at(u + 1))
                    for i in range(2):
                        act.activation(w[:, i, CTX:T], bs[:, CTX:T], ACT.Exp, bias=gT[:, 4 + i, row:row + 1])
                    for i in range(2):
                        act.wait_ge(arg_done.sem, arg_done.at(4 * u + 1 + i))
                        act.activation(w[:, i, 0:CTX], w[:, i, 0:CTX], ACT.Exp, bias=gT[:, i, row:row + 1]
                                       ).then_inc(w_done.sem, 1)
                    for i in range(2):
                        act.wait_ge(arg_done.sem, arg_done.at(4 * u + 3 + i))
                        last = act.activation(w[:, 2, i * SEQ:(i + 1) * SEQ], w[:, 2, i * SEQ:(i + 1) * SEQ], ACT.Exp,
                                              bias=gT[:, 2 + i, row:row + 1])
                    last.then_inc(w_done.sem, 1)
                    if d == 1:
                        act.activation(os[:], pn[:, MO_T + h], ACT.Sigmoid).then_inc(o_sig.sem, 1)
                        act.wait_ge(h_dir.sem, h_dir.at(u + 1))
                        act.activation(hd[:], hh[:], ACT.Square).then_inc(hsq_done.sem, 1)
                        act.wait_ge(hsum_done.sem, hsum_done.at(h + 1))
                        act.activation(hd[:], psM[:, 0], ACT.Sqrt, scale=1.0 / P, bias=k.cst("eps")[:, 0:1]
                                       ).then_inc(hroot_done.sem, 1)

            @block.vector
            def _(dve):
                dve.tensor_scalar(cap[0:8], k.par(l, "ib", 8), 1 / GATE_CAP, None, ALU.mult)
                dve.tensor_scalar(cap[32:40], k.par_sb[32:40, l * NPAR + PAR["fb"][0]:l * NPAR + PAR["fb"][0] + 1],
                                  1 / GATE_CAP, None, ALU.mult).then_inc(cap_in.sem, 1)
                for i in range(4):
                    dve.wait_ge(rot_ps.sem, rot_ps.at(i + 1))
                    dve.tensor_tensor(rot[:, i], psM[:, 0, 0:SEQ] if i % 2 == 0 else psN[:, 0:SEQ], k.cst("sin"),
                                      ALU.mult)
                    dve.tensor_tensor(pn[:, MQ_T + i, CTX:T], pn[:, MQ_T + i, CTX:T], k.cst("cos"), ALU.mult)
                    dve.drain()
                    dve.tensor_tensor(pn[:, MQ_T + i, CTX:T], pn[:, MQ_T + i, CTX:T], rot[:, i], ALU.add
                                      ).then_inc(rot_done.sem, 1)
                dve.wait_ge(log_done.sem, log_done.at(1))
                dve.tensor_scalar(ig[:], ig[:], GATE_CAP, None, ALU.mult)
                dve.tensor_tensor_scan(F[:], k.cst("segres", 8), lf[:], 0.0, ALU.mult, ALU.add)
                dve.drain()
                sgn = k.cst("sgn", 8)
                for s in range(2):
                    dve.tensor_scalar(side[:, s * SEQ:(s + 1) * SEQ], lf[:, s * SEQ:(s + 1) * SEQ],
                                      F[:, (s + 1) * SEQ - 1:(s + 1) * SEQ], sgn[:, 1:2], ALU.add, ALU.mult)
                dve.drain()
                dve.scalar_tensor_tensor(out=b[:], in0=F[:], scalar=sgn[:, 0:1], in1=side[:], op0=ALU.mult,
                                         op1=ALU.add)
                dve.drain()
                dve.tensor_tensor(g[:], ig[:], b[:], ALU.subtract)
                dve.drain()
                dve.tensor_scalar(gc[:], g[:, 0:CTX], F[:, CTX - 1:CTX], None, ALU.add).then_inc(b_done.sem, 1)
                dve.wait_ge(cst_in.sem, cst_in.at(16))
                for u, (h, d) in enumerate(units):
                    dve.wait_ge(bs_done.sem, bs_done.at(u + 1))
                    if u:
                        dve.drain()
                    for i in range(2):
                        dve.tensor_tensor(w[:, i, 0:CTX], bs[:, 0:CTX], mask[:, d, i], ALU.add
                                          ).then_inc(arg_done.sem, 1)
                    for i in range(2):
                        dve.tensor_tensor(w[:, 2, i * SEQ:(i + 1) * SEQ], bs[:, CTX:T], mask[:, d, i], ALU.add
                                          ).then_inc(arg_done.sem, 1)
                    if d == 0:
                        dve.wait_ge(qk_done.sem, qk_done.at(h + 1))
                    if u:
                        dve.wait_ge(nd_done.sem, nd_done.at(u))
                    for i in range(3):
                        dve.wait_ge(w_done.sem, w_done.at(3 * u + i + 1))
                        dve.scalar_tensor_tensor(out=pw[:, i], in0=psA[:, i], scalar=HD ** -0.5, in1=w[:, i],
                                                 op0=ALU.mult, op1=ALU.mult).then_inc(pw_done.sem, 1)
                    dve.wait_ge(nd_done.sem, nd_done.at(u + 1))
                    dve.tensor_scalar(den[:], psD[:], -1.0, 1.0, ALU.mult, ALU.max)
                    dve.drain()
                    dve.tensor_tensor(den[:], psD[:], den[:], ALU.max)
                    dve.drain()
                    dve.reciprocal(den[:], den[:])
                    dve.drain()
                    if d == 0:
                        dve.tensor_tensor(hh[:], psN[:], den[:], ALU.mult).then_inc(h_dir.sem, 1)
                    else:
                        dve.tensor_tensor(den[:], psN[:], den[:], ALU.mult)
                        dve.drain()
                        dve.tensor_tensor(hh[:], hh[:], den[:], ALU.add).then_inc(h_dir.sem, 1)
                        dve.wait_ge(hroot_done.sem, hroot_done.at(h + 1))
                        dve.reciprocal(hd[:], hd[:])
                        dve.drain()
                        dve.scalar_tensor_tensor(out=hh[:], in0=hh[:], scalar=k.par(l, "mg")[:, h:h + 1], in1=hd[:],
                                                 op0=ALU.mult, op1=ALU.mult)
                        dve.drain()
                        dve.wait_ge(o_sig.sem, o_sig.at(h + 1))
                        dve.tensor_tensor(pn[:, MO_T + h], hh[:], os[:], ALU.mult).then_inc(h_out.sem, 1)
                        dve.drain()

            @block.tensor
            def _(pe):
                for i in range(4):
                    if i >= 2:
                        pe.wait_ge(rot_done.sem, rot_done.at(i - 1))
                    pe.matmul(psM[:, 0, 0:SEQ] if i % 2 == 0 else psN[:, 0:SEQ], k.cst("perm"), pn[:, MQ_T + i, CTX:T],
                              start=True, stop=True).then_inc(rot_ps.sem, 1)
                pe.wait_ge(b_done.sem, b_done.at(1))
                for i in range(6):
                    src = g[:, i * P:(i + 1) * P] if i < 4 else gc[:, (i - 4) * P:(i - 3) * P]
                    last = pe.transpose(psM[:, 1, i * 8:(i + 1) * 8], src, k.cst("ident", 8)[:, 0:8])
                last.then_inc(gt_ps.sem, 1)
                pe.wait_ge(rot_done.sem, rot_done.at(4))
                pe.wait_ge(cst_in.sem, cst_in.at(16))
                for u, (h, d) in enumerate(units):
                    r = (h % 2) * HD
                    kt, qt = MK_T + h // 2, MQ_T + h // 2
                    if u:
                        pe.wait_ge(pw_done.sem, pw_done.at(3 * u))
                    pe.matmul(psB[:], sel[:, d * 4 + h], b[:], start=True, stop=True).then_inc(bb_done.sem, 1)
                    if d == 0:
                        for i in range(2):
                            pe.matmul(psA[:, i], pn[r:r + HD, kt, i * P:(i + 1) * P], pn[r:r + HD, qt],
                                      start=True, stop=True)
                        for i in range(2):
                            last = pe.matmul(psA[:, 2, i * SEQ:(i + 1) * SEQ],
                                             pn[r:r + HD, kt, CTX + i * P:CTX + (i + 1) * P], pn[r:r + HD, qt, CTX:T],
                                             start=True, stop=True)
                        last.then_inc(qk_done.sem, 1)
                    if u:
                        pe.wait_ge(h_dir.sem, h_dir.at(u))
                    for ps, lhs in ((psN, lambda i: vml[:, i, h * P:(h + 1) * P]), (psD, lambda i: k.cst("ones"))):
                        for i in range(4):
                            pe.wait_ge(pw_done.sem, pw_done.at(3 * u + min(i, 2) + 1))
                            if i < 2:
                                last = pe.matmul(ps[:], lhs(i), pw[:, i], start=i == 0, stop=False)
                            else:
                                last = pe.matmul(ps[:, CTX:T], lhs(i), pw[:, 2, (i - 2) * SEQ:(i - 1) * SEQ],
                                                 start=False, stop=i == 3)
                    last.then_inc(nd_done.sem, 1)
                    if d == 1:
                        pe.wait_ge(hsq_done.sem, hsq_done.at(h + 1))
                        if h:
                            pe.wait_ge(hroot_done.sem, hroot_done.at(h))
                        pe.matmul(psM[:, 0], k.cst("ones"), hd[:], start=True, stop=True).then_inc(hsum_done.sem, 1)
        for sg, n in zip((cap_in, tanh_done, sig_done, log_done, b_done, gt_ps, gt_done, rot_ps, rot_done, cst_in,
                          qk_done, bb_done, bs_done, arg_done, w_done, pw_done, nd_done, h_dir, hsq_done, hsum_done, hroot_done,
                          o_sig, h_out),
                         (1, 2, 1, 1, 1, 1, 1, 4, 4, 16, 4, 8, 8, 32, 24, 24, 8, 8, 4, 4, 4, 4, 4)):
            sg.advance(n)


def stage_rwkv_features(nc, k, l, pr, sg, aa, kk, ka, g):
    (w_in, mix_done, sum_done, own_done, shifted, act_done, lora_done, lora_out, vf_moved, low_out, gate_out, v_done,
     ksq_done, ksum_done, kroot_done, kk_done) = k.signals(
        "rw_w_in", "rw_mix", "rw_shift_sum", "rw_shift_own", "rw_shifted", "rw_lora_in", "rw_lora", "rw_lora_out",
        "rw_vf", "rw_low_out", "rw_vgate", "rw_v", "rw_ksq", "rw_ksum", "rw_kroot", "rw_kk")
    NT = 15
    jobs = [("w", d, c) for d in range(2) for c in range(KC)] + [("a", d, c) for d in range(2) for c in range(KC)] + \
        [("g", None, c) for c in range(KC)]
    if l:
        jobs += [("v1", None, 0)] + [("v2", None, c) for c in range(KC)]
    with ExitStack() as ctx:
        def sb(name, shape):
            return ctx.enter_context(nc.sbuf_tensor(f"rf_{name}{l}", shape, F32))

        lw = sb("lw", [P, 3 * C + KC * 32 + C])
        m1 = sb("m1", [P, NT])
        mh = sb("mh", [P, NT])
        oka = sb("oka", [P, KC])
        s = sb("s", [P, 2, T])
        sq = sb("sq", [P, 2, T])
        root = sb("root", [P, 2, T])
        if l:
            vf = sb("vf", [P, KC, T])
            vs = sb("vs", [P, KC, T])
            low = sb("low", [32, T])
        ps = ctx.enter_context(nc.psum_tensor(f"rf_ps{l}", [P, 4, 512], F32))
        psK = ctx.enter_context(nc.psum_tensor(f"rf_psK{l}", [P, 2, 512], F32))
        w2, a2, g2 = lw[:, 0:C], lw[:, C:2 * C], lw[:, 2 * C:3 * C]
        v1 = lw[:, 3 * C:3 * C + KC * 32].rearrange("p (c n) -> p c n", c=KC)
        v2 = lw[0:32, 3 * C + KC * 32:]
        with nc.Block(no_gpsimd_drain=True) as block:

            @block.sync
            def _(sp):
                sp.dma_start(lw[:], k.d_lora[l]).then_inc(w_in.sem, 16)
                if l:
                    sp.dma_start(vf[:], k.d_vf).then_inc(vf_moved.sem, 16)
                else:
                    sp.wait_ge(shifted.sem, shifted.at(NT))
                    sp.dma_start(k.d_vf, pr[:, V_T:V_T + KC]).then_inc(vf_moved.sem, 16)
                    sp.wait_ge(vf_moved.sem, vf_moved.at(16))

            @block.scalar
            def _(act):
                act.wait_ge(mix_done.sem, mix_done.at(1))
                for i in range(NT):
                    act.wait_ge(sum_done.sem, sum_done.at(i + 1))
                    act.activation(pr[:, i], pr[:, i], ACT.Identity, scale=m1[:, i:i + 1]).then_inc(own_done.sem, 1)
                act.wait_ge(shifted.sem, shifted.at(NT))
                act.activation(pr[:, WD_T], pr[:, WD_T], ACT.Tanh).then_inc(act_done.sem, 1)
                act.activation(pr[:, GD_T], pr[:, GD_T], ACT.Sigmoid).then_inc(act_done.sem, 1)
                for n, (kind, d, c) in enumerate(jobs):
                    act.wait_ge(lora_done.sem, lora_done.at(n + 1))
                    if kind == "w":
                        last = act.activation(sg[:, d, c], ps[:, n % 4], ACT.Sigmoid,
                                              bias=k.par(l, "w0")[:, d * KC + c:d * KC + c + 1])
                    elif kind == "a":
                        last = act.activation(aa[:, d, c], ps[:, n % 4], ACT.Sigmoid,
                                              bias=k.par(l, "a0")[:, d * KC + c:d * KC + c + 1])
                    elif kind == "g":
                        last = act.activation(g[:, c], ps[:, n % 4], ACT.Copy)
                    elif kind == "v1":
                        last = act.activation(low[:], ps[0:32, n % 4], ACT.Copy)
                    else:
                        last = act.activation(vs[:, c], ps[:, n % 4], ACT.Sigmoid, bias=k.par(l, "v0")[:, c:c + 1])
                    last.then_inc(lora_out.sem, 1)
                for c in range(KC):
                    act.wait_ge(ksum_done.sem, ksum_done.at(c + 1))
                    if c >= 2:
                        act.wait_ge(kk_done.sem, kk_done.at(c - 1))
                    act.activation(root[:, c % 2], psK[:, c % 2], ACT.Sqrt).then_inc(kroot_done.sem, 1)

            @block.vector
            def _(dve):
                mu = k.par(l, "mu")
                dve.tensor_scalar(m1[:], mu, -1.0, 1.0, ALU.mult, ALU.add)
                dve.tensor_scalar(oka[:], k.par(l, "ka"), -1.0, 1.0, ALU.mult, ALU.add)
                dve.tensor_scalar(mh[:], mu, 0.5, None, ALU.mult).then_inc(mix_done.sem, 1)

                def both(ap):
                    return ap.rearrange("p (s t) -> p s t", s=2)

                def finish(i):
                    dve.wait_ge(own_done.sem, own_done.at(i + 1))
                    dve.scalar_tensor_tensor(out=pr[:, i], in0=s[:, i % 2], scalar=mh[:, i:i + 1], in1=pr[:, i],
                                             op0=ALU.mult, op1=ALU.add).then_inc(shifted.sem, 1)

                for i in range(NT):
                    z, o = both(pr[:, i]), both(s[:, i % 2])
                    dve.drain()
                    dve.tensor_tensor(o[:, :, 1:SEQ - 1], z[:, :, 0:SEQ - 2], z[:, :, 2:SEQ], ALU.add)
                    dve.tensor_copy(o[:, :, 0:SEQ:SEQ - 1], z[:, :, 1:SEQ - 1:SEQ - 3]).then_inc(sum_done.sem, 1)
                    if i:
                        finish(i - 1)
                dve.drain()
                finish(NT - 1)
                dve.drain()
                for c in range(KC):
                    dve.tensor_scalar(kk[:, c], pr[:, K_T + c], k.par(l, "kk")[:, c:c + 1], None, ALU.mult)
                    dve.drain()
                    if c >= 2:
                        dve.wait_ge(ksum_done.sem, ksum_done.at(c - 1))
                    dve.tensor_tensor(sq[:, c % 2], kk[:, c], kk[:, c], ALU.mult).then_inc(ksq_done.sem, 1)
                for c in range(KC):
                    dve.tensor_scalar(ka[:, c], pr[:, K_T + c], k.par(l, "ka")[:, c:c + 1], None, ALU.mult)
                    dve.tensor_scalar(pr[:, K_T + c], pr[:, K_T + c], oka[:, c:c + 1], None, ALU.mult)
                for c in range(KC):
                    dve.wait_ge(kroot_done.sem, kroot_done.at(c + 1))
                    dve.tensor_scalar(root[:, c % 2], root[:, c % 2], 1e-12, None, ALU.max)
                    dve.drain()
                    dve.reciprocal(root[:, c % 2], root[:, c % 2])
                    dve.drain()
                    dve.tensor_tensor(kk[:, c], kk[:, c], root[:, c % 2], ALU.mult).then_inc(kk_done.sem, 1)
                if l:
                    dve.wait_ge(vf_moved.sem, vf_moved.at(16))
                    dve.wait_ge(lora_out.sem, lora_out.at(len(jobs)))
                    for c in range(KC):
                        dve.tensor_tensor(vf[:, c], vf[:, c], pr[:, V_T + c], ALU.subtract)
                    dve.drain()
                    for c in range(KC):
                        dve.tensor_tensor(vf[:, c], vf[:, c], vs[:, c], ALU.mult)
                    dve.drain()
                    for c in range(KC):
                        dve.tensor_tensor(pr[:, V_T + c], pr[:, V_T + c], vf[:, c], ALU.add)

            @block.tensor
            def _(pe):
                pe.wait_ge(w_in.sem, w_in.at(16))
                pe.wait_ge(act_done.sem, act_done.at(2))
                for n, (kind, d, c) in enumerate(jobs):
                    if n >= 4:
                        pe.wait_ge(lora_out.sem, lora_out.at(n - 3))
                    o = ps[:, n % 4]
                    if kind in "wa":
                        src, wt = (pr[:, WD_T], w2) if kind == "w" else (pr[:, AD_T], a2)
                        r = d * HD
                        last = pe.matmul(o, wt[r:r + HD, c * P:(c + 1) * P], src[r:r + HD], start=True, stop=True)
                    elif kind == "g":
                        last = pe.matmul(o, g2[:, c * P:(c + 1) * P], pr[:, GD_T], start=True, stop=True)
                    elif kind == "v1":
                        for i in range(KC):
                            last = pe.matmul(ps[0:32, n % 4], v1[:, i], pr[:, V_T + i], start=i == 0, stop=i == KC - 1)
                    else:
                        if c == 0:
                            pe.wait_ge(lora_out.sem, lora_out.at(n))
                        last = pe.matmul(o, v2[:, c * P:(c + 1) * P], low[:], start=True, stop=True)
                    last.then_inc(lora_done.sem, 1)
                for c in range(KC):
                    pe.wait_ge(ksq_done.sem, ksq_done.at(c + 1))
                    if c >= 2:
                        pe.wait_ge(kroot_done.sem, kroot_done.at(c - 1))
                    pe.matmul(psK[:, c % 2], k.cst("blk"), sq[:, c % 2], start=True, stop=True
                              ).then_inc(ksum_done.sem, 1)
        for x, n in zip((w_in, mix_done, sum_done, own_done, shifted, act_done, lora_done, lora_out, vf_moved,
                         ksq_done, ksum_done, kroot_done, kk_done),
                        (16, 1, NT, NT, NT, 2, len(jobs), len(jobs), 16, KC, KC, KC, KC)):
            x.advance(n)


def stage_rwkv_scan(nc, k, l, pr, pn, sg, aa, kk, ka, y):
    names = ("gates", "exps", "feats", "mats", "turned", "masked", "parts", "tok", "cmask", "x", "xi", "nn", "nout",
             "rhs", "rhsout", "u", "uout", "sy", "yout", "state")
    per_step = dict(gates=1, exps=1, feats=1, mats=1, turned=1, masked=1, parts=1, tok=1, cmask=2, x=6, xi=6, nn=5,
                    nout=5, rhs=1, rhsout=1, u=1, uout=1, sy=1, yout=1, state=1)
    sem = [dict(zip(names, k.signals(*[f"scan{d}_{n}" for n in names]))) for d in range(2)]
    (waited,) = k.signals("scan_waited", fresh=True)
    NCH = SEQ // L
    with ExitStack() as ctx:
        def sb(name, shape):
            return [ctx.enter_context(nc.sbuf_tensor(f"sc_{name}{l}{d}", shape, F32)) for d in range(2)]

        sgs = sb("sgs", [P, KC, L])
        F = sb("F", [P, KC, L])
        E = sb("E", [P, KC, L])
        R = sb("R", [P, KC, L])
        Z = sb("Z", [P, KC, L])
        vst = sb("vst", [P, KC, L])
        ex = sb("ex", [P, 4, KC, L])
        bb, kd, S2 = E, R, Z
        ra = [sb("ra", [P, KC, 2, L]),
              [pn[:, NK_T + d].rearrange("p (c a n) -> p c a n", c=KC, a=2) for d in range(2)]]
        hat = sb("hat", [P, KC, 3, L])
        pri = sb("pri", [P, KC, 3, L])
        M = sb("M", [P, 2, KC, P])
        at = sb("at", [P, KC, L])
        cm = [pr[:, WD_T:WD_T + 3].rearrange("p a (b c n) -> p (a b) c n", b=2, c=KC),
              ctx.enter_context(nc.sbuf_tensor(f"sc_cm{l}", [P, 6, KC, L], F32))[:]]
        N = sb("N", [P, KC, L])
        NT = sb("NT", [P, KC, L])
        XI = sb("XI", [P, KC, L])
        bk = sb("bk", [P, HEADS, L])
        uv = sb("uv", [P, HEADS, L])
        rhs = sb("rhsb", [P, KC, L])
        S = sb("S", [P, KC, L])
        wl = [sb(f"wl{b}", [P, KC]) for b in range(2)]
        ps = [ctx.enter_context(nc.psum_tensor(f"sc_ps{l}{d}", [P, 4, 512], F32)) for d in range(2)]

        def half(d, bank, i):
            return ps[d][:, bank, i * 256:(i + 1) * 256].rearrange("p (c n) -> p c n", c=KC)

        psA = [ps[d][:, 0:2].rearrange("p b (h n) -> p b h n", n=P) for d in range(2)]
        psX = [half(d, 0, 0) for d in range(2)]
        psN = [half(d, 0, 1) for d in range(2)]
        psNT = [half(d, 1, 0) for d in range(2)]
        psR = [half(d, 3, 1) for d in range(2)]
        psBK = [[half(d, 2 + o, 0) for o in range(2)] for d in range(2)]
        psV = [[half(d, 2 + o, 1) for o in range(2)] for d in range(2)]
        psAV = [half(d, 2, 1) for d in range(2)]
        psU = [half(d, 2, 0) for d in range(2)]
        psS = [half(d, 2, 1) for d in range(2)]
        psY = [half(d, 3, 0) for d in range(2)]

        def columns(d, seg, i):
            return bass.ds(seg * SEQ + (i * L if d == 0 else (NCH - 1) * L - i * L), L)

        def w(eng, d, name, seg, i, n=1):
            s, m = sem[d][name], per_step[name]
            eng.wait_ge(s.sem, s.at(n) + (seg * NCH + i) * m)

        eye = k.cst("eye").unsqueeze(1).broadcast_to([P, KC, L])
        with nc.Block(no_gpsimd_drain=True) as block:

            @block.scalar
            def _(act):
                def exponentials(seg, i):
                    for d in range(2):
                        w(act, d, "gates", seg, i)
                        incl, excl, prime = (F, E, R) if d == 0 else (Z, R, E)
                        act.activation(wl[i % 2][d][:], F[d][:, :, L - 1], ACT.Exp, scale=-DECAY)
                        act.activation(ex[d][:, 0], incl[d][:], ACT.Exp, scale=-DECAY)
                        act.activation(ex[d][:, 1], excl[d][:], ACT.Exp, scale=-DECAY)
                        act.activation(ex[d][:, 2], incl[d][:], ACT.Exp, scale=DECAY)
                        act.activation(ex[d][:, 3], prime[d][:], ACT.Exp, scale=-DECAY).then_inc(sem[d]["exps"].sem, 1)

                def step(seg, i):
                    for d in range(2):
                        w(act, d, "turned", seg, i)
                        act.activation(bk[d][:, 0:HEADS:2], psBK[d][0], ACT.Copy)
                        act.activation(bk[d][:, 1:HEADS:2], psBK[d][1], ACT.Copy)
                        act.activation(uv[d][HD:P, 0:HEADS:2], psV[d][0][HD:P], ACT.Copy)
                        act.activation(uv[d][0:HD, 1:HEADS:2], psV[d][1][0:HD], ACT.Copy
                                       ).then_inc(sem[d]["tok"].sem, 1)
                        w(act, d, "masked", seg, i)
                        act.activation(at[d][0:HD], M[d][0:HD, 0, :, L:P], ACT.Copy)
                        act.activation(at[d][HD:P], M[d][HD:P, 1, :, L:P], ACT.Copy
                                       ).then_inc(sem[d]["parts"].sem, 1)
                    for m in range(1, 6):
                        for d in range(2):
                            w(act, d, "nn", seg, i, m)
                            if m < 5:
                                act.activation(N[d][:], psN[d], ACT.Copy)
                            act.activation(NT[d][:], psNT[d], ACT.Copy).then_inc(sem[d]["nout"].sem, 1)
                        if m == 1 and i + 1 < NCH:
                            exponentials(seg, i + 1)
                    for d in range(2):
                        w(act, d, "u", seg, i)
                        act.activation(uv[d][0:HD, 0:HEADS:2], psU[d][0:HD], ACT.Copy)
                        act.activation(uv[d][HD:P, 1:HEADS:2], psU[d][HD:P], ACT.Copy).then_inc(sem[d]["uout"].sem, 1)
                    for d in range(2):
                        w(act, d, "sy", seg, i)
                        act.activation(y[:, d, :, columns(d, seg, i)], psY[d], ACT.Copy
                                       ).then_inc(sem[d]["yout"].sem, 1)

                with act.Fori(0, 2) as seg:
                    exponentials(seg, 0)
                    for i in range(NCH):
                        step(seg, i)

            @block.vector
            def _(dve):
                for d in range(2):
                    dve.memset(S[d][:], 0.0).then_inc(sem[d]["state"].sem, 1)
                    dve.memset(k.scratch[:, d:d + 1], 0.0).then_inc(sem[d]["yout"].sem, 1)
                dve.drain()

                def cumulate(d, seg, i):
                    col = columns(d, seg, i)
                    dve.tensor_copy(sgs[d][:], sg[:, d, :, col])
                    dve.tensor_copy(vst[d][:], pr[:, V_T:V_T + KC, col])
                    dve.drain()
                    dve.tensor_tensor_scan(F[d][:].rearrange("p c n -> p (c n)"), k.cst("reset"),
                                           sgs[d][:].rearrange("p c n -> p (c n)"), 0.0, ALU.mult, ALU.add)
                    dve.drain()
                    dve.tensor_tensor(R[d][:], F[d][:, :, L - 1:L].broadcast_to([P, KC, L]), F[d][:], ALU.subtract)
                    dve.tensor_tensor(E[d][:], F[d][:], sgs[d][:], ALU.subtract)
                    dve.drain()
                    dve.tensor_tensor(Z[d][:], R[d][:], sgs[d][:], ALU.add).then_inc(sem[d]["gates"].sem, 1)

                def operands(d, seg, i):
                    col = columns(d, seg, i)
                    o_ra = ra[i % 2][d]
                    w(dve, d, "exps", seg, i)
                    dve.tensor_tensor(bb[d][:], kk[:, :, col], aa[:, d, :, col], ALU.mult)
                    dve.tensor_tensor(kd[d][:], ka[:, :, col], aa[:, d, :, col], ALU.mult)
                    dve.drain()
                    dve.tensor_tensor(kd[d][:], kd[d][:], pr[:, K_T:K_T + KC, col], ALU.add)
                    dve.tensor_tensor(o_ra[:, :, 0], pr[:, R_T:R_T + KC, col], ex[d][:, 0], ALU.mult)
                    dve.scalar_tensor_tensor(out=o_ra[:, :, 1], in0=kk[:, :, col], scalar=-1.0,
                                             in1=ex[d][:, 1], op0=ALU.mult, op1=ALU.mult)
                    dve.drain()
                    for o, e in ((hat, 2), (pri, 3)):
                        dve.tensor_tensor(o[d][:, :, 0], bb[d][:], ex[d][:, e], ALU.mult)
                        dve.tensor_tensor(o[d][:, :, 1], kd[d][:], ex[d][:, e], ALU.mult)
                        last = dve.tensor_tensor(o[d][HD:P, :, 2], bb[d][HD:P], ex[d][HD:P, e], ALU.mult)
                    last.then_inc(sem[d]["feats"].sem, 1)

                def step(seg, i):
                    for d in range(2):
                        w(dve, d, "mats", seg, i)
                        for o in range(2):
                            last = dve.tensor_tensor(M[d][:, o], psA[d][:, o],
                                                     k.cst(f"mra{d}").unsqueeze(1).broadcast_to([P, KC, P]), ALU.mult)
                        last.then_inc(sem[d]["masked"].sem, 1)

                    def levels(d, first, end):
                        lev = k.cst(f"lev{d}").rearrange("p (m n) -> p m n", m=6)
                        for m in range(first, end):
                            last = dve.tensor_tensor(cm[d][:, m], at[d][:],
                                                     lev[:, m].unsqueeze(1).broadcast_to([P, KC, L]), ALU.mult)
                        return last

                    def correct(d, m):
                        w(dve, d, "x", seg, i, m + 1)
                        dve.tensor_tensor(N[d][:] if m == 0 else XI[d][:], psX[d], eye, ALU.add
                                          ).then_inc(sem[d]["xi"].sem, 1)

                    for d in range(2):
                        w(dve, d, "parts", seg, i)
                        levels(d, 0, 1)
                        dve.drain()
                        dve.tensor_tensor(NT[d][:], cm[d][:, 0], eye, ALU.add).then_inc(sem[d]["cmask"].sem, 1)
                        if d == 0:
                            levels(0, 1, 6).then_inc(sem[0]["cmask"].sem, 1)
                    correct(0, 0)
                    levels(1, 1, 6).then_inc(sem[1]["cmask"].sem, 1)
                    correct(1, 0)
                    for m in range(1, 6):
                        for d in range(2):
                            correct(d, m)
                        if i + 1 < NCH:
                            if m == 1:
                                for d in range(2):
                                    w(dve, d, "turned", seg, i)
                                    cumulate(d, seg, i + 1)
                            elif m in (2, 3):
                                operands(m - 2, seg, i + 1)
                    for d in range(2):
                        w(dve, d, "rhs", seg, i)
                        dve.tensor_copy(rhs[d][:], psR[d])
                        dve.drain()
                        dve.tensor_tensor(rhs[d][:], rhs[d][:], psAV[d], ALU.add).then_inc(sem[d]["rhsout"].sem, 1)
                        dve.tensor_tensor(S2[d][:], S[d][:], wl[i % 2][d][:].unsqueeze(2).broadcast_to([P, KC, L]),
                                          ALU.mult)
                    dve.drain()
                    for d in range(2):
                        w(dve, d, "sy", seg, i)
                        dve.tensor_tensor(S[d][:], S2[d][:], psS[d], ALU.add).then_inc(sem[d]["state"].sem, 1)
                    dve.drain()

                with dve.Fori(0, 2) as seg:
                    for d in range(2):
                        cumulate(d, seg, 0)
                    for d in range(2):
                        operands(d, seg, 0)
                    for i in range(NCH):
                        step(seg, i)

            @block.tensor
            def _(pe):
                heads = [(h, h // 2, (h % 2) * HD) for h in range(HEADS)]
                def wp(d, name, seg, i, n=1):
                    w(pe, d, name, seg, i, n)
                    pe.sem_inc(waited.sem, 1)

                def step(seg, i):
                    for d in range(2):
                        w(pe, d, "feats", seg, i)
                        for h, hp, r in heads:
                            o = h % 2
                            last = pe.matmul(psA[d][:, o, hp], hat[d][r:r + HD, hp, o:o + 2].rearrange("p a n -> p (a n)"),
                                             ra[i % 2][d][r:r + HD, hp].rearrange("p a n -> p (a n)"), start=True, stop=True)
                        last.then_inc(sem[d]["mats"].sem, 1)
                        wp(d, "state", seg, i)
                        wp(d, "yout", seg, i)
                        for h, hp, r in heads:
                            o = h % 2
                            pe.transpose(psBK[d][o][:, hp], pri[d][r:r + HD, hp, o:o + 2].rearrange("p a n -> p (a n)"),
                                         k.cst("ident")[r:r + HD, r:r + HD])
                        for h, hp, r in heads:
                            q = HD - r
                            last = pe.matmul(psV[d][h % 2][q:q + HD, hp], vst[d][r:r + HD, hp],
                                             k.cst("ident")[r:r + HD, r:r + HD], start=True, stop=True)
                        last.then_inc(sem[d]["turned"].sem, 1)
                    for m in range(6):
                        for d in range(2):
                            if m == 0:
                                wp(d, "cmask", seg, i)
                            elif m > 1:
                                wp(d, "nout", seg, i, m - 1)
                            else:
                                wp(d, "xi", seg, i, 1)
                                wp(d, "cmask", seg, i, 2)
                            for h, hp, r in heads:
                                last = pe.matmul(psX[d][r:r + HD, hp], cm[d][r:r + HD, m, hp],
                                                 N[d][r:r + HD, hp] if m else k.cst("eye")[r:r + HD],
                                                 start=True, stop=True)
                            last.then_inc(sem[d]["x"].sem, 1)
                        if m == 0:
                            continue
                        for d in range(2):
                            wp(d, "xi", seg, i, m + 1)
                            for h, hp, r in heads:
                                if m < 5:
                                    pe.matmul(psN[d][r:r + HD, hp], NT[d][r:r + HD, hp], XI[d][r:r + HD, hp],
                                              start=True, stop=True)
                                last = pe.matmul(psNT[d][r:r + HD, hp], XI[d][r:r + HD, hp], NT[d][r:r + HD, hp],
                                                 start=True, stop=True)
                            last.then_inc(sem[d]["nn"].sem, 1)
                    for d in range(2):
                        wp(d, "tok", seg, i)
                        for h, hp, r in heads:
                            q = HD - r
                            pe.matmul(psR[d][r:r + HD, hp], ra[i % 2][d][r:r + HD, hp, 1], S[d][r:r + HD, hp],
                                      start=True, stop=True)
                            last = pe.matmul(psAV[d][r:r + HD, hp], M[d][q:q + HD, h % 2, hp, L:P], uv[d][q:q + HD, h],
                                             start=True, stop=True)
                        last.then_inc(sem[d]["rhs"].sem, 1)
                    for d in range(2):
                        wp(d, "rhsout", seg, i)
                        wp(d, "nout", seg, i, 5)
                        for h, hp, r in heads:
                            last = pe.matmul(psU[d][r:r + HD, hp], NT[d][r:r + HD, hp], rhs[d][r:r + HD, hp],
                                             start=True, stop=True)
                        last.then_inc(sem[d]["u"].sem, 1)
                    for d in range(2):
                        wp(d, "uout", seg, i)
                        for h, hp, r in heads:
                            pe.matmul(psS[d][r:r + HD, hp], bk[d][:, h], uv[d][:, h], start=True, stop=True)
                        for h, hp, r in heads:
                            pe.matmul(psY[d][r:r + HD, hp], S[d][r:r + HD, hp], ra[i % 2][d][r:r + HD, hp, 0],
                                      start=True, stop=False)
                            last = pe.matmul(psY[d][r:r + HD, hp], uv[d][:, h], M[d][:, h % 2, hp, 0:L],
                                             start=False, stop=True)
                        last.then_inc(sem[d]["sy"].sem, 1)

                with pe.Fori(0, 2) as seg:
                    for i in range(NCH):
                        step(seg, i)
        for d in range(2):
            for n in names:
                sem[d][n].advance(per_step[n] * 2 * NCH + (n in ("state", "yout")))


def stage_rwkv_readout(nc, k, l, pr, aa, ka, g, y):
    (y_sum, mean_ps, cen, sq_done, var_ps, root_done, bon_in, bon_ps, out_done) = k.signals(
        "ro_ysum", "ro_mean", "ro_centred", "ro_sq", "ro_var", "ro_root", "ro_bonus_in", "ro_bonus", "ro_out")
    with ExitStack() as ctx:
        def sb(name):
            return ctx.enter_context(nc.sbuf_tensor(f"ro_{name}{l}", [P, 2, T], F32))

        sq, root, bon, t1 = sb("sq"), sb("root"), sb("bon"), sb("t1")
        psM = ctx.enter_context(nc.psum_tensor(f"ro_psM{l}", [P, 2, 512], F32))
        psV = ctx.enter_context(nc.psum_tensor(f"ro_psV{l}", [P, 2, 512], F32))
        psB = ctx.enter_context(nc.psum_tensor(f"ro_psB{l}", [P, 2, 512], F32))
        with nc.Block(no_gpsimd_drain=True) as block:

            @block.vector
            def _(dve):
                for c in range(KC):
                    dve.tensor_tensor(y[:, 0, c], y[:, 0, c], y[:, 1, c], ALU.add).then_inc(y_sum.sem, 1)
                for c in range(KC):
                    dve.tensor_tensor(t1[:, c % 2], aa[:, 0, c], aa[:, 1, c], ALU.add)
                    dve.drain()
                    dve.tensor_tensor(t1[:, c % 2], t1[:, c % 2], ka[:, c], ALU.mult)
                    dve.drain()
                    dve.scalar_tensor_tensor(out=t1[:, c % 2], in0=pr[:, K_T + c], scalar=2.0, in1=t1[:, c % 2],
                                             op0=ALU.mult, op1=ALU.add)
                    dve.drain()
                    if c >= 2:
                        dve.wait_ge(bon_ps.sem, bon_ps.at(c - 1))
                    dve.scalar_tensor_tensor(out=bon[:, c % 2], in0=t1[:, c % 2], scalar=k.par(l, "rk")[:, c:c + 1],
                                             in1=pr[:, R_T + c], op0=ALU.mult, op1=ALU.mult).then_inc(bon_in.sem, 1)
                    dve.wait_ge(mean_ps.sem, mean_ps.at(c + 1))
                    dve.scalar_tensor_tensor(out=y[:, 0, c], in0=psM[:, c % 2], scalar=-1.0 / HD, in1=y[:, 0, c],
                                             op0=ALU.mult, op1=ALU.add).then_inc(cen.sem, 1)
                    dve.wait_ge(bon_ps.sem, bon_ps.at(c + 1))
                    dve.tensor_tensor(t1[:, c % 2], psB[:, c % 2], pr[:, V_T + c], ALU.mult)
                    dve.wait_ge(root_done.sem, root_done.at(c + 1))
                    dve.reciprocal(root[:, c % 2], root[:, c % 2])
                    dve.drain()
                    dve.tensor_tensor(y[:, 0, c], y[:, 0, c], root[:, c % 2], ALU.mult)
                    dve.drain()
                    dve.tensor_scalar(y[:, 0, c], y[:, 0, c], k.par(l, "lg")[:, c:c + 1], k.par(l, "lb")[:, c:c + 1],
                                      ALU.mult, ALU.add)
                    dve.drain()
                    dve.tensor_tensor(y[:, 0, c], y[:, 0, c], t1[:, c % 2], ALU.add)
                    dve.drain()
                    dve.tensor_tensor(pr[:, R_T + c], y[:, 0, c], g[:, c], ALU.mult).then_inc(out_done.sem, 1)

            @block.scalar
            def _(act):
                for c in range(KC):
                    act.wait_ge(cen.sem, cen.at(c + 1))
                    if c >= 2:
                        act.wait_ge(var_ps.sem, var_ps.at(c - 1))
                    act.activation(sq[:, c % 2], y[:, 0, c], ACT.Square).then_inc(sq_done.sem, 1)
                    act.wait_ge(var_ps.sem, var_ps.at(c + 1))
                    if c >= 2:
                        act.wait_ge(out_done.sem, out_done.at(c - 1))
                    act.activation(root[:, c % 2], psV[:, c % 2], ACT.Sqrt, scale=1.0 / HD, bias=k.cst("eps")[:, 1:2]
                                   ).then_inc(root_done.sem, 1)

            @block.tensor
            def _(pe):
                for c in range(KC):
                    pe.wait_ge(y_sum.sem, y_sum.at(c + 1))
                    if c >= 2:
                        pe.wait_ge(cen.sem, cen.at(c - 1))
                    pe.matmul(psM[:, c % 2], k.cst("blk"), y[:, 0, c], start=True, stop=True).then_inc(mean_ps.sem, 1)
                    pe.wait_ge(bon_in.sem, bon_in.at(c + 1))
                    if c >= 2:
                        pe.wait_ge(out_done.sem, out_done.at(c - 1))
                    pe.matmul(psB[:, c % 2], k.cst("blk"), bon[:, c % 2], start=True, stop=True
                              ).then_inc(bon_ps.sem, 1)
                    pe.wait_ge(sq_done.sem, sq_done.at(c + 1))
                    if c >= 2:
                        pe.wait_ge(root_done.sem, root_done.at(c - 1))
                    pe.matmul(psV[:, c % 2], k.cst("blk"), sq[:, c % 2], start=True, stop=True).then_inc(var_ps.sem, 1)
        for x in (y_sum, mean_ps, cen, sq_done, var_ps, root_done, bon_in, bon_ps, out_done):
            x.advance(KC)


def stage_merge(nc, k, l, pr, pn, x, h, t0, x_source):
    N = T - t0
    (w_in, mg_in, wo_in, hx_in, g_done, g_out, y_done, y_used, merged, o_done, x_done, x_saved) = k.signals(
        "mg_w_in0", "mg_w_in1", "mg_wo_in", "mg_hx_in", "mg_gate", "mg_gate_out", "mg_y", "mg_y_used", "mg_merged",
        "mg_o", "mg_x", "mg_x_saved")
    ring_in = (w_in, mg_in)
    NW = 3 * KD + 3 * KC
    with ExitStack() as ctx:
        ring = ctx.enter_context(nc.sbuf_tensor(f"mg_ring{l}", [P, 2, NW, P], F32))
        wo = ctx.enter_context(nc.sbuf_tensor(f"mg_wo{l}", [P, KD, D], F32))
        gate = ctx.enter_context(nc.sbuf_tensor(f"mg_gateb{l}", [P, 3, T], F32))
        mg = ctx.enter_context(nc.sbuf_tensor(f"mg_m{l}", [P, KD, T], F32))
        psG = ctx.enter_context(nc.psum_tensor(f"mg_psG{l}", [P, 3, 512], F32))
        psY = ctx.enter_context(nc.psum_tensor(f"mg_psY{l}", [P, 3, 512], F32))
        psO = ctx.enter_context(nc.psum_tensor(f"mg_psO{l}", [P, 2, 512], F32))
        branch = (lambda c: pr[:, R_T + c, t0:T], lambda c: pn[:, NQ_T + c, t0:T], lambda c: pn[:, MO_T + c, t0:T])
        with nc.Block(no_gpsimd_drain=True) as block:

            @block.sync
            def _(sp):
                def load(j, i):
                    sp.dma_start(ring[:, j], k.d_mg[l, bass.ds(i * 2 + j, 1)].rearrange(
                        "a p (k n) -> p (a k) n", n=P)).then_inc(ring_in[j].sem, 16)

                sp.dma_start(h[:, :, t0:T], k.d_h[:, :, t0:T]).then_inc(hx_in.sem, 16)
                load(0, 0)
                load(1, 0)
                sp.dma_start(wo[:], k.d_wo[l]).then_inc(wo_in.sem, 16)
                sp.dma_start(x[:, :, t0:T], x_source[:, :, t0:T]).then_inc(wo_in.sem, 16)
                with sp.Fori(1, KD // 2) as i:
                    for j in range(2):
                        sp.wait_ge(y_done.sem, y_done.at(3 * (j - 1)) + i * 6)
                        load(j, i)
                sp.wait_ge(x_done.sem, x_done.at(KD))
                sp.dma_start(k.d_x[:, :, t0:T], x[:, :, t0:T]).then_inc(x_saved.sem, 16)
                sp.wait_ge(x_saved.sem, x_saved.at(16))

            @block.gpsimd
            def _(pool):
                pool.memset(k.scratch[:, 0:1], 0.0).then_inc(y_used.sem, 1)

            @block.tensor
            def _(pe):
                pe.wait_ge(hx_in.sem, hx_in.at(16))
                with pe.Fori(0, KD // 2) as i:
                    for j in range(2):
                        pe.wait_ge(ring_in[j].sem, ring_in[j].at(16) + i * 16)
                        pe.wait_ge(y_used.sem, y_used.at(1 + j) + i * 2)
                        for b in range(3):
                            for c in range(KD):
                                last = pe.matmul(psG[:, b, 0:N], ring[:, j, b * KD + c], h[:, c, t0:T],
                                                 start=c == 0, stop=c == KD - 1)
                            last.then_inc(g_done.sem, 1)
                        for b in range(3):
                            for c in range(KC):
                                last = pe.matmul(psY[:, b, 0:N], ring[:, j, 3 * KD + b * KC + c], branch[b](c),
                                                 start=c == 0, stop=c == KC - 1)
                            last.then_inc(y_done.sem, 1)
                pe.wait_ge(wo_in.sem, wo_in.at(32))
                pe.wait_ge(merged.sem, merged.at(KD))
                for m in range(KD):
                    if m >= 2:
                        pe.wait_ge(x_done.sem, x_done.at(m - 1))
                    for c in range(KD):
                        last = pe.matmul(psO[:, m % 2, 0:N], wo[:, c, m * P:(m + 1) * P], mg[:, c, t0:T],
                                         start=c == 0, stop=c == KD - 1)
                    last.then_inc(o_done.sem, 1)

            @block.scalar
            def _(act):
                with act.Fori(0, KD // 2) as i:
                    for j in range(2):
                        act.wait_ge(y_used.sem, y_used.at(1 + j) + i * 2)
                        for b in range(3):
                            act.wait_ge(g_done.sem, g_done.at(3 * j + b + 1) + i * 6)
                            act.activation(gate[:, b, 0:N], psG[:, b, 0:N], ACT.Sigmoid).then_inc(g_out.sem, 1)

            @block.vector
            def _(dve):
                with dve.Fori(0, KD // 2) as i:
                    for j in range(2):
                        for b in range(3):
                            dve.wait_ge(g_out.sem, g_out.at(3 * j + b + 1) + i * 6)
                            dve.wait_ge(y_done.sem, y_done.at(3 * j + b + 1) + i * 6)
                            dve.tensor_tensor(gate[:, b, 0:N], gate[:, b, 0:N], psY[:, b, 0:N], ALU.mult)
                        dve.drain()
                        dve.tensor_tensor(gate[:, 0, 0:N], gate[:, 0, 0:N], gate[:, 1, 0:N], ALU.add)
                        dve.drain()
                        dve.tensor_tensor(mg[:, bass.ds(i * 2 + j, 1), t0:T].rearrange("p a t -> p (a t)"),
                                          gate[:, 0, 0:N], gate[:, 2, 0:N], ALU.add).then_inc(merged.sem, 1)
                        dve.wait_ge(merged.sem, merged.at(j + 1) + i * 2)
                        dve.memset(k.scratch[:, 1:2], 0.0).then_inc(y_used.sem, 1)
                for m in range(KD):
                    dve.wait_ge(o_done.sem, o_done.at(m + 1))
                    for s in range(2):
                        if s * CTX >= t0:
                            last = dve.scalar_tensor_tensor(
                                out=x[:, m, s * CTX:(s + 1) * CTX], in0=psO[:, m % 2, s * CTX - t0:(s + 1) * CTX - t0],
                                scalar=k.mod[:, l, s, 2 * KD + m:2 * KD + m + 1], in1=x[:, m, s * CTX:(s + 1) * CTX],
                                op0=ALU.mult, op1=ALU.add)
                    last.then_inc(x_done.sem, 1)
        for s, n in zip((w_in, mg_in, wo_in, hx_in, g_done, g_out, y_done, y_used, merged, o_done, x_done, x_saved),
                        (64, 64, 32, 16, 24, 24, 24, 9, 8, 8, 8, 16)):
            s.advance(n)


def stage_dispatch(nc, k, l, x, h, t0, gj, passes):
    N = T - t0
    NTT = N // P
    NE, GS = E_ROUTED, E_ROUTED // GROUPS
    (w_in, sw_in, s_ps, s_out, picked, maskT, placedT, place_ps, placed, ht_ps, ht_out, ht_moved,
     tab_set, tab_free, tok_ids, gu_done, sig_done, act_done, d_done, x_done) = k.signals(
        "rt_w_in", "sh_w_in", "rt_scores_ps", "rt_scores", "rt_picked", "rt_mask_turned", 
        "rt_place_turned", "rt_place_back", "rt_placed", "ht_ps", "ht_out", "ht_moved", "tab_fill",
        "tab_filled", "tok_ids", "sh_gu", "sh_sig", "sh_act", "sh_down", "sh_x")
    (scattered,) = k.signals("scattered", fresh=True)
    with ExitStack() as ctx:
        def sb(name, shape, dt=F32):
            return ctx.enter_context(nc.sbuf_tensor(f"rt_{name}{l}", shape, dt))

        wr = sb("wr", [P, KD + 1, NE])
        sw = sb("sw", [P, 2, 3 * KD, P])
        sc = sb("sc", [P, NTT, NE])
        sel = sb("sel", [P, NTT, NE])
        top = sb("top", [P, NTT, GROUPS, 8])
        gs = sb("gs", [P, NTT, GROUPS])
        best = sb("best", [P, NTT, 8])
        rep = sb("rep", [P, NTT, GROUPS])
        msk = sb("msk", [P, NTT, GROUPS])
        neg = sb("neg", [P, NTT, GROUPS])
        cut = sb("cut", [P, NTT, NE])
        pick = sb("pick", [P, NTT, NE])
        gates = sb("gates", [P, NTT, NE])
        tot = sb("tot", [P, NTT])
        one = sb("one", [NE, N])
        mT = sb("mT", [NE, N])
        rank = sb("rank", [NE, N])
        plT = sb("plT", [NE, N])
        place = sb("place", [P, NTT, NE])
        last8 = sb("last8", [P, NTT, 8])
        eq = sb("eq", [P, NTT, 8, NE])
        cmax = sb("cmax", [1, 8])
        ids = sb("ids", [P, NTT, TOP_K], U32)
        addr = sb("addr", [P, NTT * TOP_K], U32)
        fill = sb("fill", [P, T * NE // P], U32)
        ht = sb("ht", [P, 2, KD, P])
        sg = sb("sg", [P, 2, T])
        a = sb("a", [P, 2, T])
        psR = ctx.enter_context(nc.psum_tensor(f"rt_psR{l}", [P, 512], F32))
        psH = ctx.enter_context(nc.psum_tensor(f"rt_psH{l}", [P, 2, 4, P], F32))
        psG = ctx.enter_context(nc.psum_tensor(f"rt_psG{l}", [P, 2, 512], F32))
        psC = ctx.enter_context(nc.psum_tensor(f"rt_psC{l}", [P, 512], F32))
        psD = ctx.enter_context(nc.psum_tensor(f"rt_psD{l}", [P, 2, 512], F32))
        psS = psR[:, 0:NTT * NE].rearrange("p (t e) -> p t e", e=NE)
        with nc.Block() as block:

            @block.sync
            def _(sp):
                sp.dma_start(wr[:], k.d_rt[l].rearrange("p (c n) -> p c n", n=NE)).then_inc(w_in.sem, 16)
                sp.dma_start(sw[:], k.d_moe[l, E_ROUTED:E_ALL].rearrange("a p (c n) -> p a c n", n=P)
                             ).then_inc(sw_in.sem, 16)
                sp.wait_ge(tab_set.sem, tab_set.at(1))
                sp.dma_start(k.d_tab.rearrange("(p n) o -> p (n o)", p=P), fill[:]).then_inc(tab_free.sem, 16)
                for tt in range(NTT):
                    sp.wait_ge(ht_out.sem, ht_out.at(2 * (tt + 1)))
                    sp.dma_start(k.d_ht[tt * P:(tt + 1) * P], ht[:, tt % 2].rearrange("p c n -> p (c n)")
                                 ).then_inc(ht_moved.sem, 16)
                    sp.wait_ge(ht_moved.sem, ht_moved.at(16 * (tt + 1)))

            @block.gpsimd
            def _(pool):
                pool.memset(fill[:], NO_TOKEN).then_inc(tab_set.sem, 1)
                pool.iota(ids[:], [[P * TOP_K, NTT], [1, TOP_K]], base=0, channel_multiplier=TOP_K).then_inc(tok_ids.sem, 1)
                pool.wait_ge(tok_ids.sem, tok_ids.at(1))
                pool.wait_ge(tab_free.sem, tab_free.at(16))
                pool.wait_ge(placed.sem, placed.at(1))
                for tt in range(NTT):
                    for j in range(8):
                        m = tt * 8 + j
                        pool.indirect_dma_start(k.d_tab, bass.IndirectOffsetOnAxis(ap=addr[:, m:m + 1], axis=0),
                                                ids[:, tt, j:j + 1], None).then_inc(scattered.sem, 16)
                pool.wait_ge(scattered.sem, scattered.at(16 * 8 * NTT))

            @block.tensor
            def _(pe):
                pe.wait_ge(w_in.sem, w_in.at(16))
                for tt in range(NTT):
                    for c in range(KD):
                        last = pe.matmul(psS[:, tt], h[:, c, t0 + tt * P:t0 + (tt + 1) * P], wr[:, c],
                                         start=c == 0, stop=c == KD - 1)
                last.then_inc(s_ps.sem, 1)

                def turn_tokens(tt):
                    for q in range(2):
                        if tt:
                            pe.wait_ge(ht_out.sem, ht_out.at(2 * tt - 1 + q))
                        for c in range(4):
                            last = pe.transpose(psH[:, q, c], h[:, q * 4 + c, t0 + tt * P:t0 + (tt + 1) * P],
                                                k.cst("ident"))
                        last.then_inc(ht_ps.sem, 1)

                for tt in range(NTT):
                    turn_tokens(tt)
                pe.wait_ge(picked.sem, picked.at(1))
                for tt in range(NTT):
                    last = pe.transpose(psR[0:NE, tt * P:(tt + 1) * P], pick[:, tt], k.cst("ident"))
                last.then_inc(maskT.sem, 1)
                pe.wait_ge(sw_in.sem, sw_in.at(16))

                def gate_up(j):
                    for q in range(2):
                        if j:
                            pe.wait_ge(act_done.sem, act_done.at(j))
                        for c in range(KD):
                            last = pe.matmul(psG[:, q, 0:N], sw[:, j, q * KD + c], h[:, c, t0:T],
                                             start=c == 0, stop=c == KD - 1)
                    last.then_inc(gu_done.sem, 1)

                gate_up(0)
                pe.wait_ge(placedT.sem, placedT.at(1))
                for tt in range(NTT):
                    pe.transpose(psS[:, tt], plT[:, tt * P:(tt + 1) * P], k.cst("ident", NE)[:, 0:NE])
                pe.transpose(psC[0:1, 0:NE], rank[:, N - 1:N], k.cst("ident", NE)[:, 0:NE]).then_inc(place_ps.sem, 1)
                gate_up(1)
                pe.wait_ge(act_done.sem, act_done.at(2))
                for c in range(KD):
                    if c >= 2:
                        pe.wait_ge(x_done.sem, x_done.at(c - 1))
                    for j in range(2):
                        last = pe.matmul(psD[:, c % 2, 0:N], sw[:, j, 2 * KD + c], a[:, j, 0:N],
                                         start=j == 0, stop=j == 1)
                    last.then_inc(d_done.sem, 1)

            @block.scalar
            def _(act):
                act.wait_ge(s_ps.sem, s_ps.at(1))
                act.activation(sc[:], psS, ACT.Sigmoid).then_inc(s_out.sem, 1)
                for tt in range(NTT):
                    for q in range(2):
                        act.wait_ge(ht_ps.sem, ht_ps.at(2 * tt + q + 1))
                        if tt >= 2:
                            act.wait_ge(ht_moved.sem, ht_moved.at(16 * (tt - 1)))
                        act.activation(ht[:, tt % 2, q * 4:q * 4 + 4], psH[:, q], ACT.Copy).then_inc(ht_out.sem, 1)
                for j in range(2):
                    act.wait_ge(gu_done.sem, gu_done.at(j + 1))
                    act.activation(sg[:, j, 0:N], psG[:, 0, 0:N], ACT.Sigmoid).then_inc(sig_done.sem, 1)

            @block.vector
            def _(dve):
                dve.memset(one[:], 1.0)
                dve.wait_ge(s_out.sem, s_out.at(1))
                for tt in range(NTT):
                    dve.tensor_tensor(sel[:, tt], sc[:, tt], wr[:, KD], ALU.add)
                dve.drain()
                for tt in range(NTT):
                    for q in range(GROUPS):
                        dve.max(top[:, tt, q], sel[:, tt, q * GS:(q + 1) * GS])
                dve.drain()
                dve.tensor_tensor(gs[:], top[:, :, :, 0], top[:, :, :, 1], ALU.add)
                dve.drain()
                for tt in range(NTT):
                    dve.max(best[:, tt], gs[:, tt])
                dve.drain()
                dve.memset(best[:, :, TOPK_GROUPS:8], -NEG)
                dve.drain()
                for tt in range(NTT):
                    dve.match_replace(rep[:, tt], best[:, tt], gs[:, tt], NEG)
                dve.drain()
                dve.tensor_scalar(msk[:], rep[:], NEG, None, ALU.is_equal)
                dve.drain()
                dve.tensor_scalar(neg[:], msk[:], -1.0, -NEG, ALU.add, ALU.mult)
                dve.drain()
                for tt in range(NTT):
                    dve.tensor_tensor(cut[:, tt].rearrange("p (q e) -> p q e", q=GROUPS),
                                      sel[:, tt].rearrange("p (q e) -> p q e", q=GROUPS),
                                      msk[:, tt].unsqueeze(2).broadcast_to([P, GROUPS, GS]), ALU.mult)
                dve.drain()
                for tt in range(NTT):
                    g3 = cut[:, tt].rearrange("p (q e) -> p q e", q=GROUPS)
                    dve.tensor_tensor(g3, g3, neg[:, tt].unsqueeze(2).broadcast_to([P, GROUPS, GS]), ALU.add)
                dve.drain()
                for tt in range(NTT):
                    dve.max(best[:, tt], cut[:, tt])
                dve.drain()
                for tt in range(NTT):
                    dve.match_replace(pick[:, tt], best[:, tt], cut[:, tt], 2 * NEG)
                dve.drain()
                dve.tensor_scalar(pick[:], pick[:], 2 * NEG, None, ALU.is_equal).then_inc(picked.sem, 1)
                dve.wait_ge(picked.sem, picked.at(1))
                dve.tensor_tensor(gates[:], pick[:], sc[:], ALU.mult)
                dve.drain()
                dve.tensor_reduce(tot[:], gates[:], AX.X, ALU.add)
                dve.drain()
                dve.reciprocal(tot[:], tot[:])
                dve.drain()
                for tt in range(NTT):
                    dve.tensor_scalar(gates[:, tt], gates[:, tt], tot[:, tt:tt + 1], ROUTED_SCALE, ALU.mult, ALU.mult)
                dve.wait_ge(maskT.sem, maskT.at(1))
                dve.tensor_copy(mT[:], psR[0:NE, 0:N])
                dve.drain()
                dve.tensor_tensor_scan(rank[:], one[:], mT[:], 0.0, ALU.mult, ALU.add)
                dve.drain()
                dve.tensor_scalar(plT[:], rank[:], float(NE), k.cst("ecol", NE), ALU.mult, ALU.add)
                dve.drain()
                dve.tensor_tensor(plT[:], plT[:], mT[:], ALU.mult).then_inc(placedT.sem, 1)
                dve.wait_ge(place_ps.sem, place_ps.at(1))
                dve.tensor_copy(place[:], psS)
                dve.tensor_reduce(cmax[:, 0:1], psC[0:1, 0:NE], AX.X, ALU.max)
                dve.drain()
                dve.tensor_scalar(cmax[:, 1:2], cmax[:, 0:1], float(SLOTS), 1.0, ALU.is_gt, ALU.add)
                dve.tensor_scalar(cmax[:, 2:3], cmax[:, 0:1], float(2 * SLOTS), None, ALU.is_gt)
                dve.tensor_scalar(cmax[:, 3:4], cmax[:, 0:1], float(3 * SLOTS), None, ALU.is_gt)
                dve.drain()
                dve.tensor_reduce(cmax[:, 4:5], cmax[:, 1:4], AX.X, ALU.add)
                for tt in range(NTT):
                    dve.max(last8[:, tt], place[:, tt])
                dve.drain()
                dve.tensor_copy(passes[:], cmax[:, 4:5])
                dve.tensor_scalar(addr[:], last8[:].rearrange("p t j -> p (t j)"), -1.0, None, ALU.add
                                  ).then_inc(placed.sem, 1)
                for tt in range(NTT):
                    for j in range(8):
                        dve.scalar_tensor_tensor(out=eq[:, tt, j], in0=place[:, tt], scalar=last8[:, tt, j:j + 1],
                                                 in1=gates[:, tt], op0=ALU.is_equal, op1=ALU.mult)
                dve.drain()
                dve.tensor_reduce(gj[:], eq[:].rearrange("p t j e -> p (t j) e"), AX.X, ALU.add)
                for j in range(2):
                    dve.wait_ge(sig_done.sem, sig_done.at(j + 1))
                    dve.tensor_tensor(sg[:, j, 0:N], sg[:, j, 0:N], psG[:, 0, 0:N], ALU.mult)
                    dve.drain()
                    dve.tensor_tensor(a[:, j, 0:N], sg[:, j, 0:N], psG[:, 1, 0:N], ALU.mult).then_inc(act_done.sem, 1)
                for c in range(KD):
                    dve.wait_ge(d_done.sem, d_done.at(c + 1))
                    for s in range(2):
                        if s * CTX >= t0:
                            last = dve.scalar_tensor_tensor(
                                out=x[:, c, s * CTX:(s + 1) * CTX], in0=psD[:, c % 2, s * CTX - t0:(s + 1) * CTX - t0],
                                scalar=k.mod[:, l, s, 5 * KD + c:5 * KD + c + 1], in1=x[:, c, s * CTX:(s + 1) * CTX],
                                op0=ALU.mult, op1=ALU.add)
                    last.then_inc(x_done.sem, 1)
        for s, n in zip((w_in, sw_in, s_ps, s_out, picked, maskT, placedT, place_ps, placed, ht_ps,
                         ht_out, ht_moved, tab_set, tab_free, tok_ids, gu_done, sig_done, act_done, d_done,
                         x_done),
                        (16, 16, 1, 1, 1, 1, 1, 1, 1, 2 * NTT, 2 * NTT, 16 * NTT, 1, 16, 1, 2, 2, 2,
                         KD, KD)):
            s.advance(n)


def stage_experts(nc, k, l, t0, passes):
    N = T - t0
    UN = 8
    NB = E_ROUTED // UN
    names = ["xp_w0", "xp_w1", "xp_w2", "xp_w3", "xp_g0", "xp_g1", "xp_g2", "xp_g3", "xp_st0", "xp_st1", "xp_tab",
             "xp_tok", "xp_ix", "xp_dst", "xp_waited", "xp_turned", "xp_xt", "xp_gu", "xp_sig", "xp_act", "xp_y", "xp_out0", "xp_out1", "xp_ready"]
    sg_ = k.signals(*names, fresh=True)
    w_in, g_in, stored = sg_[0:4], sg_[4:8], sg_[8:10]
    (tab_in, tok_done, ix_done, dst_done, waited, turned, xt_out, gu_done, sig_done, act_done, y_done, out0, out1,
     ready) = sg_[10:]
    with ExitStack() as ctx:
        def sb(name, shape, dt=F32):
            return ctx.enter_context(nc.sbuf_tensor(f"xp_{name}{l}", shape, dt))

        ring = sb("ring", [P, 4, 3 * KD, P])
        tab = sb("tab", [P, E_ROUTED], U32)
        ix = sb("ix", [P, 4], U32)
        tok = sb("tok", [P, E_ROUTED], U32)
        dst = sb("dst", [P, 2], U32)
        xg = sb("xg", [P, 4, D])
        xt = sb("xt", [P, 2, KD, SLOTS])
        sg = sb("sg", [P, 2, SLOTS])
        a = sb("a", [P, 2, SLOTS])
        y = sb("y", [P, 2, D])
        psT = ctx.enter_context(nc.psum_tensor(f"xp_psT{l}", [P, 2, KD, SLOTS], F32))
        psG = ctx.enter_context(nc.psum_tensor(f"xp_psG{l}", [P, 2, 512], F32))
        psY = ctx.enter_context(nc.psum_tensor(f"xp_psY{l}", [P, 2, 512], F32))
        d_tab = k.d_tab.rearrange("(r s e) o -> r s (e o)", s=SLOTS, e=E_ROUTED)
        with nc.Block() as block:

            def loops(eng):
                return eng.value_load(passes[0:1, 0:1], min_val=1, max_val=T // SLOTS)

            def n_at(r, i, u):
                return r * E_ROUTED + i * UN + u

            @block.sync
            def _(sp):
                R = loops(sp)
                sp.wait_ge(ready.sem, 1)
                with sp.Fori(0, R) as r, sp.Fori(0, NB) as i:
                    for u in range(UN):
                        sp.wait_ge(y_done.sem, n_at(r, i, u) + 1)
                        sp.dma_start(ring[:, u % 4], k.d_moe[l, bass.ds(i * UN + u, 1)].rearrange(
                            "a p (c n) -> p (a c) n", n=P)).then_inc(w_in[u % 4].sem, 16)

            @block.gpsimd
            def _(pool):
                def scatter_rows(j):
                    pool.indirect_dma_start(k.d_y[0:N * TOP_K],
                                            bass.IndirectOffsetOnAxis(ap=dst[:, j:j + 1], axis=0), y[:, j], None,
                                            bounds_check=N * TOP_K - 1, oob_is_err=False).then_inc(stored[j].sem, 16)

                pool.memset(k.scratch[:, 0:1], 0.0).then_inc(y_done.sem, 4)
                pool.memset(k.scratch[:, 1:2], 0.0).then_inc(turned.sem, 4)
                pool.memset(k.scratch[:, 2:3], 0.0).then_inc(out0.sem, 1)
                pool.memset(k.scratch[:, 3:4], 0.0).then_inc(out1.sem, 1)
                pool.memset(xg[:], 0.0).then_inc(ready.sem, 1)
                pool.memset(y[:], 0.0)
                pool.memset(dst[:], NO_TOKEN).then_inc(ready.sem, 1)
                pool.wait_ge(ready.sem, 2)
                for j in range(2):
                    scatter_rows(j)
                R = loops(pool)
                with pool.Fori(0, R) as r:
                    def gather(i, u):
                        pool.wait_ge(turned.sem, n_at(r, i, u) + 1)
                        pool.sem_inc(waited.sem, 1)
                        pool.tensor_copy(ix[:, u % 4:u % 4 + 1], tok[:, bass.ds(i * UN + u, 1)]
                                         ).then_inc(ix_done.sem, 1)
                        pool.wait_ge(ix_done.sem, n_at(r, i, u) + 1)
                        pool.sem_inc(waited.sem, 1)
                        pool.indirect_dma_start(xg[:, u % 4], None, k.d_ht[0:N],
                                                bass.IndirectOffsetOnAxis(ap=ix[:, u % 4:u % 4 + 1], axis=0),
                                                bounds_check=N - 1, oob_is_err=False).then_inc(g_in[u % 4].sem, 16)

                    def scatter(i, u):
                        pool.wait_ge(out0.sem, n_at(r, i, u) + 2)
                        pool.wait_ge(out1.sem, n_at(r, i, u) + 2)
                        pool.sem_inc(waited.sem, 1)
                        pool.tensor_copy(dst[:, u % 2:u % 2 + 1], tab[:, bass.ds(i * UN + u, 1)]
                                         ).then_inc(dst_done.sem, 1)
                        pool.wait_ge(dst_done.sem, n_at(r, i, u) + 1)
                        pool.sem_inc(waited.sem, 1)
                        scatter_rows(u % 2)

                    def ahead(i, last):
                        for u in range(UN):
                            if u + 4 < UN:
                                gather(i, u + 4)
                            elif not last:
                                gather(i + 1, u + 4 - UN)
                            scatter(i, u)

                    pool.dma_start(tab[:], d_tab[bass.ds(r, 1)].rearrange("a s e -> (a s) e")).then_inc(tab_in.sem, 16)
                    pool.wait_ge(tok_done.sem, r + 1)
                    for u in range(4):
                        gather(0, u)
                    with pool.Fori(0, NB - 1) as i:
                        ahead(i, False)
                    ahead(NB - 1, True)
                for j in range(2):
                    pool.wait_ge(stored[j].sem, R * (E_ROUTED // 2 * 16) + 16)
                pool.sem_inc(ready.sem, 1)

            @block.tensor
            def _(pe):
                R = loops(pe)
                with pe.Fori(0, R) as r, pe.Fori(0, NB) as i:
                    def slot_count(u):
                        return (r * (E_ROUTED // 4) + i * (UN // 4) + u // 4) * 16 + 16

                    def turn(u):
                        pe.wait_ge(g_in[u % 4].sem, slot_count(u))
                        for c in range(KD):
                            last = pe.transpose(psT[:, u % 2, c], xg[:, u % 4, c * P:(c + 1) * P], k.cst("ident"))
                        last.then_inc(turned.sem, 1)

                    def gate_up(u):
                        pe.wait_ge(w_in[u % 4].sem, slot_count(u))
                        pe.wait_ge(xt_out.sem, n_at(r, i, u) + 1)
                        for q in range(2):
                            for c in range(KD):
                                last = pe.matmul(psG[:, u % 2, q * SLOTS:(q + 1) * SLOTS], ring[:, u % 4, q * KD + c],
                                                 xt[:, u % 2, c], start=c == 0, stop=c == KD - 1)
                        last.then_inc(gu_done.sem, 1)

                    def down(u):
                        pe.wait_ge(act_done.sem, n_at(r, i, u) + 1)
                        pe.wait_ge(out0.sem, n_at(r, i, u) + 1)
                        pe.wait_ge(out1.sem, n_at(r, i, u) + 1)
                        wd = ring[:, u % 4, 2 * KD:].rearrange("p c n -> p (c n)")
                        for q in range(2):
                            last = pe.matmul(psY[:, q], a[:, u % 2], wd[:, q * 512:(q + 1) * 512],
                                             start=True, stop=True)
                        last.then_inc(y_done.sem, 1)

                    turn(0)
                    for u in range(UN):
                        if u + 1 < UN:
                            turn(u + 1)
                        gate_up(u)
                        if u:
                            down(u - 1)
                    down(UN - 1)

            @block.scalar
            def _(act):
                R = loops(act)
                with act.Fori(0, R) as r, act.Fori(0, NB) as i:
                    def tokens_out(u):
                        act.wait_ge(turned.sem, n_at(r, i, u) + 5)
                        for q in range(2):
                            last = act.activation(xt[:, u % 2, q * 4:q * 4 + 4], psT[:, u % 2, q * 4:q * 4 + 4],
                                                  ACT.Copy)
                        last.then_inc(xt_out.sem, 1)

                    def sigmoid(u):
                        act.wait_ge(gu_done.sem, n_at(r, i, u) + 1)
                        act.activation(sg[:, u % 2], psG[:, u % 2, 0:SLOTS], ACT.Sigmoid).then_inc(sig_done.sem, 1)

                    def rows_out(u):
                        act.wait_ge(y_done.sem, n_at(r, i, u) + 5)
                        act.wait_ge(stored[u % 2].sem, (r * (E_ROUTED // 2) + i * (UN // 2) + u // 2) * 16 + 16)
                        act.activation(y[:, u % 2, 0:512], psY[:, 0], ACT.Copy).then_inc(out0.sem, 1)

                    tokens_out(0)
                    for u in range(UN):
                        if u + 1 < UN:
                            tokens_out(u + 1)
                        sigmoid(u)
                        if u:
                            rows_out(u - 1)
                    rows_out(UN - 1)

            @block.vector
            def _(dve):
                R = loops(dve)
                with dve.Fori(0, R) as r:
                    dve.wait_ge(tab_in.sem, r * 16 + 16)
                    dve.tensor_scalar(tok[:], tab[:], 3, None, ALU.logical_shift_right).then_inc(tok_done.sem, 1)
                    with dve.Fori(0, NB) as i:
                        def activate(u):
                            dve.wait_ge(sig_done.sem, n_at(r, i, u) + 1)
                            dve.tensor_tensor(sg[:, u % 2], sg[:, u % 2], psG[:, u % 2, 0:SLOTS], ALU.mult)
                            dve.drain()
                            dve.tensor_tensor(a[:, u % 2], sg[:, u % 2], psG[:, u % 2, SLOTS:2 * SLOTS], ALU.mult
                                              ).then_inc(act_done.sem, 1)

                        def rows_out(u):
                            dve.wait_ge(y_done.sem, n_at(r, i, u) + 5)
                            dve.wait_ge(stored[u % 2].sem, (r * (E_ROUTED // 2) + i * (UN // 2) + u // 2) * 16 + 16)
                            dve.tensor_copy(y[:, u % 2, 512:D], psY[:, 1]).then_inc(out1.sem, 1)

                        for u in range(UN):
                            activate(u)
                            if u:
                                rows_out(u - 1)
                        rows_out(UN - 1)


def stage_combine(nc, k, l, x, t0, gj):
    N = T - t0
    NTT = N // P
    SL, PER = 4, 2
    NL = NTT * TOP_K // PER
    y_in = k.signals(*[f"cb_y{j}" for j in range(SL)])
    summed, turned, x_done, out_done = k.signals("cb_summed", "cb_turned", "cb_x", "cb_out")
    with ExitStack() as ctx:
        yg = ctx.enter_context(nc.sbuf_tensor(f"cb_yg{l}", [P, SL, PER, D], F32))
        acc = ctx.enter_context(nc.sbuf_tensor(f"cb_acc{l}", [P, 2, D], F32))
        ps = ctx.enter_context(nc.psum_tensor(f"cb_ps{l}", [P, 2, KD, P], F32))
        d_y = k.d_y.rearrange("(t p g j) n -> t g p j n", p=P, g=TOP_K // PER, j=PER)
        with nc.Block() as block:

            @block.sync
            def _(sp):
                for m in range(NL):
                    if m >= SL:
                        sp.wait_ge(summed.sem, summed.at(PER * (m - SL + 1)))
                    sp.dma_start(yg[:, m % SL], d_y[m // (NL // NTT), m % (NL // NTT)]).then_inc(y_in[m % SL].sem, 16)
                sp.wait_ge(x_done.sem, x_done.at(NTT))
                if l == DEPTH - 1:
                    sp.dma_start(k.d_out, x[:, :, CTX:T]).then_inc(out_done.sem, 16)
                else:
                    sp.dma_start(k.d_x, x[:]).then_inc(out_done.sem, 16)
                sp.wait_ge(out_done.sem, out_done.at(16))

            @block.vector
            def _(dve):
                def residual(tt):
                    dve.wait_ge(turned.sem, turned.at(tt + 1))
                    s = (t0 + tt * P) // CTX
                    cols = slice(t0 + tt * P, t0 + (tt + 1) * P)
                    for c in range(KD):
                        last = dve.scalar_tensor_tensor(
                            out=x[:, c, cols], in0=ps[:, tt % 2, c], scalar=k.mod[:, l, s, 5 * KD + c:5 * KD + c + 1],
                            in1=x[:, c, cols], op0=ALU.mult, op1=ALU.add)
                    last.then_inc(x_done.sem, 1)

                for tt in range(NTT):
                    for j in range(TOP_K):
                        n = tt * TOP_K + j
                        m = n // PER
                        if j % PER == 0:
                            dve.wait_ge(y_in[m % SL].sem, y_in[m % SL].at(16 * (m // SL) + 16))
                        row = yg[:, m % SL, j % PER]
                        if j == 0:
                            dve.tensor_scalar(acc[:, tt % 2], row, gj[:, n:n + 1], None, ALU.mult
                                              ).then_inc(summed.sem, 1)
                        else:
                            dve.wait_ge(summed.sem, summed.at(n))
                            dve.scalar_tensor_tensor(out=acc[:, tt % 2], in0=row, scalar=gj[:, n:n + 1],
                                                     in1=acc[:, tt % 2], op0=ALU.mult, op1=ALU.add
                                                     ).then_inc(summed.sem, 1)
                    if tt:
                        residual(tt - 1)
                residual(NTT - 1)

            @block.tensor
            def _(pe):
                for tt in range(NTT):
                    pe.wait_ge(summed.sem, summed.at(8 * (tt + 1)))
                    if tt >= 2:
                        pe.wait_ge(x_done.sem, x_done.at(tt - 1))
                    for c in range(KD):
                        last = pe.transpose(ps[:, tt % 2, c], acc[:, tt % 2, c * P:(c + 1) * P], k.cst("ident"))
                    last.then_inc(turned.sem, 1)

        for j in range(SL):
            y_in[j].advance(16 * NL // SL)
        for s, n in zip((summed, turned, x_done, out_done), (8 * NTT, NTT, NTT, 16)):
            s.advance(n)


def hybrid_backbone_kernel(nc, d):
    k = Kit(nc)
    k.d_cst, k.d_par, k.d_mlc, k.d_xin, k.d_c, k.d_ada = (d[n] for n in ("cst", "par", "mlc", "xin", "c", "ada"))
    k.d_win, k.d_mg, k.d_wo, k.d_lora, k.d_nab = (d[n] for n in ("win", "mg", "wo", "lora", "nab"))
    k.d_rt, k.d_moe, k.d_out = d["rt"], d["moe"], d["out"]
    k.d_x = nc.dram_tensor("x_keep", (P, KD, T), F32).ap()
    k.d_h = nc.dram_tensor("h_keep", (P, KD, T), F32).ap()
    k.d_vf = nc.dram_tensor("v_first", (P, KC, T), F32).ap()
    k.d_ht = nc.dram_tensor("h_rows", (T, D), F32).ap()
    k.d_tab = nc.dram_tensor("places", (T * E_ROUTED, 1), U32).ap()
    k.d_y = nc.dram_tensor("y_rows", (T * TOP_K, D), F32).ap()
    with ExitStack() as top:
        def keep(name, shape, dt=F32):
            return top.enter_context(nc.sbuf_tensor(name, shape, dt))

        k.cst_sb = keep("cst", [P, NCST])
        k.par_sb = keep("par", [P, DEPTH * NPAR])
        k.mod = keep("mod", [P, DEPTH, 2, 6 * KD])
        k.scratch = keep("scratch", [P, 8])
        stage_modulation(nc, k)
        k.end_stage()
        for l in range(DEPTH):
            t0 = 0 if l < DEPTH - 1 else CTX
            x_source = k.d_xin if l == 0 else k.d_x
            with ExitStack() as lay:
                pr = lay.enter_context(nc.sbuf_tensor(f"pr{l}", [P, 16, T], F32))
                pn = lay.enter_context(nc.sbuf_tensor(f"pn{l}", [P, 16, T], F32))
                with ExitStack() as mix:
                    vna = mix.enter_context(nc.sbuf_tensor(f"vna{l}", [P, 4, C], F32))
                    vml = mix.enter_context(nc.sbuf_tensor(f"vml{l}", [P, 4, C], F32))
                    with nc.sbuf_tensor(f"h1_{l}", [P, KD, T], F32) as h:
                        with nc.sbuf_tensor(f"x1_{l}", [P, KD, T], F32) as x:
                            stage_norm(nc, k, l, 1, x, h, 0, x_source)
                            k.end_stage()
                        stage_projection(nc, k, l, h, pr, pn, vna, vml)
                        k.end_stage()
                    stage_attention(nc, k, l, pn, vna)
                    k.end_stage()
                    stage_mlstm(nc, k, l, pr, pn, vml)
                    k.end_stage()
                with ExitStack() as rw:
                    def big(name, shape):
                        return rw.enter_context(nc.sbuf_tensor(f"{name}{l}", shape, F32))

                    sg = big("decay", [P, 2, KC, T])
                    aa = big("aa", [P, 2, KC, T])
                    kk = big("kkn", [P, KC, T])
                    ka = big("kka", [P, KC, T])
                    g = big("gg", [P, KC, T])
                    stage_rwkv_features(nc, k, l, pr, sg, aa, kk, ka, g)
                    k.end_stage()
                    stage_rwkv_scan(nc, k, l, pr, pn, sg, aa, kk, ka, sg)
                    k.end_stage()
                    stage_rwkv_readout(nc, k, l, pr, aa, ka, g, sg)
                    k.end_stage()
                with nc.sbuf_tensor(f"x2_{l}", [P, KD, T], F32) as x, nc.sbuf_tensor(f"h2_{l}", [P, KD, T], F32) as h:
                    stage_merge(nc, k, l, pr, pn, x, h, t0, x_source)
                    k.end_stage()
            NTT = (T - t0) // P
            with nc.sbuf_tensor(f"x3_{l}", [P, KD, T], F32) as x, \
                    nc.sbuf_tensor(f"gj{l}", [P, NTT * 8], F32) as gj, nc.sbuf_tensor(f"ps{l}", [1, 1], U32) as passes:
                with nc.sbuf_tensor(f"h3_{l}", [P, KD, T], F32) as h:
                    stage_norm(nc, k, l, 2, x, h, t0, k.d_x)
                    k.end_stage()
                    stage_dispatch(nc, k, l, x, h, t0, gj, passes)
                    k.end_stage()
                stage_experts(nc, k, l, t0, passes)
                k.end_stage()
                stage_combine(nc, k, l, x, t0, gj)
                k.end_stage()


def layout(i):
    f = np.float32
    a = {n: np.asarray(v) for n, v in i.items()}

    def tiles(v):
        return np.moveaxis(v.reshape(*v.shape[:-1], -1, P), -1, -2)

    def wt(w, cols=None):
        return w.reshape(-1, P, w.shape[-1]).transpose(1, 0, 2)

    out = {}
    xin = np.concatenate([a["ctx"][0], a["x"][0]], 0)
    out["xin"] = xin.T.reshape(KD, P, T).transpose(1, 0, 2)
    out["c"] = np.stack([a["c_ctx"], a["c"][0]], -1).reshape(KD, P, 2).transpose(1, 0, 2)
    out["ada"] = a["w_ada"].reshape(DEPTH, KD, P, 12, 512).transpose(0, 3, 2, 1, 4).reshape(DEPTH, 12, P, KD * 512)
    o = np.cumsum([0, C, C, C, 384, C, C, C, 256, 256, C, C, 16])
    w = a["w_in"]
    r, kk, v, lora, nq, nk_, nv, mq, mk, mv, mo, gates = [w[:, :, o[j]:o[j + 1]] for j in range(12)]
    gt = np.zeros((DEPTH, D, P), f)
    gt[:, :, 0:8], gt[:, :, 32:40] = gates[:, :, 0:8], gates[:, :, 8:16]
    blocks = [r, kk, v, np.concatenate([lora, gt], -1), nq, nk_, np.concatenate([mq, mk], -1), mo, nv, mv]
    out["win"] = np.stack(blocks, 1).reshape(DEPTH, 10, KD, P, 512).transpose(0, 1, 3, 2, 4).reshape(
        DEPTH, 10, P, KD * 512)
    g3 = w[:, :, o[12]:].reshape(DEPTH, KD, P, 3, KD, P).transpose(0, 4, 2, 3, 1, 5).reshape(DEPTH, KD, P, -1)
    b3 = a["w_branch"].reshape(DEPTH, 3, KC, P, KD, P).transpose(0, 4, 3, 1, 2, 5).reshape(DEPTH, KD, P, -1)
    out["mg"] = np.concatenate([g3, b3], -1)
    out["wo"] = a["w_out"].reshape(DEPTH, KD, P, D).transpose(0, 2, 1, 3)
    zero = np.zeros((1, C), f)
    par = []
    for l in range(DEPTH):
        ib, fb = np.zeros((P, 1), f), np.zeros((P, 1), f)
        ib[0:8, 0], fb[32:40, 0] = a["ml_i_bias"][l].reshape(8), a["ml_f_bias"][l].reshape(8)
        par += [tiles(a["norm1_g"][l]), tiles(a["norm2_g"][l]), tiles(a["b_ada"][l]), tiles(a["rw_mu"][l]),
                tiles(a["rw_w0"][l].reshape(-1)), tiles(a["rw_a0"][l].reshape(-1)), tiles(a["rw_k_k"][l]),
                tiles(a["rw_k_a"][l]), tiles(a["rw_r_k"][l].reshape(-1)), tiles(a["rw_lnx_g"][l]),
                tiles(a["rw_lnx_b"][l]), tiles(a["rw_v0"][l - 1] if l else zero[0]), tiles(a["ml_norm_g"][l]),
                np.tile(a["na_qn_g"][l], 2)[:, None], np.tile(a["na_kn_g"][l], 2)[:, None], ib, fb]
    out["par"] = np.concatenate(par, 1)
    lora = np.zeros((DEPTH, P, 3 * C + KC * 32 + C), f)
    for l in range(DEPTH):
        lora[l, :, 0:C] = a["rw_w2"][l].reshape(P, C)
        lora[l, :, C:2 * C] = a["rw_a2"][l].reshape(P, C)
        lora[l, :, 2 * C:3 * C] = a["rw_g2"][l]
        if l:
            lora[l, :, 3 * C:3 * C + KC * 32] = wt(a["rw_v1"][l - 1]).reshape(P, -1)
            lora[l, 0:32, 3 * C + KC * 32:] = a["rw_v2"][l - 1]
    out["lora"] = lora
    t = np.arange(SEQ)
    row, col = t // GRID_W, t % GRID_W
    cs = np.clip(col - NA_WIN_C // 2, 0, GRID_W - NA_WIN_C)
    inside = (col[None, :] >= cs[:, None]) & (col[None, :] < cs[:, None] + NA_WIN_C)
    ri = row[None, :] - row[:, None] + NA_WIN_R - 1
    ci = np.clip(col[None, :] - col[:, None] + NA_WIN_C - 1, 0, 2 * NA_WIN_C - 2)
    nab = np.full((DEPTH, HEADS, SEQ, SEQ), NEG, f)
    nab[:, :, inside] = a["na_rpb"][:, :, ri[inside], ci[inside]]
    out["nab"] = nab.reshape(DEPTH, HEADS, 2, P, SEQ).transpose(0, 3, 1, 2, 4).reshape(DEPTH, P, -1)
    rt = np.concatenate([a["moe_router"].reshape(DEPTH, KD, P, E_ROUTED).transpose(0, 2, 1, 3).reshape(DEPTH, P, -1),
                         np.broadcast_to(a["moe_bias"][:, None, :], (DEPTH, P, E_ROUTED))], -1)
    out["rt"] = rt
    moe = np.zeros((DEPTH, E_ALL, P, 3 * KD * P), f)
    for j, (rn, sn) in enumerate((("moe_w_gate", "sh_w_gate"), ("moe_w_up", "sh_w_up"))):
        sh = a[sn].reshape(DEPTH, D, 2, P).transpose(0, 2, 1, 3)
        full = np.concatenate([a[rn], sh], 1)
        moe[..., j * D:(j + 1) * D] = full.reshape(DEPTH, E_ALL, KD, P, P).transpose(0, 1, 3, 2, 4).reshape(
            DEPTH, E_ALL, P, D)
    moe[..., 2 * D:] = np.concatenate([a["moe_w_down"], a["sh_w_down"].reshape(DEPTH, 2, P, D)], 1)
    out["moe"] = moe
    out["cst"], out["mlc"] = constants()
    return {n: np.ascontiguousarray(v) for n, v in out.items()}


def kernel(**inputs):
    import concourse.bacc as bacc
    from concourse.bass_utils import run_bass_kernel_spmd

    nc = bacc.Bacc("TRN2", target_bir_lowering=False, num_devices=1)
    arrays = layout(inputs)
    d = {n: nc.dram_tensor("in_" + n, v.shape, mybir.dt.from_np(v.dtype), kind="ExternalInput").ap()
         for n, v in arrays.items()}
    d["out"] = nc.dram_tensor("out_dram", (P, KD, SEQ), F32, kind="ExternalOutput").ap()
    hybrid_backbone_kernel(nc, d)
    r = run_bass_kernel_spmd(nc, [{"in_" + n: v for n, v in arrays.items()}], core_ids=[0])
    got = r.results[0]["out_dram"]
    return got.transpose(2, 1, 0).reshape(1, SEQ, D)
```
